# Optimizing a Trainium2 kernel written in Bass

```python
import jax, jax.numpy as jnp
from jax import lax
import numpy as np

D_MODEL = 1024
BATCH = 1
SEQ = 512
DEPTH = 1
DEC_BATCH = 1
DEC_SEQ = 64
PAST_LEN = 256

CHUNK = 64
Q_BLOCK = 128
EPS = 1e-5
CONV_CH = 512
CONV_WIDTH = 31
MLA_HEADS = 8
Q_LORA = 384
KV_LORA = 256
QK_NOPE = 64
QK_ROPE = 32
V_HEAD = 64
ROPE_BASE = 10000.0
MLA_SCALE = (QK_NOPE + QK_ROPE) ** -0.5
MEM_TOKENS = 256
MEM_HEADS = 4
MEM_HEAD_DIM = 128
MEM_SCALE = MEM_HEAD_DIM ** -0.5
N_BRANCH = 3
N_GROUPS = 4
EXPERTS_PER_GROUP = 8
TOP_K = 2
D_EXPERT = 256
DEEPNORM_ALPHA = (2.0 * DEPTH) ** 0.25
DEEPNORM_BETA = (8.0 * DEPTH) ** -0.25
IN_GLU = 2 * CONV_CH
IN_QDOWN = Q_LORA
IN_KVDOWN = KV_LORA + QK_ROPE
IN_MEMQ = MEM_HEADS * MEM_HEAD_DIM
IN_GATE = N_BRANCH * D_MODEL
D_IN = IN_GLU + IN_QDOWN + IN_KVDOWN + IN_MEMQ + IN_GATE
SPLIT_POINTS = (IN_GLU, IN_GLU + IN_QDOWN, IN_GLU + IN_QDOWN + IN_KVDOWN, IN_GLU + IN_QDOWN + IN_KVDOWN + IN_MEMQ)

kernel_name = 'hybrid_conv_mla_memx_hmoe_stream'

def layer_norm(x, g, b):
    xf = x.astype(jnp.float32)
    mu = jnp.mean(xf, axis=-1, keepdims=True)
    var = jnp.mean(jnp.square(xf - mu), axis=-1, keepdims=True)
    return ((xf - mu) * lax.rsqrt(var + EPS) * g + b).astype(x.dtype)

def rms_norm(x, g):
    xf = x.astype(jnp.float32)
    return (xf * lax.rsqrt(jnp.mean(xf * xf, axis=-1, keepdims=True) + EPS) * g).astype(x.dtype)

def rope_tables(pos):
    half = QK_ROPE // 2
    inv = jnp.power(ROPE_BASE, -jnp.arange(half, dtype=jnp.float32) / half)
    ang = pos.astype(jnp.float32)[:, None] * inv[None, :]
    return jnp.cos(ang), jnp.sin(ang)

def apply_rope(x, cos, sin):
    half = QK_ROPE // 2
    x1 = x[..., :half].astype(jnp.float32)
    x2 = x[..., half:].astype(jnp.float32)
    return jnp.concatenate([x1 * cos - x2 * sin, x1 * sin + x2 * cos], axis=-1).astype(x.dtype)

def conv_branch(glu_in, conv_state, w_dw, b_dw, g_cn, b_cn, w_co):
    a, b = jnp.split(glu_in, 2, axis=-1)
    u = a * jax.nn.sigmoid(b)
    padded = jnp.concatenate([conv_state.astype(u.dtype), u], axis=1)
    y = lax.conv_general_dilated(padded, w_dw[:, None, :].astype(u.dtype), window_strides=(1,), padding='VALID',
                                 dimension_numbers=('NWC', 'WIO', 'NWC'), feature_group_count=CONV_CH) + b_dw
    y = jax.nn.silu(layer_norm(y, g_cn, b_cn))
    return y @ w_co, padded[:, -(CONV_WIDTH - 1):]

def mla_attend(q_lat, q_rot, c_kv, k_rot, q_pos, k_pos):
    s = jnp.einsum('nqhc,nkc->nhqk', q_lat, c_kv) + jnp.einsum('nqhr,nkr->nhqk', q_rot, k_rot)
    s = s.astype(jnp.float32) * MLA_SCALE
    mask = (k_pos[None, :] // CHUNK) <= (q_pos[:, None] // CHUNK)
    s = jnp.where(mask[None, None], s, -1e30)
    p = jax.nn.softmax(s, axis=-1).astype(c_kv.dtype)
    return jnp.einsum('nhqk,nkc->nqhc', p, c_kv)

def mem_attend(q, mem_k, mem_v):
    s = jnp.einsum('nthd,nmhd->nhtm', q, mem_k).astype(jnp.float32) * MEM_SCALE
    p = jax.nn.softmax(s, axis=-1).astype(mem_v.dtype)
    return jnp.einsum('nhtm,nmhd->nthd', p, mem_v)

def hier_moe(x, w_group, b_group, w_router, b_router, w_e1, w_e3, w_e2):
    n, t, d = x.shape
    xt = x.reshape(n * t, d)
    p_group = jax.nn.softmax((xt @ w_group + b_group).astype(jnp.float32), axis=-1)
    g_val, g_idx = lax.top_k(p_group, 1)
    g_onehot = jax.nn.one_hot(g_idx[:, 0], N_GROUPS, dtype=jnp.float32)
    e_logits = (xt @ w_router + b_router).astype(jnp.float32).reshape(n * t, N_GROUPS, EXPERTS_PER_GROUP)
    e_sel = jnp.einsum('mge,mg->me', e_logits, g_onehot)
    p_exp = jax.nn.softmax(e_sel, axis=-1)
    e_val, e_idx = lax.top_k(p_exp, TOP_K)
    e_val = e_val / jnp.sum(e_val, axis=-1, keepdims=True)
    w_in_group = jnp.sum(jax.nn.one_hot(e_idx, EXPERTS_PER_GROUP, dtype=jnp.float32) * e_val[..., None], axis=1)
    combine = ((g_val * g_onehot)[:, :, None] * w_in_group[:, None, :]).astype(x.dtype)
    out = jnp.zeros_like(xt)
    for gi in range(N_GROUPS):
        h = jax.nn.silu(jnp.einsum('md,edf->mef', xt, w_e1[gi])) * jnp.einsum('md,edf->mef', xt, w_e3[gi])
        out = out + jnp.einsum('mef,efd->md', h * combine[:, gi, :, None], w_e2[gi])
    return out.reshape(n, t, d)

def trunk_layer(x, pos, conv_state, past_lat, past_krot, mem_k, mem_v,
                w_in, b_gate, w_dw, b_dw, g_cn, b_cn, w_co,
                g_qa, w_uq, g_kva, w_uk, w_uv, w_mo, w_mem_o, w_out, g_ln1, b_ln1,
                w_group, b_group, w_router, b_router, w_e1, w_e3, w_e2, g_ln2, b_ln2):
    n, t, _ = x.shape
    proj = x @ w_in
    glu_in, q_down, kv_down, mem_q, gate_pre = jnp.split(proj, SPLIT_POINTS, axis=-1)
    y_conv, new_conv = conv_branch(glu_in, conv_state, w_dw, b_dw, g_cn, b_cn, w_co)
    cos, sin = rope_tables(pos)
    q = (rms_norm(q_down, g_qa) @ w_uq).reshape(n, t, MLA_HEADS, QK_NOPE + QK_ROPE)
    q_lat = jnp.einsum('nthd,chd->nthc', q[..., :QK_NOPE], w_uk)
    q_rot = apply_rope(q[..., QK_NOPE:], cos[:, None, :], sin[:, None, :])
    c_kv = rms_norm(kv_down[..., :KV_LORA], g_kva)
    k_rot = apply_rope(kv_down[..., KV_LORA:], cos, sin)
    if past_lat is None:
        nblk = t // Q_BLOCK
        to_blocks = lambda a: jnp.swapaxes(a.reshape((n, nblk, Q_BLOCK) + a.shape[2:]), 0, 1)
        o_lat = lax.map(lambda blk: mla_attend(blk[0], blk[1], c_kv, k_rot, blk[2], pos),
                        (to_blocks(q_lat), to_blocks(q_rot), pos.reshape(nblk, Q_BLOCK)))
        o_lat = jnp.swapaxes(o_lat, 0, 1).reshape(n, t, MLA_HEADS, KV_LORA)
    else:
        keys_lat = jnp.concatenate([past_lat, c_kv], axis=1)
        keys_rot = jnp.concatenate([past_krot, k_rot], axis=1)
        k_pos = jnp.arange(keys_lat.shape[1], dtype=jnp.int32)
        o_lat = mla_attend(q_lat, q_rot, keys_lat, keys_rot, pos, k_pos)
    y_mla = jnp.einsum('nthc,chv->nthv', o_lat, w_uv).reshape(n, t, MLA_HEADS * V_HEAD) @ w_mo
    y_mem = mem_attend(mem_q.reshape(n, t, MEM_HEADS, MEM_HEAD_DIM), mem_k, mem_v).reshape(n, t, IN_MEMQ) @ w_mem_o
    gates = jax.nn.sigmoid(gate_pre + b_gate).reshape(n, t, N_BRANCH, D_MODEL)
    merged = gates[:, :, 0] * y_conv + gates[:, :, 1] * y_mla + gates[:, :, 2] * y_mem
    x1 = layer_norm(DEEPNORM_ALPHA * x + merged @ w_out, g_ln1, b_ln1)
    y = hier_moe(x1, w_group, b_group, w_router, b_router, w_e1, w_e3, w_e2)
    x2 = layer_norm(DEEPNORM_ALPHA * x1 + y, g_ln2, b_ln2)
    return x2, new_conv, c_kv, k_rot

def setup_inputs(seed: int = 0) -> dict:
    key = jax.random.key(seed)
    ks = iter(jax.random.split(key, 40))
    nrm = lambda shape, scale: scale * jax.random.normal(next(ks), shape, jnp.float32)
    L, D = DEPTH, D_MODEL
    G, E, F = N_GROUPS, EXPERTS_PER_GROUP, D_EXPERT
    return {
        'x_prompt': nrm((BATCH, SEQ, D), 1.0),
        'x_sample': nrm((DEC_BATCH, DEC_SEQ, D), 1.0),
        'cache_conv': nrm((L, DEC_BATCH, CONV_WIDTH - 1, CONV_CH), 0.5),
        'cache_mla_latent': nrm((L, DEC_BATCH, PAST_LEN, KV_LORA), 1.0),
        'cache_mla_krope': nrm((L, DEC_BATCH, PAST_LEN, QK_ROPE), 1.0),
        'cache_mem_k': nrm((L, DEC_BATCH, MEM_TOKENS, MEM_HEADS, MEM_HEAD_DIM), 1.0),
        'cache_mem_v': nrm((L, DEC_BATCH, MEM_TOKENS, MEM_HEADS, MEM_HEAD_DIM), 1.0),
        'mem_prompt': nrm((BATCH, MEM_TOKENS, D), 1.0),
        'w_in': nrm((L, D, D_IN), D ** -0.5),
        'b_gate': nrm((L, IN_GATE), 0.1),
        'w_dw': nrm((L, CONV_WIDTH, CONV_CH), CONV_WIDTH ** -0.5),
        'b_dw': nrm((L, CONV_CH), 0.02),
        'g_cn': 1.0 + nrm((L, CONV_CH), 0.05),
        'b_cn': nrm((L, CONV_CH), 0.02),
        'w_co': nrm((L, CONV_CH, D), CONV_CH ** -0.5),
        'g_qa': 1.0 + nrm((L, Q_LORA), 0.05),
        'w_uq': nrm((L, Q_LORA, MLA_HEADS * (QK_NOPE + QK_ROPE)), Q_LORA ** -0.5),
        'g_kva': 1.0 + nrm((L, KV_LORA), 0.05),
        'w_uk': nrm((L, KV_LORA, MLA_HEADS, QK_NOPE), KV_LORA ** -0.5),
        'w_uv': nrm((L, KV_LORA, MLA_HEADS, V_HEAD), KV_LORA ** -0.5),
        'w_mo': nrm((L, MLA_HEADS * V_HEAD, D), (MLA_HEADS * V_HEAD) ** -0.5),
        'w_mem_k': nrm((L, D, IN_MEMQ), D ** -0.5),
        'w_mem_v': nrm((L, D, IN_MEMQ), D ** -0.5),
        'w_mem_o': nrm((L, IN_MEMQ, D), IN_MEMQ ** -0.5),
        'w_out': nrm((L, D, D), DEEPNORM_BETA * D ** -0.5),
        'g_ln1': 1.0 + nrm((L, D), 0.05),
        'b_ln1': nrm((L, D), 0.02),
        'w_group': nrm((L, D, G), D ** -0.5),
        'b_group': nrm((L, G), 0.01),
        'w_router': nrm((L, D, G * E), D ** -0.5),
        'b_router': nrm((L, G * E), 0.01),
        'w_e1': nrm((L, G, E, D, F), D ** -0.5),
        'w_e3': nrm((L, G, E, D, F), D ** -0.5),
        'w_e2': nrm((L, G, E, F, D), DEEPNORM_BETA * F ** -0.5),
        'g_ln2': 1.0 + nrm((L, D), 0.05),
        'b_ln2': nrm((L, D), 0.02),
    }

def reference(x_prompt, x_sample, cache_conv, cache_mla_latent, cache_mla_krope, cache_mem_k, cache_mem_v,
              mem_prompt, w_in, b_gate, w_dw, b_dw, g_cn, b_cn, w_co, g_qa, w_uq, g_kva, w_uk, w_uv, w_mo,
              w_mem_k, w_mem_v, w_mem_o, w_out, g_ln1, b_ln1, w_group, b_group, w_router, b_router,
              w_e1, w_e3, w_e2, g_ln2, b_ln2):
    n_p, s_p, _ = x_prompt.shape
    n_s, s_s, _ = x_sample.shape
    n_mem = mem_prompt.shape[1]
    past_len = cache_mla_latent.shape[2]
    pos_p = jnp.arange(s_p, dtype=jnp.int32)
    pos_s = past_len + jnp.arange(s_s, dtype=jnp.int32)
    h_p, h_s = x_prompt, x_sample
    conv_p, lat_p, kr_p, mk_p, mv_p = [], [], [], [], []
    conv_s, lat_s, kr_s = [], [], []
    for l in range(DEPTH):
        lw = (w_in[l], b_gate[l], w_dw[l], b_dw[l], g_cn[l], b_cn[l], w_co[l],
              g_qa[l], w_uq[l], g_kva[l], w_uk[l], w_uv[l], w_mo[l], w_mem_o[l], w_out[l], g_ln1[l], b_ln1[l],
              w_group[l], b_group[l], w_router[l], b_router[l], w_e1[l], w_e3[l], w_e2[l], g_ln2[l], b_ln2[l])
        mem_k_l = (mem_prompt @ w_mem_k[l]).reshape(n_p, n_mem, MEM_HEADS, MEM_HEAD_DIM)
        mem_v_l = (mem_prompt @ w_mem_v[l]).reshape(n_p, n_mem, MEM_HEADS, MEM_HEAD_DIM)
        conv0 = jnp.zeros((n_p, CONV_WIDTH - 1, CONV_CH), x_prompt.dtype)
        h_p, c_p, l_p, r_p = trunk_layer(h_p, pos_p, conv0, None, None, mem_k_l, mem_v_l, *lw)
        conv_p.append(c_p); lat_p.append(l_p); kr_p.append(r_p); mk_p.append(mem_k_l); mv_p.append(mem_v_l)
        h_s, c_s, l_s, r_s = trunk_layer(h_s, pos_s, cache_conv[l], cache_mla_latent[l], cache_mla_krope[l],
                                         cache_mem_k[l], cache_mem_v[l], *lw)
        conv_s.append(c_s); lat_s.append(l_s); kr_s.append(r_s)
    return (h_p, h_s,
            jnp.stack(conv_p, axis=0), jnp.stack(lat_p, axis=0), jnp.stack(kr_p, axis=0),
            jnp.stack(mk_p, axis=0), jnp.stack(mv_p, axis=0),
            jnp.stack(conv_s, axis=0), jnp.stack(lat_s, axis=0), jnp.stack(kr_s, axis=0))


_drawn_inputs = setup_inputs


def setup_inputs(seed=0):
    import zlib

    import numpy as np

    out = dict(_drawn_inputs(seed))
    spreads = {}
    factors = {'cache_mla_krope': 4.129,
     'b_gate': 3.85,
     'b_dw': 4.402,
     'g_cn': 4.057,
     'b_cn': 7.213,
     'g_qa': 8.0,
     'b_group': 45.615,
     'b_router': 14.369,
     'b_ln2': 2.943,
     'cache_mem_k': 2.92}
    for name, (base, spread) in spreads.items():
        noise = np.random.default_rng([zlib.crc32(name.encode()), seed]).standard_normal(out[name].shape)
        drawn = base * np.exp(spread * noise) if base else spread * noise
        out[name] = __import__('jax').numpy.asarray(drawn.astype(out[name].dtype))
    for name, factor in factors.items():
        out[name] = (out[name] * factor).astype(out[name].dtype)
    return out
```

```python
from contextlib import ExitStack

import numpy as np

import concourse.bass as bass
from concourse import mybir

F32 = mybir.dt.float32
BF16 = mybir.dt.bfloat16
I32 = mybir.dt.int32
ALU = mybir.AluOpType
ACT = mybir.ActivationFunctionType
AX = mybir.AxisListType

D = 1024
TP, TS = 512, 64
T = TP + TS
HT = T // 2
PAST = 256
CH = 512
CW = 31
PAD = CW - 1
NH, NOPE, ROPE, VD = 8, 64, 32, 64
QK = NOPE + ROPE
QL, KVL = 384, 256
KEYS = TP + PAST + TS
MH, MD, MT = 4, 128, 256
EPS = 1e-5
ALPHA = 2.0 ** 0.25
NG, NE_G, FE = 4, 8, 256
NE = NG * NE_G
KT = D // 128
CAP = 128
NCH = -(-T // CAP)
TILES = [(i * 128, 128) for i in range(4)] + [(TP, TS)]
NT = len(TILES)
SKIP = 1 << 14
CAUSAL = 64
UW = PAD + TP + PAD + TS

JOBS = []
for _c in range(4):
    JOBS += [f"glu_b{_c}", f"glu_a{_c}"]
JOBS += ["q0", "q1", "q2", "kv0", "kv1", "kr", "q_ss", "kv_ss", "mk0", "mk1", "mk2", "mk3", "conv_mean",
         "mv0", "mv1", "mq0", "mq1", "conv_var", "mq2", "mq3"]
JOBS += [f"un{i}" for i in range(4)] + ["ur0", "ur1"] + [f"uk{i}" for i in range(4)] + [f"uv{i}" for i in range(7)]
for _j in range(8):
    JOBS += [f"g0_{_j}", f"yc_{_j}", f"g1_{_j}", f"ym_{_j}", f"g2_{_j}", f"yx_{_j}"]
JOBS += ["c0", "c1", "t0", "c2", "l0", "t1", "c3", "l1", "t2", "c4", "l2", "t3", "l3", "t4", "l4", "rank", "count"]
JOB = {n: i for i, n in enumerate(JOBS)}

RING = 6
SLOT = 1024
ITEMS = []
for _c in range(4):
    ITEMS += [(f"glu_b{_c}", 1024, f"glu_b{_c}"), (f"glu_a{_c}", 1024, f"glu_a{_c}")]
ITEMS += [(n, 1024, n) for n in ("q0", "q1", "q2", "kv0", "kv1")] + [("kr", 256, "kr")]
ITEMS += [(f"mk{i}", 1024, f"mk{i}") for i in range(4)] + [(f"mv_{i}", 1024, "mv1") for i in range(4)]
ITEMS += [(f"mq{i}", 1024, f"mq{i}") for i in range(4)]
ITEMS += [("uq0", 768, "un1"), ("uq1", 768, "un3"), ("uq2", 768, "ur1"), ("uk", 1024, "uk3"), ("uv", 1024, "uv6")]
for _j in range(8):
    ITEMS += [(f"g0_{_j}", 1024, f"g0_{_j}"), (f"comx_{_j}", 1024, f"ym_{_j}"), (f"g1_{_j}", 1024, f"g1_{_j}"),
              (f"g2_{_j}", 1024, f"g2_{_j}"), (f"xo_{_j}", 512, f"yx_{_j}")]
ITEM = {n: i for i, (n, _, _) in enumerate(ITEMS)}

MEM_UNITS = [("mem", i, h) for i in range(NT) for h in range(MH)]
MLA_UNITS = [("mla", i, h) for i in range(NT) for h in range(NH)]


def key_tiles(kind, i):
    if kind == "mem":
        return [(0, 0, 128), (1, 128, 128)]
    if i < 4:
        return [(k, 128 * k, 128) for k in range(i + 1)]
    return [(4, TP, 128), (5, TP + 128, 128), (6, TP + PAST, TS)]


def program(nc, a, o):
    ctx = ExitStack()
    with ctx:
        def sb(name, shape, dt=F32):
            return ctx.enter_context(nc.sbuf_tensor(name, shape, dt))

        def sem(name):
            return ctx.enter_context(nc.semaphore(name))

        XT = sb("XT", [128, 4608])
        xT = XT[:, :].rearrange("p (k t) -> p k t", k=KT)
        x1T = XT[:, 0:2048].rearrange("p (b k t) -> p b k t", b=2, k=KT)
        xg = XT[:, 2048:4096].rearrange("p (b d) -> p b d", b=2)
        Z = sb("Z", [128, 2304])
        zT = Z[:, :].rearrange("p (c t) -> p c t", c=4)
        xgT = Z[:, 0:1024].rearrange("p (k s) -> p k s", k=KT)
        hg = Z[:, 1024:1280]
        hm = Z[:, 1280:1536]
        hT = Z[:, 1536:1792].rearrange("p (j s) -> p j s", j=2)
        OM = sb("OM", [128, 2304])
        omT = OM[:, :].rearrange("p (c t) -> p c t", c=4)
        OX = sb("OX", [128, 2304])
        oxT = OX[:, :].rearrange("p (c t) -> p c t", c=4)
        ysb = OM[:, 0:2048].rearrange("p (b d) -> p b d", b=2)
        QH = sb("QH", [128, 4608])
        qh = QH[:, :].rearrange("p (h t) -> p h t", h=NH)
        norms = QH[:, 0:2304].rearrange("p (n t) -> p n t", n=4)
        merged = QH[:, :].rearrange("p (k t) -> p k t", k=KT)
        GH = sb("GH", [128, 10240])
        kh = GH[:, 0:6656].rearrange("p (h t) -> p h t", h=NH)
        V = GH[:, 6656:10240].rearrange("p (k n) -> p k n", k=7)
        memq = GH[:, 0:2304].rearrange("p (h t) -> p h t", h=MH)
        mkT = GH[:, 2304:4352].rearrange("p (s h m) -> p s h m", s=2, h=MH)
        mv = GH[:, 4352:6400].rearrange("p (s k n) -> p s k n", s=2, k=2)
        w_out = GH[:, 0:8192].rearrange("p (k n) -> p k n", k=KT)
        xtok = GH[:, 8192:10240].rearrange("p (b d) -> p b d", b=2)
        RG = sb("RG", [128, RING * SLOT])
        ring = RG[:, :].rearrange("p (r n) -> p r n", r=RING)
        x1 = RG[:, 0:5120].rearrange("p (t d) -> p t d", t=NT)
        KM = sb("KM", [128, 4592])
        U = KM[:, 0:2544].rearrange("p (c t) -> p c t", c=4)
        memT = KM[:, 2544:4592].rearrange("p (k m) -> p k m", k=KT)
        Pb = KM[:, 0:1536].rearrange("p (b n) -> p b n", b=3)
        PT = KM[:, 1536:3072].rearrange("p (b n) -> p b n", b=3)
        osb = KM[:, 3072:4096].rearrange("p (b n) -> p b n", b=2)
        gate = KM[:, 0:3456].rearrange("p (b n t) -> p b n t", b=2, n=3)
        lnbc = KM[:, 0:4096].rearrange("p (n d) -> p n d", n=4)
        WE = sb("WE", [128, 2, 6144])
        w13 = [WE[:, b, 0:4096].rearrange("p (s k f) -> p s k f", s=2, k=KT) for b in range(2)]
        w2 = [WE[:, b, 4096:6144].rearrange("p (j d) -> p j d", j=2) for b in range(2)]
        WF = WE[:, :, :].rearrange("p b n -> p (b n)")
        sq = WF[:, 0:2304].rearrange("p (c t) -> p c t", c=4)
        qd = WF[:, 2304:4032].rearrange("p (c t) -> p c t", c=3)
        kvd = WF[:, 4032:5184].rearrange("p (c t) -> p c t", c=2)
        cos = WF[:, 5184:5760]
        sin = WF[:, 5760:6336]
        krot = WF[0:32, 6336:7168]
        rp = WF[:, 7168:8896].rearrange("p (n t) -> p n t", n=3)
        ck = WF[:, 8896:10560].rearrange("p (c t) -> p c t", c=2)
        yab = WF[:, 0:10240].rearrange("p (t c d) -> p t c d", t=NT, c=2)

        ident = sb("ident", [128, 128])
        ones = sb("ones", [128, 128])
        rowmask = sb("rowmask", [128, 128])
        negrow = sb("negrow", [128, 64])
        wdw = sb("wdw", [128, 4, CW])
        vec = sb("vec", [128, 3, 4])
        gqa = sb("gqa", [128, 3])
        gkva = sb("gkva", [128, 2])
        bgate = sb("bgate", [128, 24])
        eps = sb("eps", [128, 1])
        nb = sb("nb", [128, 8])
        rs = sb("rs", [128, 2, 8])
        rinv = sb("rinv", [128, 2, 8])
        st = sb("st", [128, 2, 2, 6])
        mva = sb("mva", [128, 2, 2])
        rstd = sb("rstd", [128, 2, 2])
        wr = sb("wr", [128, KT, 36])
        rbias = sb("rbias", [128, 36])
        lg = sb("lg", [128, NT, 36])
        tri = sb("tri", [128, 128], BF16)
        onesb = sb("onesb", [128, 128], BF16)
        desc = sb("desc", [128, NE_G])
        idx32 = sb("idx32", [128, NE])
        gm = sb("gm", [128, 12, NT])
        g4 = sb("g4", [128, 3, NT, NG])
        e8 = sb("e8", [128, 4, NT, NE_G])
        e32 = sb("e32", [128, 4, NT, NE])
        maskb = sb("maskb", [128, NT, NE], BF16)
        wsel = sb("wsel", [128, 2, NT])
        addr = sb("addr", [128, 2, NT], I32)
        rowid = sb("rowid", [128, 2, NT], I32)
        tab0 = sb("tab0", [128, NCH * NE], I32)
        tabs = sb("tabs", [128, NCH * NE], I32)
        flag = sb("flag", [128, 1], I32)

        PS = ctx.enter_context(nc.psum_tensor("PS", [128, 8, 512], F32))

        tab_d = nc.dram_tensor("slot_table", (CAP * NCH * NE, 1), I32, kind="Internal").ap()
        x1_d = nc.dram_tensor("x1_rows", (2 * T, D), F32, kind="Internal").ap()
        y_d = nc.dram_tensor("expert_rows", (2 * T, D), F32, kind="Internal").ap()

        ring_full = [sem(f"ring_full{i}") for i in range(RING)]
        job_done = sem("job_done")
        in_x = sem("in_x")
        in_small = sem("in_small")
        in_conv = sem("in_conv")
        in_mem = sem("in_mem")
        in_cache = sem("in_cache")
        in_past = sem("in_past")
        in_wout = sem("in_wout")
        in_ln = sem("in_ln")
        in_xtok = [sem("in_xtok0"), sem("in_xtok1")]
        in_route = sem("in_route")
        out_sem = sem("out_sem")
        const_ready = sem("const_ready")
        pool_chain = sem("pool_chain")
        dve_chain = sem("dve_chain")
        act_chain = sem("act_chain")
        glu_sig = sem("glu_sig")
        u_ready = sem("u_ready")
        conv_raw = sem("conv_raw")
        kr_raw = sem("kr_raw")
        mean_read = sem("mean_read")
        conv_std = sem("conv_std")
        route_const = sem("route_const")
        conv_out = sem("conv_out")
        lat_out = sem("lat_out")
        mem_out = sem("mem_out")
        conv_cent = sem("conv_cent")
        conv_sq = sem("conv_sq")
        conv_norm = sem("conv_norm")
        z_ready = sem("z_ready")
        lat_raw = sem("lat_raw")
        lat_sq = sem("lat_sq")
        lat_std = sem("lat_std")
        qn_ready = sem("qn_ready")
        ck_ready = sem("ck_ready")
        krot_ready = sem("krot_ready")
        mem_proj = sem("mem_proj")
        ur_raw = sem("ur_raw")
        ur_rot = sem("ur_rot")
        qk_ready = sem("qk_ready")
        kr_copied = sem("kr_copied")
        score_done = sem("score_done")
        max_done = sem("max_done")
        exp_done = sem("exp_done")
        pt_done = sem("pt_done")
        pt_evac = sem("pt_evac")
        pv_done = sem("pv_done")
        o_norm = sem("o_norm")
        ot_done = sem("ot_done")
        ot_evac = sem("ot_evac")
        gate_sig = sem("gate_sig")
        gate_mul = sem("gate_mul")
        merged_ready = sem("merged_ready")
        ln1_res = sem("ln1_res")
        ln1_var = sem("ln1_var")
        ln1_std = sem("ln1_std")
        ln1_hat = sem("ln1_hat")
        x1_ready = sem("x1_ready")
        x1_out = sem("x1_out")
        x1T_ready = sem("x1T_ready")
        lg_ready = sem("lg_ready")
        route_dve = sem("route_dve")
        route_exp = sem("route_exp")
        mask_ready = sem("mask_ready")
        addr_ready = sem("addr_ready")
        flag_ready = sem("flag_ready")
        tab_init = sem("tab_init")
        tab_written = sem("tab_written")
        tab_loaded = sem("tab_loaded")
        xg_zero = sem("xg_zero")
        x1_scaled = sem("x1_scaled")
        we13 = [sem("we13_0"), sem("we13_1")]
        we2 = [sem("we2_0"), sem("we2_1")]
        e_rows = [sem("e_rows0"), sem("e_rows1")]
        e_tx = sem("e_tx")
        e_xgT = sem("e_xgT")
        e_xgT2 = sem("e_xgT2")
        e_h = sem("e_h")
        e_silu = sem("e_silu")
        e_hm = sem("e_hm")
        e_ht = sem("e_ht")
        e_hT = sem("e_hT")
        e_y = sem("e_y")
        e_ya = sem("e_ya")
        e_yb = sem("e_yb")
        e_out = [sem("e_out0"), sem("e_out1")]
        ov_w = sem("ov_w")
        ov_rows = sem("ov_rows")
        ov_tx = sem("ov_tx")
        ov_xgT = sem("ov_xgT")
        ov_h = sem("ov_h")
        ov_silu = sem("ov_silu")
        ov_hm = sem("ov_hm")
        ov_ht = sem("ov_ht")
        ov_hT = sem("ov_hT")
        ov_y = sem("ov_y")
        ov_ysb = sem("ov_ysb")
        ov_out = sem("ov_out")
        in_y = [sem(f"in_y{i}") for i in range(NT)]
        ln2_var = sem("ln2_var")
        ln2_std = sem("ln2_std")
        ln2_hat = sem("ln2_hat")
        ln2_out = sem("ln2_out")

        def pair(name):
            p = JOB[name] % 4
            return PS[:, 2 * p:2 * p + 2, :]

        def half(name, s, m=128, n=HT):
            return PS[0:m, 2 * (JOB[name] % 4) + s, 0:n]

        def both(name, m=128, n=HT):
            return PS[0:m, 2 * (JOB[name] % 4):2 * (JOB[name] % 4) + 2, 0:n]

        def wait_job(eng, name):
            eng.wait_ge(job_done, JOB[name] + 1)

        def read_of(name):
            kind = name.rstrip("0123456789")
            i = int(name[len(kind):] or 0)
            if kind.endswith("_") and kind[0] in "gy":
                gates = {"g0_": 0, "g1_": 1, "g2_": 2}
                return (gate_sig, 3 * i + gates[kind] + 1) if kind in gates else (gate_mul, 3 * i + {"yc_": 0, "ym_": 1, "yx_": 2}[kind] + 1)
            return {
                "glu_b": (glu_sig, i + 1), "glu_a": (u_ready, i + 1), "q": (lat_raw, i + 1), "kv": (lat_raw, i + 4),
                "kr": (kr_raw, 1), "q_ss": (lat_std, 1), "kv_ss": (lat_std, 2), "mk": (mem_proj, i + 1),
                "mv": (mem_proj, i + 5), "mq": (mem_proj, i + 7), "conv_mean": (mean_read, 1), "conv_var": (conv_std, 1),
                "un": (qk_ready, 2 * i + 2), "ur": (ur_raw, i + 1), "uk": (qk_ready, 2 * i + 10), "uv": (qk_ready, i + 17),
                "c": (ln1_res, i + 1), "t": (x1T_ready, i + 1), "l": (lg_ready, i + 1), "rank": (addr_ready, 2),
                "count": (flag_ready, 1),
            }[kind]

        def split(ap):
            return ap.rearrange("p (s t) -> p s t", s=2)

        def w_item(name):
            return ring[:, ITEM[name] % RING, :]

        MEM_LAST, MLA_LAST = len(MEM_UNITS), len(MEM_UNITS) + len(MLA_UNITS)
        UNITS = MEM_UNITS + MLA_UNITS
        GROUPS = []
        for u in UNITS:
            if u[:2] not in GROUPS:
                GROUPS.append(u[:2])
        group_of = [GROUPS.index(u[:2]) for u in UNITS]
        last_of_group = {g: max(n for n, x in enumerate(group_of) if x == g) for g in range(len(GROUPS))}
        N_G = len(GROUPS)
        N_MEM_G = NT

        block = ctx.enter_context(nc.Block())

        @block.sync
        def _(sp):
            def src(name):
                for key in ("glu_b", "glu_a"):
                    if name.startswith(key):
                        return a["w_glu_t"][int(name[5:]) + 4 * (key == "glu_a")]
                if name[0] == "q":
                    return a["w_q_t"][int(name[1:])]
                if name == "kr":
                    return a["w_kr_t"]
                if name[:2] == "kv":
                    return a["w_kv_t"][int(name[2:])]
                if name[:2] == "mk":
                    return a["w_mk_t"][int(name[2:])]
                if name[:2] == "mv":
                    return a["w_mv_t"][int(name[3:])]
                if name[:2] == "mq":
                    return a["w_mq_t"][int(name[2:])]
                if name[:2] == "uq":
                    return a["w_uq_t"][int(name[2:])]
                if name == "uk":
                    return a["w_uk_t"]
                if name == "uv":
                    return a["w_uv_t"]
                j = int(name.split("_")[1])
                if name[0] == "g":
                    return a["w_gate_t"][8 * int(name[1]) + j]
                if name[:4] == "comx":
                    return a["w_como_t"][j]
                return a["w_xo_t"][j]

            sp.dma_start(ring[:, 0, :], src("glu_b0")).then_inc(ring_full[0], 16)
            sp.dma_start(xT[:, 0:4, :], a["xT"][:, 0:4, :]).then_inc(in_x, 16)
            sp.dma_start(xT[:, 4:8, :], a["xT"][:, 4:8, :]).then_inc(in_x, 16)
            for i, (name, n, _) in enumerate(ITEMS):
                if i == 0:
                    continue
                if i >= RING:
                    wait_job(sp, ITEMS[i - RING][2])
                sp.dma_start(ring[:, i % RING, 0:n], src(name)).then_inc(ring_full[i % RING], 16)
                if name == "glu_a0":
                    sp.dma_start(memT, a["memT"]).then_inc(in_mem, 16)
                if name == "g0_0":
                    wait_job(sp, "uv6")
                    sp.wait_ge(qk_ready, 8 + 8 + 7)
                    sp.wait_ge(kr_copied, 1)
                    sp.wait_ge(ur_rot, 2)
                    sp.wait_ge(lat_out, 64)
                    for b in range(2):
                        sp.dma_start(w13[b][:, 0], a["w_e1"][b].rearrange("(p k) f -> p k f", k=KT)).then_inc(we13[b], 16)
                        sp.dma_start(w13[b][:, 1], a["w_e3"][b].rearrange("(p k) f -> p k f", k=KT)).then_inc(we13[b], 16)
                        sp.dma_start(w2[b], a["w_e2"][b].rearrange("(p j) d -> p j d", j=2)).then_inc(we2[b], 16)
                if name == "g0_1":
                    sp.wait_ge(pv_done, MLA_LAST)
                    sp.dma_start(w_out, a["w_out"].rearrange("(k p) n -> p k n", p=128)).then_inc(in_wout, 16)
                    for b in range(2):
                        sp.dma_start(xtok[:, b, :], a["x_tok"][128 * b:128 * b + 128]).then_inc(in_xtok[b], 16)
            sp.wait_ge(merged_ready, 8)
            for n, name in enumerate(("g_ln1", "b_ln1", "g_ln2", "b_ln2")):
                sp.dma_start(lnbc[:, n, :], a[name].broadcast_to([128, D])).then_inc(in_ln, 16)
            for tt in range(2, NT):
                t0, nr = TILES[tt]
                sp.wait_ge(ln1_res, tt - 1)
                sp.dma_start(xtok[0:nr, tt % 2, :], a["x_tok"][t0:t0 + nr]).then_inc(in_xtok[tt % 2], 16)
            for tt in range(NT):
                t0, nr = TILES[tt]
                sp.wait_ge(x1_ready, tt + 1)
                for c in range(2):
                    sp.dma_start(x1_d[c * T + t0:c * T + t0 + nr], x1[0:nr, tt, :]).then_inc(x1_out, 16)

            with sp.Fori(1, NE // 2) as h:
                for b in range(2):
                    ee = h * 2 + b
                    sp.wait_ge(e_h, ee - 1)
                    sp.dma_start(w13[b][:, 0], a["w_e1"][bass.ds(ee, 1)].rearrange("a (p k) f -> p (a k) f", k=KT)).then_inc(we13[b], 16)
                    sp.dma_start(w13[b][:, 1], a["w_e3"][bass.ds(ee, 1)].rearrange("a (p k) f -> p (a k) f", k=KT)).then_inc(we13[b], 16)
                    sp.wait_ge(e_y, ee - 1)
                    sp.dma_start(w2[b], a["w_e2"][bass.ds(ee, 1)].rearrange("a (p j) d -> p (a j) d", j=2)).then_inc(we2[b], 16)

            sp.wait_ge(e_y, NE)
            sp.wait_ge(flag_ready, 1)
            over = sp.value_load(flag[0:1, 0:1], min_val=0, max_val=T)
            with sp.If(over > CAP):
                def load_again(e):
                    sp.dma_start(w13[0][:, 0], a["w_e1"][bass.ds(e, 1)].rearrange("a (p k) f -> p (a k) f", k=KT)).then_inc(ov_w, 16)
                    sp.dma_start(w13[0][:, 1], a["w_e3"][bass.ds(e, 1)].rearrange("a (p k) f -> p (a k) f", k=KT)).then_inc(ov_w, 16)
                    sp.dma_start(w2[0], a["w_e2"][bass.ds(e, 1)].rearrange("a (p j) d -> p (a j) d", j=2)).then_inc(ov_w, 16)

                load_again(0)
                with sp.Fori(1, NE) as e:
                    sp.wait_ge(ov_y, e * (NCH - 1))
                    load_again(e)
                sp.wait_ge(ov_out, 16 * NE * (NCH - 1))
            for b in range(2):
                sp.wait_ge(e_out[b], 16 * NE // 2)
            for tt in range(NT):
                t0, nr = TILES[tt]
                for c in range(2):
                    sp.dma_start(yab[0:nr, tt, c, :], y_d[c * T + t0:c * T + t0 + nr]).then_inc(in_y[tt], 16)
            for tt in range(NT):
                t0, nr = TILES[tt]
                sp.wait_ge(ln2_out, tt + 1)
                dst = o["y_prompt"][t0:t0 + nr] if tt < 4 else o["y_sample"]
                sp.dma_start(dst, x1[0:nr, tt, :]).then_inc(out_sem, 16)
            sp.wait_ge(conv_out, 32)
            sp.wait_ge(lat_out, 64)
            sp.wait_ge(mem_out, 32)
            sp.wait_ge(out_sem, 16 * NT)

        @block.tensor
        def _(pe):
            def begin(name):
                n = JOB[name]
                if n >= 4:
                    pe.wait_ge(*read_of(JOBS[n - 4]))

            def item(name):
                i = ITEM[name]
                pe.wait_ge(ring_full[i % RING], 16 * (i // RING + 1))
                return w_item(name)

            def gemm(name, w, rhs, nk, m=128, n=HT, halves=2):
                begin(name)
                for k in range(nk):
                    for s in range(halves):
                        mm = pe.matmul(half(name, s, m, n), w[:, k, :], rhs(k, s), start=(k == 0), stop=(k == nk - 1))
                mm.then_inc(job_done, 1)

            def x_half(k, s):
                return xT[:, k, HT * s:HT * s + HT]

            def on(buf):
                return lambda k, s: buf[:, k, HT * s:HT * s + HT]

            def proj(name, m=128):
                w = item(name)[:, 0:KT * m].rearrange("p (k m) -> p k m", k=KT)
                gemm(name, w, x_half, KT, m)

            def total(name, nk, buf):
                begin(name)
                for k in range(nk):
                    for s in range(2):
                        mm = pe.matmul(half(name, s), ones[:, :], buf[:, k, HT * s:HT * s + HT],
                                       start=(k == 0), stop=(k == nk - 1))
                mm.then_inc(job_done, 1)

            pe.wait_ge(in_x, 32)
            for c in range(4):
                proj(f"glu_b{c}")
                proj(f"glu_a{c}")
            for name in ("q0", "q1", "q2", "kv0", "kv1"):
                proj(name)
            proj("kr", 32)
            pe.wait_ge(const_ready, 6)
            pe.wait_ge(lat_sq, 3)
            total("q_ss", 3, sq)
            pe.wait_ge(lat_sq, 5)
            total("kv_ss", 2, rp)
            pe.wait_ge(in_mem, 16)
            for h in range(MH):
                w = item(f"mk{h}").rearrange("p (k m) -> p k m", k=KT)
                gemm(f"mk{h}", w, lambda k, s: memT[:, k, :], KT, n=MT, halves=1)
            pe.wait_ge(conv_raw, 4)
            total("conv_mean", 4, zT)
            begin("mv0")
            begin("mv1")
            for i in range(4):
                w = item(f"mv_{i}").rearrange("p (k n) -> p k n", k=2)
                for kk in range(2):
                    k = 2 * i + kk
                    for m in range(2):
                        mm = pe.matmul(half(f"mv{m}", 0, 128, 512), memT[:, k, 128 * m:128 * m + 128], w[:, kk, :],
                                       start=(k == 0), stop=(k == KT - 1))
                        if k == KT - 1:
                            mm.then_inc(job_done, 1)
            proj("mq0")
            proj("mq1")
            pe.wait_ge(conv_sq, 4)
            total("conv_var", 4, sq)
            proj("mq2")
            proj("mq3")

            def scores(n):
                kind, i, h = UNITS[n]
                t0, nr = TILES[i]
                if n >= 2:
                    pe.wait_ge(exp_done, n - 1)
                out = PS[0:nr, n % 2, :]
                if kind == "mem":
                    mm = pe.matmul(out[:, 0:MT], memq[:, h, t0:t0 + nr], mkT[:, i // 4, h, :], start=True, stop=True)
                elif i < 4:
                    nk = 128 * (i + 1)
                    pe.matmul(out[:, 0:nk], qh[0:QK, h, t0:t0 + nr], kh[0:QK, h, 0:nk], start=True, stop=True)
                    mm = pe.matmul(out[:, nk - CAUSAL:nk], rowmask[0:QK, :], negrow[0:QK, :], start=False, stop=True,
                                   skip_group_check=True)
                else:
                    mm = pe.matmul(out[:, 0:PAST + TS], qh[0:QK, h, t0:t0 + nr], kh[0:QK, h, TP:KEYS], start=True, stop=True)
                mm.then_inc(score_done, 1)

            def turn(n):
                kind, i, h = UNITS[n]
                nr = TILES[i][1]
                pe.wait_ge(exp_done, n + 1)
                if n >= 2:
                    pe.wait_ge(pt_evac, n - 1)
                kts = key_tiles(kind, i)
                for j, (_, c0, nk) in enumerate(kts):
                    mm = pe.transpose(PS[0:nk, 2 + n % 2, 128 * j:128 * j + nr], Pb[0:nr, n % 3, 128 * j:128 * j + nk],
                                      ident[0:nr, 0:nr])
                mm.then_inc(pt_done, 1)

            def values(n):
                kind, i, h = UNITS[n]
                nr = TILES[i][1]
                g = group_of[n]
                pe.wait_ge(pt_evac, n + 1)
                if h == 0 and g >= 2:
                    pe.wait_ge(o_norm, g - 1)
                kts = key_tiles(kind, i)
                w = MD if kind == "mem" else VD
                for j, (kt, _, nk) in enumerate(kts):
                    v = mv[0:nk, i // 4, kt, h * MD:(h + 1) * MD] if kind == "mem" else V[0:nk, kt, h * VD:(h + 1) * VD]
                    mm = pe.matmul(PS[0:nr, 4 + g % 2, h * w:(h + 1) * w], PT[0:nk, n % 3, 128 * j:128 * j + nr], v,
                                   start=(j == 0), stop=(j == len(kts) - 1))
                mm.then_inc(pv_done, 1)

            def turn_out(g):
                nr = TILES[GROUPS[g][1]][1]
                pe.wait_ge(o_norm, g + 1)
                if g >= 2:
                    pe.wait_ge(ot_evac, g - 1)
                for c in range(4):
                    mm = pe.transpose(PS[:, 6 + g % 2, 128 * c:128 * c + nr], osb[0:nr, g % 2, 128 * c:128 * c + 128],
                                      ident[0:nr, 0:nr])
                mm.then_inc(ot_done, 1)

            def attend(first, end):
                for n in range(first, end + 4):
                    if n < end:
                        scores(n)
                    if first <= n - 1 < end:
                        turn(n - 1)
                    if first <= n - 2 < end:
                        values(n - 2)
                    if first <= n - 3 < end and last_of_group[group_of[n - 3]] == n - 3:
                        turn_out(group_of[n - 3])

            def all_read():
                for name in JOBS[now - 4:now]:
                    pe.wait_ge(*read_of(name))

            now = JOB["mq3"] + 1
            all_read()
            pe.wait_ge(mem_proj, 10)
            pe.wait_ge(in_cache, 32)
            attend(0, MEM_LAST)
            pe.wait_ge(ot_evac, N_MEM_G)

            pe.wait_ge(qn_ready, 3)
            for i in range(3):
                w = item(f"uq{i}")[:, 0:768].rearrange("p (m k n) -> p m k n", m=2, k=3)
                for m in range(2):
                    gemm(f"un{2 * i + m}" if i < 2 else f"ur{m}", w[:, m], on(qd), 3)
            pe.wait_ge(ck_ready, 2)
            pe.wait_ge(in_past, 48)
            w = item("uk").rearrange("p (m k n) -> p m k n", m=4, k=2)
            for m in range(4):
                gemm(f"uk{m}", w[:, m], lambda k, s: ck[:, k, 416 * s:416 * s + 416], 2, n=416)
            w = item("uv").rearrange("p (k n) -> p k n", k=2)
            for kt in range(7):
                begin(f"uv{kt}")
                nk = 128 if kt < 6 else TS
                for k in range(2):
                    mm = pe.matmul(half(f"uv{kt}", 0, nk, 512), ck[:, k, 128 * kt:128 * kt + nk], w[:, k, :],
                                   start=(k == 0), stop=(k == 1))
                mm.then_inc(job_done, 1)
            now = JOB["uv6"] + 1
            all_read()
            pe.wait_ge(qk_ready, 8 + 8 + 7)
            pe.wait_ge(ur_rot, 2)
            pe.wait_ge(kr_copied, 1)
            attend(MEM_LAST, MLA_LAST)
            pe.wait_ge(ot_evac, N_G)
            pe.wait_ge(z_ready, 4)

            for j in range(8):
                proj(f"g0_{j}")
                w = item(f"comx_{j}").rearrange("p (b k m) -> p b k m", b=2, k=4)
                gemm(f"yc_{j}", w[:, 0], on(zT), 4)
                proj(f"g1_{j}")
                gemm(f"ym_{j}", w[:, 1], on(omT), 4)
                proj(f"g2_{j}")
                wx = item(f"xo_{j}")[:, 0:512].rearrange("p (k m) -> p k m", k=4)
                gemm(f"yx_{j}", wx, on(oxT), 4)

            def out_proj(tt):
                t0, nr = TILES[tt]
                begin(f"c{tt}")
                for k in range(KT):
                    for s in range(2):
                        mm = pe.matmul(half(f"c{tt}", s, nr, 512), merged[:, k, t0:t0 + nr], w_out[:, k, 512 * s:512 * s + 512],
                                       start=(k == 0), stop=(k == KT - 1))
                mm.then_inc(job_done, 1)

            def turn_x1(tt):
                nr = TILES[tt][1]
                begin(f"t{tt}")
                pe.wait_ge(x1_ready, tt + 1)
                for k in range(KT):
                    mm = pe.transpose(PS[:, 2 * (JOB[f"t{tt}"] % 4) + k // 4, 128 * (k % 4):128 * (k % 4) + nr],
                                      x1[0:nr, tt, 128 * k:128 * k + 128], ident[0:nr, 0:nr])
                mm.then_inc(job_done, 1)

            def router(tt):
                nr = TILES[tt][1]
                begin(f"l{tt}")
                pe.wait_ge(x1T_ready, tt + 1)
                for k in range(KT):
                    mm = pe.matmul(half(f"l{tt}", 0, nr, 36), x1T[:, tt % 2, k, 0:nr], wr[:, k, :],
                                   start=(k == 0), stop=(k == KT - 1))
                mm.then_inc(job_done, 1)

            pe.wait_ge(merged_ready, 8)
            pe.wait_ge(in_wout, 16)
            pe.wait_ge(in_route, 32)
            for name in JOBS[JOB["c0"]:JOB["rank"]]:
                {"c": out_proj, "t": turn_x1, "l": router}[name[0]](int(name[1:]))

            pe.wait_ge(mask_ready, 1)
            pe.wait_ge(route_const, 1)
            begin("rank")
            for tt in range(NT):
                for t2 in range(tt + 1):
                    nr = TILES[t2][1]
                    lhs = tri if t2 == tt else onesb
                    mm = pe.matmul(half("rank", 0, 128, 512)[:, 32 * tt:32 * tt + 32], lhs[0:nr, :], maskb[0:nr, t2, :],
                                   start=(t2 == 0), stop=(t2 == tt))
            mm.then_inc(job_done, 1)
            begin("count")
            for tt in range(NT):
                nr = TILES[tt][1]
                mm = pe.matmul(half("count", 0, 128, 32), onesb[0:nr, :], maskb[0:nr, tt, :], start=(tt == 0), stop=(tt == NT - 1))
            mm.then_inc(job_done, 1)
            now = JOB["count"] + 1
            all_read()

            def expert_turn_rows(b):
                for k in range(KT):
                    mm = pe.transpose(PS[:, k // 4, 128 * (k % 4):128 * (k % 4) + CAP],
                                      xg[0:CAP, b, :].rearrange("p (q k) -> p k q", k=KT)[:, k, :], ident[0:CAP, 0:CAP])
                return mm

            def expert_hidden(b):
                for k in range(KT):
                    mm = pe.matmul(PS[0:CAP, 2, :].rearrange("p (s f) -> p s f", s=2), xgT[:, k, 0:CAP], w13[b][:, :, k, :],
                                   start=(k == 0), stop=(k == KT - 1))
                return mm

            def expert_turn_hidden():
                for j in range(2):
                    mm = pe.transpose(PS[:, 3, 128 * j:128 * j + CAP], hm[0:CAP, :].rearrange("p (q j) -> p j q", j=2)[:, j, :],
                                      ident[0:CAP, 0:CAP])
                return mm

            def expert_result(b):
                for j in range(2):
                    for s in range(2):
                        mm = pe.matmul(PS[0:CAP, 4 + s, :], hT[:, j, 0:CAP], w2[b][:, j, 512 * s:512 * s + 512],
                                       start=(j == 0), stop=(j == 1))
                return mm

            def rows_step(e, b, k, first=False):
                pe.wait_ge(e_rows[b], 16 * k)
                if not first:
                    pe.wait_ge(e_xgT, e)
                    pe.wait_ge(e_xgT2, e)
                expert_turn_rows(b).then_inc(e_tx, 1)

            def hidden_step(e, b, k, first=False):
                pe.wait_ge(e_xgT, e + 1)
                pe.wait_ge(e_xgT2, e + 1)
                pe.wait_ge(we13[b], 32 * k)
                if not first:
                    pe.wait_ge(e_hm, e)
                expert_hidden(b).then_inc(e_h, 1)

            def hidden_turn_step(e, first=False):
                pe.wait_ge(e_hm, e + 1)
                if not first:
                    pe.wait_ge(e_hT, e)
                expert_turn_hidden().then_inc(e_ht, 1)

            def result_step(e, b, k):
                pe.wait_ge(e_hT, e + 1)
                pe.wait_ge(we2[b], 16 * k)
                pe.wait_ge(e_ya, e)
                pe.wait_ge(e_yb, e)
                expert_result(b).then_inc(e_y, 1)

            rows_step(0, 0, 1, first=True)
            hidden_step(0, 0, 1, first=True)
            rows_step(1, 1, 1)
            hidden_turn_step(0, first=True)
            def expert_pair(h):
                e = h * 2 + 1
                hidden_step(e, 1, h + 1)
                rows_step(e + 1, 0, h + 2)
                result_step(e - 1, 0, h + 1)
                hidden_turn_step(e)
                hidden_step(e + 1, 0, h + 2)
                rows_step(e + 2, 1, h + 2)
                result_step(e, 1, h + 1)
                hidden_turn_step(e + 1)

            expert_pair(0)
            with pe.Fori(1, NE // 2 - 1) as h:
                expert_pair(h)
            hidden_step(NE - 1, 1, NE // 2)
            result_step(NE - 2, 0, NE // 2)
            hidden_turn_step(NE - 1)
            result_step(NE - 1, 1, NE // 2)

            pe.wait_ge(flag_ready, 1)
            over = pe.value_load(flag[0:1, 0:1], min_val=0, max_val=T)
            with pe.If(over > CAP):
                pe.wait_ge(e_ya, NE)
                pe.wait_ge(e_yb, NE)
                with pe.Fori(0, NE) as e:
                    with pe.Fori(0, NCH - 1) as c:
                        n = e * (NCH - 1) + c
                        pe.wait_ge(ov_w, e * 48 + 48)
                        pe.wait_ge(ov_rows, n * 16 + 16)
                        expert_turn_rows(0).then_inc(ov_tx, 1)
                        pe.wait_ge(ov_xgT, n + 1)
                        expert_hidden(0).then_inc(ov_h, 1)
                        pe.wait_ge(ov_hm, n + 1)
                        expert_turn_hidden().then_inc(ov_ht, 1)
                        pe.wait_ge(ov_hT, n + 1)
                        expert_result(0).then_inc(ov_y, 1)

        @block.scalar
        def _(act):
            chain = [0]

            def link(ins):
                chain[0] += 1
                ins.then_inc(act_chain, 1)
                act.wait_ge(act_chain, chain[0])

            act.dma_start(U[:, :, PAD + TP:2 * PAD + TP], a["conv_state_T"]).then_inc(in_conv, 16)
            act.dma_start(wdw[:, :, :], a["w_dw_T"]).then_inc(in_conv, 16)
            for dst, name in ((vec, "conv_vec"), (gqa, "g_qa_T"), (gkva, "g_kva_T"), (bgate, "b_gate_T")):
                act.dma_start(dst[:], a[name]).then_inc(in_small, 16)
            act.dma_start(cos, a["rope_cos"]).then_inc(in_small, 16)
            act.dma_start(sin, a["rope_sin"]).then_inc(in_small, 16)
            act.dma_start(krot[:, TP:TP + PAST], a["past_krope_T"]).then_inc(in_past, 16)
            for c in range(2):
                act.dma_start(ck[:, c, TP:TP + PAST], a["past_lat_T"][c]).then_inc(in_past, 16)
            act.dma_start(mkT[:, 1], a["mem_k_T"]).then_inc(in_cache, 16)
            act.dma_start(mv[:, 1], a["cache_mem_v"]).then_inc(in_cache, 16)
            act.dma_start(wr[:, :, :], a["w_route"]).then_inc(in_route, 16)
            act.dma_start(rbias[:, :], a["b_route"].broadcast_to([128, 36])).then_inc(in_route, 16)

            for c in range(4):
                wait_job(act, f"glu_b{c}")
                act.activation(split(sq[:, c, :]), both(f"glu_b{c}"), ACT.Sigmoid).then_inc(glu_sig, 1)
            act.wait_ge(u_ready, 4)
            for i in range(3):
                wait_job(act, f"q{i}")
                act.activation(split(qd[:, i, :]), both(f"q{i}"), ACT.Copy).then_inc(lat_raw, 1)
                act.wait_ge(lat_raw, i + 1)
                act.activation(sq[:, i, :], qd[:, i, :], ACT.Square).then_inc(lat_sq, 1)
            for i in range(2):
                wait_job(act, f"kv{i}")
                act.activation(split(kvd[:, i, :]), both(f"kv{i}"), ACT.Copy).then_inc(lat_raw, 1)
                act.wait_ge(lat_raw, i + 4)
                act.activation(rp[:, i, :], kvd[:, i, :], ACT.Square).then_inc(lat_sq, 1)
            act.wait_ge(const_ready, 6)
            wait_job(act, "kr")
            act.activation(split(rp[0:32, 2, :]), both("kr", 32), ACT.Copy).then_inc(kr_raw, 1)
            wait_job(act, "q_ss")
            act.activation(split(norms[:, 2, :]), both("q_ss"), ACT.Sqrt, bias=eps[:, :], scale=1.0 / QL).then_inc(lat_std, 1)
            wait_job(act, "kv_ss")
            act.activation(split(norms[:, 3, :]), both("kv_ss"), ACT.Sqrt, bias=eps[:, :], scale=1.0 / KVL).then_inc(lat_std, 1)
            for h in range(MH):
                wait_job(act, f"mk{h}")
                act.activation(mkT[:, 0, h, :], half(f"mk{h}", 0, 128, MT), ACT.Copy).then_inc(mem_proj, 1)
            for m in range(2):
                wait_job(act, f"mv{m}")
                act.activation(mv[:, 0, m, :], half(f"mv{m}", 0, 128, 512), ACT.Copy).then_inc(mem_proj, 1)
            act.wait_ge(conv_cent, 4)
            for c in range(4):
                act.activation(sq[:, c, :], zT[:, c, :], ACT.Square).then_inc(conv_sq, 1)
            for h in range(2):
                wait_job(act, f"mq{h}")
                act.activation(split(memq[:, h, :]), both(f"mq{h}"), ACT.Copy, scale=MD ** -0.5).then_inc(mem_proj, 1)
            wait_job(act, "conv_var")
            act.activation(split(norms[:, 1, :]), both("conv_var"), ACT.Sqrt, bias=eps[:, :], scale=1.0 / CH).then_inc(conv_std, 1)
            for h in range(2, MH):
                wait_job(act, f"mq{h}")
                act.activation(split(memq[:, h, :]), both(f"mq{h}"), ACT.Copy, scale=MD ** -0.5).then_inc(mem_proj, 1)
            act.wait_ge(in_small, 96)
            for c in range(4):
                act.wait_ge(conv_norm, c + 1)
                act.activation(zT[:, c, :], zT[:, c, :], ACT.Silu, scale=vec[:, 1, c:c + 1],
                               bias=vec[:, 2, c:c + 1]).then_inc(z_ready, 1)

            def attend(first, end):
                for n in range(first, end + 5):
                    if n < end:
                        kind, i, h = UNITS[n]
                        nr = TILES[i][1]
                        nk = sum(k[2] for k in key_tiles(kind, i))
                        g = group_of[n]
                        act.wait_ge(max_done, n + 1)
                        if n >= 3:
                            act.wait_ge(pt_done, n - 2)
                        if h == 0 and g >= 2:
                            act.wait_ge(o_norm, g - 1)
                        act.activation(Pb[0:nr, n % 3, 0:nk], PS[0:nr, n % 2, 0:nk], ACT.Exp, bias=nb[0:nr, n % 8:n % 8 + 1],
                                       accum_out=rs[0:nr, g % 2, h:h + 1]).then_inc(exp_done, 1)
                    if first <= n - 4 < end and last_of_group[group_of[n - 4]] == n - 4:
                        g = group_of[n - 4]
                        kind, i = GROUPS[g]
                        t0, nr = TILES[i]
                        dst = (oxT if kind == "mem" else omT)[:, :, t0:t0 + nr]
                        act.wait_ge(ot_done, g + 1)
                        act.activation(dst, PS[:, 6 + g % 2, :].rearrange("p (c t) -> p c t", c=4)[:, :, 0:nr],
                                       ACT.Copy).then_inc(ot_evac, 1)

            act.wait_ge(conv_out, 32)
            attend(0, MEM_LAST)
            act.wait_ge(pv_done, MEM_LAST)
            act.wait_ge(mem_out, 32)
            act.wait_ge(z_ready, 4)
            act.wait_ge(qn_ready, 3)
            act.wait_ge(ck_ready, 2)
            act.wait_ge(krot_ready, 1)
            act.wait_ge(in_past, 48)
            for i in range(4):
                wait_job(act, f"un{i}")
                for s in range(2):
                    act.activation(split(qh[0:64, 2 * i + s, :]), PS[64 * s:64 * s + 64, 2 * (JOB[f"un{i}"] % 4):2 * (JOB[f"un{i}"] % 4) + 2, 0:HT],
                                   ACT.Copy, scale=QK ** -0.5).then_inc(qk_ready, 1)
            for i in range(2):
                wait_job(act, f"ur{i}")
                if i:
                    act.wait_ge(ur_rot, 1)
                act.activation(split(rp[:, 0, :]), both(f"ur{i}"), ACT.Copy, scale=QK ** -0.5).then_inc(ur_raw, 1)
            for i in range(4):
                wait_job(act, f"uk{i}")
                for s in range(2):
                    act.activation(kh[0:64, 2 * i + s, :].rearrange("p (s t) -> p s t", s=2),
                                   PS[64 * s:64 * s + 64, 2 * (JOB[f"uk{i}"] % 4):2 * (JOB[f"uk{i}"] % 4) + 2, 0:416],
                                   ACT.Copy).then_inc(qk_ready, 1)
            for i in range(7):
                nk = 128 if i < 6 else TS
                wait_job(act, f"uv{i}")
                act.activation(V[0:nk, i, :], half(f"uv{i}", 0, nk, 512), ACT.Copy).then_inc(qk_ready, 1)
            attend(MEM_LAST, MLA_LAST)
            for j in range(8):
                for n in range(3):
                    wait_job(act, f"g{n}_{j}")
                    if j >= 2:
                        act.wait_ge(merged_ready, j - 1)
                    act.activation(split(gate[:, j % 2, n, :]), both(f"g{n}_{j}"), ACT.Sigmoid,
                                   bias=bgate[:, 8 * n + j:8 * n + j + 1]).then_inc(gate_sig, 1)
            for tt in range(NT + 1):
                if tt < NT:
                    nr = TILES[tt][1]
                    act.wait_ge(ln1_var, tt + 1)
                    act.activation(rstd[0:nr, tt % 2, 0:1], mva[0:nr, tt % 2, 1:2], ACT.Sqrt, bias=eps[0:nr, :]).then_inc(ln1_std, 1)
                if tt >= 1:
                    u = tt - 1
                    nr = TILES[u][1]
                    wait_job(act, f"t{u}")
                    if u >= 2:
                        wait_job(act, f"l{u - 2}")
                    act.activation(x1T[:, u % 2, :, 0:nr].rearrange("p (s k) t -> p s k t", s=2),
                                   pair(f"t{u}").rearrange("p s (k t) -> p s k t", k=4)[:, :, :, 0:nr], ACT.Copy).then_inc(x1T_ready, 1)
            act.wait_ge(route_dve, 1)
            act.activation(g4[:, 1], g4[:, 0], ACT.Exp).then_inc(route_exp, 1)
            act.wait_ge(route_dve, 2)
            act.activation(gm[:, 5], gm[:, 4], ACT.Exp).then_inc(route_exp, 1)

            def evac_rows(half_no):
                src = PS[:, half_no, :].rearrange("p (k t) -> p k t", k=4)[:, :, 0:CAP]
                return act.activation(xgT[:, 4 * half_no:4 * half_no + 4, 0:CAP], src, ACT.Copy)

            def silu():
                return act.activation(hg[0:CAP, :], PS[0:CAP, 2, 0:FE], ACT.Silu)

            def evac_hidden():
                return act.activation(hT[:, :, 0:CAP], PS[:, 3, 0:256].rearrange("p (j t) -> p j t", j=2)[:, :, 0:CAP], ACT.Copy)

            def evac_result(b, s):
                return act.activation(ysb[0:CAP, b, 512 * s:512 * s + 512], PS[0:CAP, 4 + s, :], ACT.Copy)

            def rows_step(e):
                act.wait_ge(e_tx, e + 1)
                act.wait_ge(e_h, e)
                evac_rows(0).then_inc(e_xgT, 1)

            def silu_step(e):
                act.wait_ge(e_h, e + 1)
                act.wait_ge(e_hm, e)
                silu().then_inc(e_silu, 1)

            def hidden_turn_step(e):
                act.wait_ge(e_ht, e + 1)
                act.wait_ge(e_y, e)
                evac_hidden().then_inc(e_hT, 1)

            def result_step(e, b, k):
                act.wait_ge(e_y, e + 1)
                act.wait_ge(e_out[b], 16 * k)
                evac_result(b, 0).then_inc(e_ya, 1)

            rows_step(0)
            silu_step(0)
            rows_step(1)
            hidden_turn_step(0)
            def expert_pair(h):
                e = h * 2 + 1
                silu_step(e)
                rows_step(e + 1)
                result_step(e - 1, 0, h)
                hidden_turn_step(e)
                silu_step(e + 1)
                rows_step(e + 2)
                result_step(e, 1, h)
                hidden_turn_step(e + 1)

            expert_pair(0)
            with act.Fori(1, NE // 2 - 1) as h:
                expert_pair(h)
            silu_step(NE - 1)
            result_step(NE - 2, 0, NE // 2 - 1)
            hidden_turn_step(NE - 1)
            result_step(NE - 1, 1, NE // 2 - 1)
            act.wait_ge(flag_ready, 1)
            over = act.value_load(flag[0:1, 0:1], min_val=0, max_val=T)
            with act.If(over > CAP):
                with act.Fori(0, NE * (NCH - 1)) as n:
                    act.wait_ge(ov_tx, n + 1)
                    link_free = evac_rows(0)
                    evac_rows(1).then_inc(ov_xgT, 1)
                    act.wait_ge(ov_h, n + 1)
                    silu().then_inc(ov_silu, 1)
                    act.wait_ge(ov_ht, n + 1)
                    evac_hidden().then_inc(ov_hT, 1)
                    act.wait_ge(ov_y, n + 1)
                    evac_result(0, 0)
                    evac_result(0, 1).then_inc(ov_ysb, 1)
            for tt in range(NT):
                nr = TILES[tt][1]
                act.wait_ge(ln2_var, tt + 1)
                act.activation(rstd[0:nr, tt % 2, 0:1], mva[0:nr, tt % 2, 1:2], ACT.Sqrt, bias=eps[0:nr, :]).then_inc(ln2_std, 1)

        @block.vector
        def _(dve):
            chain = [0]

            def link(ins):
                chain[0] += 1
                ins.then_inc(dve_chain, 1)
                dve.wait_ge(dve_chain, chain[0])

            dve.wait_ge(in_conv, 32)
            dve.wait_ge(in_small, 96)
            dve.wait_ge(const_ready, 6)
            for c in range(4):
                wait_job(dve, f"glu_a{c}")
                dve.wait_ge(glu_sig, c + 1)
                dve.tensor_tensor(U[:, c, PAD:PAD + HT], half(f"glu_a{c}", 0), sq[:, c, 0:HT], ALU.mult)
                dve.tensor_tensor(U[:, c, PAD + HT:PAD + TP], half(f"glu_a{c}", 1, 128, TP - HT), sq[:, c, HT:TP], ALU.mult)
                dve.tensor_tensor(U[:, c, 2 * PAD + TP:UW], both(f"glu_a{c}")[:, 1, TP - HT:HT], sq[:, c, TP:T],
                                  ALU.mult).then_inc(u_ready, 1)
                dve.wait_ge(u_ready, c + 1)
                for j in range(CW):
                    parts = ((zT[:, c, 0:TP], U[:, c, j:j + TP]),
                             (zT[:, c, TP:T], U[:, c, PAD + TP + j:PAD + TP + j + TS]))
                    for dst, src in parts:
                        if j == 0:
                            ins = dve.tensor_scalar(dst, src, wdw[:, c, 0:1], vec[:, 0, c:c + 1], ALU.mult, ALU.add)
                        else:
                            ins = dve.scalar_tensor_tensor(dst, src, wdw[:, c, j:j + 1], dst, ALU.mult, ALU.add)
                    if j < CW - 1:
                        link(ins)
                ins.then_inc(conv_raw, 1)

            dve.wait_ge(lat_std, 1)
            link(dve.reciprocal(norms[:, 2, :], norms[:, 2, :]))
            dve.wait_ge(lat_raw, 5)
            for i in range(3):
                dve.scalar_tensor_tensor(qd[:, i, :], qd[:, i, :], gqa[:, i:i + 1], norms[:, 2, :], ALU.mult,
                                         ALU.mult).then_inc(qn_ready, 1)
            dve.wait_ge(lat_std, 2)
            link(dve.reciprocal(norms[:, 3, :], norms[:, 3, :]))
            for i in range(2):
                dve.scalar_tensor_tensor(ck[:, i, 0:TP], kvd[:, i, 0:TP], gkva[:, i:i + 1], norms[:, 3, 0:TP], ALU.mult, ALU.mult)
                dve.scalar_tensor_tensor(ck[:, i, TP + PAST:KEYS], kvd[:, i, TP:T], gkva[:, i:i + 1], norms[:, 3, TP:T],
                                         ALU.mult, ALU.mult).then_inc(ck_ready, 1)
            swap = list(range(16, 32)) + list(range(16))
            dve.wait_ge(kr_raw, 1)
            wait_job(dve, "kv_ss")
            link(dve.stream_shuffle(rp[0:32, 1, :], rp[0:32, 2, :], swap))
            dve.tensor_tensor(rp[0:32, 2, :], rp[0:32, 2, :], cos[0:32, :], ALU.mult)
            link(dve.tensor_tensor(rp[0:32, 1, :], rp[0:32, 1, :], sin[0:32, :], ALU.mult))
            dve.tensor_tensor(krot[:, 0:TP], rp[0:32, 2, 0:TP], rp[0:32, 1, 0:TP], ALU.add)
            dve.tensor_tensor(krot[:, TP + PAST:KEYS], rp[0:32, 2, TP:T], rp[0:32, 1, TP:T], ALU.add).then_inc(krot_ready, 1)

            wait_job(dve, "conv_mean")
            dve.tensor_scalar(split(norms[:, 0, :]), both("conv_mean"), 1.0 / CH, None, ALU.mult).then_inc(mean_read, 1)
            dve.wait_ge(mean_read, 1)
            for c in range(4):
                dve.tensor_tensor(zT[:, c, :], zT[:, c, :], norms[:, 0, :], ALU.subtract).then_inc(conv_cent, 1)
            dve.wait_ge(conv_std, 1)
            link(dve.reciprocal(norms[:, 1, :], norms[:, 1, :]))
            dve.wait_ge(conv_cent, 4)
            dve.wait_ge(conv_sq, 4)
            for c in range(4):
                dve.tensor_tensor(zT[:, c, :], zT[:, c, :], norms[:, 1, :], ALU.mult).then_inc(conv_norm, 1)

            def row_max(n):
                kind, i, h = UNITS[n]
                nr = TILES[i][1]
                nk = sum(k[2] for k in key_tiles(kind, i))
                dve.wait_ge(score_done, n + 1)
                if n >= 8:
                    dve.wait_ge(exp_done, n - 7)
                dve.tensor_reduce(nb[0:nr, n % 8:n % 8 + 1], PS[0:nr, n % 2, 0:nk], AX.X, ALU.max, negate=True).then_inc(max_done, 1)

            def evac_probs(n):
                kind, i, h = UNITS[n]
                nr = TILES[i][1]
                kts = key_tiles(kind, i)
                dve.wait_ge(pt_done, n + 1)
                if n >= 3:
                    dve.wait_ge(pv_done, n - 2)
                full = len([k for k in kts if k[2] == 128])
                src = PS[:, 2 + n % 2, :].rearrange("p (k t) -> p k t", k=4)
                dst = PT[:, n % 3, :].rearrange("p (k t) -> p k t", k=4)
                ins = dve.tensor_copy(dst[:, 0:full, 0:nr], src[:, 0:full, 0:nr])
                if full < len(kts):
                    ins = dve.tensor_copy(dst[0:TS, full, 0:nr], src[0:TS, full, 0:nr])
                ins.then_inc(pt_evac, 1)

            def normalise(g):
                kind, i = GROUPS[g]
                nr = TILES[i][1]
                heads, w = (MH, MD) if kind == "mem" else (NH, VD)
                dve.wait_ge(exp_done, last_of_group[g] + 1)
                link(dve.reciprocal(rinv[0:nr, g % 2, 0:heads], rs[0:nr, g % 2, 0:heads]))
                dve.wait_ge(pv_done, last_of_group[g] + 1)
                if g >= 2:
                    dve.wait_ge(ot_done, g - 1)
                dve.tensor_tensor(osb[0:nr, g % 2, :].rearrange("p (h v) -> p h v", h=heads),
                                  PS[0:nr, 4 + g % 2, :].rearrange("p (h v) -> p h v", h=heads),
                                  rinv[0:nr, g % 2, 0:heads].unsqueeze(2).to_broadcast([nr, heads, w]), ALU.mult).then_inc(o_norm, 1)

            def attend(first, end):
                for n in range(first, end + 3):
                    if n < end:
                        row_max(n)
                    if first <= n - 1 < end:
                        evac_probs(n - 1)
                    if first <= n - 2 < end and last_of_group[group_of[n - 2]] == n - 2:
                        normalise(group_of[n - 2])

            attend(0, MEM_LAST)
            for i in range(2):
                dve.wait_ge(ur_raw, i + 1)
                link(dve.stream_shuffle(rp[:, 1, :], rp[:, 0, :], swap))
                dve.tensor_tensor(rp[:, 0, :], rp[:, 0, :], cos, ALU.mult)
                link(dve.tensor_tensor(rp[:, 1, :], rp[:, 1, :], sin, ALU.mult))
                for q in range(4):
                    ins = dve.tensor_tensor(qh[64:96, 4 * i + q, :], rp[32 * q:32 * q + 32, 0, :], rp[32 * q:32 * q + 32, 1, :], ALU.add)
                ins.then_inc(ur_rot, 1)
            attend(MEM_LAST, MLA_LAST)

            for j in range(8):
                for n, name in enumerate(("yc", "ym", "yx")):
                    wait_job(dve, f"{name}_{j}")
                    dve.wait_ge(gate_sig, 3 * j + n + 1)
                    dve.tensor_tensor(split(gate[:, j % 2, n, :]), split(gate[:, j % 2, n, :]), both(f"{name}_{j}"),
                                      ALU.mult).then_inc(gate_mul, 1)

            link(dve.memset(lg[:, :, :], 0.0))
            for tt in range(NT + 2):
                if tt < NT:
                    t0, nr = TILES[tt]
                    wait_job(dve, f"c{tt}")
                    dve.wait_ge(in_xtok[tt % 2], 16 * (tt // 2 + 1))
                    dve.scalar_tensor_tensor(x1[0:nr, tt, :].rearrange("p (s d) -> p s d", s=2),
                                             xtok[0:nr, tt % 2, :].rearrange("p (s d) -> p s d", s=2), ALPHA,
                                             pair(f"c{tt}")[0:nr], ALU.mult, ALU.add).then_inc(ln1_res, 1)
                    dve.wait_ge(ln1_res, tt + 1)
                    dve.bn_stats(st[0:nr, tt % 2, 0, :], x1[0:nr, tt, 0:512])
                    link(dve.bn_stats(st[0:nr, tt % 2, 1, :], x1[0:nr, tt, 512:1024]))
                    dve.bn_aggr(mva[0:nr, tt % 2, :], st[0:nr, tt % 2, :, :].rearrange("p a b -> p (a b)")).then_inc(ln1_var, 1)
                    dve.wait_ge(ln1_std, tt + 1)
                    link(dve.reciprocal(rstd[0:nr, tt % 2, 1:2], rstd[0:nr, tt % 2, 0:1]))
                    dve.tensor_scalar(x1[0:nr, tt, :], x1[0:nr, tt, :], mva[0:nr, tt % 2, 0:1], rstd[0:nr, tt % 2, 1:2],
                                      ALU.subtract, ALU.mult).then_inc(ln1_hat, 1)
                if tt >= 2:
                    u = tt - 2
                    nr = TILES[u][1]
                    wait_job(dve, f"l{u}")
                    dve.tensor_tensor(lg[0:nr, u, :], half(f"l{u}", 0, nr, 36), rbias[0:nr, :], ALU.add).then_inc(lg_ready, 1)

            def wide(x, n):
                return x.unsqueeze(2).to_broadcast([128, NT, n])

            def first_max(x, n, m, cand, onehot):
                link(dve.tensor_reduce(gm[:, m], x, AX.X, ALU.max))
                link(dve.tensor_tensor(cand, x, wide(gm[:, m], n), ALU.is_equal))
                link(dve.tensor_tensor(cand, cand, desc[:, NE_G - n:].unsqueeze(1).to_broadcast([128, NT, n]), ALU.mult))
                link(dve.tensor_reduce(gm[:, 11], cand, AX.X, ALU.max))
                link(dve.tensor_tensor(onehot, cand, wide(gm[:, 11], n), ALU.is_equal))

            dve.wait_ge(lg_ready, NT)
            dve.wait_ge(route_const, 1)
            first_max(lg[:, :, 0:NG], NG, 0, g4[:, 0], g4[:, 2])
            dve.tensor_tensor(g4[:, 0], lg[:, :, 0:NG], wide(gm[:, 0], NG), ALU.subtract).then_inc(route_dve, 1)
            prod = e32[:, 3].rearrange("p t (g e) -> p t g e", g=NG)
            for g in range(NG):
                ins = dve.tensor_tensor(prod[:, :, g, :], lg[:, :, NG + 8 * g:NG + 8 * g + 8],
                                        wide(g4[:, 2, :, g], NE_G), ALU.mult)
            link(ins)
            link(dve.tensor_reduce(e8[:, 0], prod.rearrange("p t g e -> p t e g"), AX.X, ALU.add))
            first_max(e8[:, 0], NE_G, 1, e8[:, 1], e8[:, 2])
            link(dve.scalar_tensor_tensor(e8[:, 0], e8[:, 2], -1e30, e8[:, 0], ALU.mult, ALU.add))
            first_max(e8[:, 0], NE_G, 2, e8[:, 1], e8[:, 3])
            dve.tensor_tensor(gm[:, 4], gm[:, 2], gm[:, 1], ALU.subtract).then_inc(route_dve, 1)
            for c in range(2):
                hot = e32[:, c].rearrange("p t (g e) -> p t g e", g=NG)
                for g in range(NG):
                    ins = dve.tensor_tensor(hot[:, :, g, :], e8[:, 2 + c], wide(g4[:, 2, :, g], NE_G), ALU.mult)
            link(ins)
            dve.tensor_tensor(maskb[:, :, :], e32[:, 0], e32[:, 1], ALU.add).then_inc(mask_ready, 1)
            dve.wait_ge(route_exp, 2)
            link(dve.tensor_reduce(gm[:, 6], g4[:, 1], AX.X, ALU.add))
            dve.reciprocal(gm[:, 6], gm[:, 6])
            link(dve.tensor_scalar(gm[:, 7], gm[:, 5], 1.0, None, ALU.add))
            link(dve.reciprocal(gm[:, 7], gm[:, 7]))
            link(dve.tensor_tensor(wsel[:, 0, :], gm[:, 6], gm[:, 7], ALU.mult))
            dve.tensor_tensor(wsel[:, 1, :], wsel[:, 0, :], gm[:, 5], ALU.mult)
            wait_job(dve, "count")
            rank = half("rank", 0, 128, 160).rearrange("p (t e) -> p t e", t=NT)
            for c in range(2):
                link(dve.tensor_tensor(e32[:, 2], e32[:, c], rank, ALU.mult))
                dve.tensor_reduce(gm[:, 8], e32[:, 2], AX.X, ALU.add)
                link(dve.tensor_tensor(e32[:, 3], e32[:, c], idx32[:, :].unsqueeze(1).to_broadcast([128, NT, NE]), ALU.mult))
                link(dve.tensor_reduce(gm[:, 9], e32[:, 3], AX.X, ALU.add))
                link(dve.tensor_scalar(gm[:, 10], gm[:, 8], float(CAP), None, ALU.is_ge))
                for k in range(2, NCH):
                    link(dve.scalar_tensor_tensor(gm[:, 10], gm[:, 8], float(k * CAP), gm[:, 10], ALU.is_ge, ALU.add))
                link(dve.scalar_tensor_tensor(gm[:, 8], gm[:, 10], -float(CAP), gm[:, 8], ALU.mult, ALU.add))
                link(dve.scalar_tensor_tensor(gm[:, 9], gm[:, 8], float(NCH * NE), gm[:, 9], ALU.mult, ALU.add))
                dve.scalar_tensor_tensor(addr[:, c, :], gm[:, 10], float(NE), gm[:, 9], ALU.mult, ALU.add).then_inc(addr_ready, 1)
                dve.wait_ge(addr_ready, c + 1)
            dve.tensor_reduce(flag[:, :], half("count", 0, 128, NE), AX.X, ALU.max).then_inc(flag_ready, 1)
            dve.wait_ge(flag_ready, 1)

            def evac_rows():
                return dve.tensor_copy(xgT[:, 4:8, 0:CAP], PS[:, 1, :].rearrange("p (k t) -> p k t", k=4)[:, :, 0:CAP])

            def hidden():
                return dve.tensor_tensor(hm[0:CAP, :], hg[0:CAP, :], PS[0:CAP, 2, FE:2 * FE], ALU.mult)

            def rows_step(e):
                dve.wait_ge(e_tx, e + 1)
                dve.wait_ge(e_h, e)
                evac_rows().then_inc(e_xgT2, 1)

            def hidden_step(e):
                dve.wait_ge(e_silu, e + 1)
                dve.wait_ge(e_ht, e)
                hidden().then_inc(e_hm, 1)

            def result_step(e, b, k):
                dve.wait_ge(e_y, e + 1)
                dve.wait_ge(e_out[b], 16 * k)
                dve.tensor_copy(ysb[0:CAP, b, 512:1024], PS[0:CAP, 5, :]).then_inc(e_yb, 1)

            rows_step(0)
            hidden_step(0)
            rows_step(1)
            def expert_pair(h):
                e = h * 2 + 1
                hidden_step(e)
                rows_step(e + 1)
                result_step(e - 1, 0, h)
                hidden_step(e + 1)
                rows_step(e + 2)
                result_step(e, 1, h)

            expert_pair(0)
            with dve.Fori(1, NE // 2 - 1) as h:
                expert_pair(h)
            hidden_step(NE - 1)
            result_step(NE - 2, 0, NE // 2 - 1)
            result_step(NE - 1, 1, NE // 2 - 1)
            over = dve.value_load(flag[0:1, 0:1], min_val=0, max_val=T)
            with dve.If(over > CAP):
                with dve.Fori(0, NE * (NCH - 1)) as n:
                    dve.wait_ge(ov_silu, n + 1)
                    hidden().then_inc(ov_hm, 1)

            dve.wait_ge(x1_scaled, NT)
            for tt in range(NT):
                nr = TILES[tt][1]
                dve.wait_ge(in_y[tt], 32)
                for c in range(2):
                    link(dve.scalar_tensor_tensor(x1[0:nr, tt, :], yab[0:nr, tt, c, :], wsel[0:nr, c, tt:tt + 1], x1[0:nr, tt, :],
                                                  ALU.mult, ALU.add))
                dve.bn_stats(st[0:nr, tt % 2, 0, :], x1[0:nr, tt, 0:512])
                link(dve.bn_stats(st[0:nr, tt % 2, 1, :], x1[0:nr, tt, 512:1024]))
                dve.bn_aggr(mva[0:nr, tt % 2, :], st[0:nr, tt % 2, :, :].rearrange("p a b -> p (a b)")).then_inc(ln2_var, 1)
                dve.wait_ge(ln2_std, tt + 1)
                link(dve.reciprocal(rstd[0:nr, tt % 2, 1:2], rstd[0:nr, tt % 2, 0:1]))
                link(dve.tensor_scalar(x1[0:nr, tt, :], x1[0:nr, tt, :], mva[0:nr, tt % 2, 0:1], rstd[0:nr, tt % 2, 1:2],
                                       ALU.subtract, ALU.mult))
                dve.tensor_tensor(x1[0:nr, tt, :], x1[0:nr, tt, :], lnbc[0:nr, 2, :], ALU.mult).then_inc(ln2_hat, 1)

        @block.gpsimd
        def _(pool):
            chain = [0]

            def link(ins):
                chain[0] += 1
                ins.then_inc(pool_chain, 1)
                pool.wait_ge(pool_chain, chain[0])

            pool.memset(ones[:, :], 1.0).then_inc(const_ready, 1)
            pool.memset(eps[:, :], EPS).then_inc(const_ready, 1)
            pool.memset(U[:, :, 0:PAD], 0.0).then_inc(const_ready, 1)
            pool.memset(ident[:, :], 0.0)
            pool.memset(rowmask[:, :], 0.0)
            link(pool.memset(negrow[:, :], 0.0))
            pool.affine_select(out=ident[:, :], in_=ident[:, :], compare_op=ALU.not_equal, fill=1.0, base=0,
                               pattern=[[-1, 128]], channel_multiplier=1).then_inc(const_ready, 1)
            pool.memset(rowmask[0:1, 0:CAUSAL], 1.0).then_inc(const_ready, 1)
            pool.memset(negrow[0:1, :], -1e30).then_inc(const_ready, 1)
            pool.memset(onesb[:, :], 1.0)
            link(pool.memset(tri[:, :], 1.0))
            pool.affine_select(out=tri[:, :], in_=tri[:, :], compare_op=ALU.is_gt, fill=0.0, base=0,
                               pattern=[[1, 128]], channel_multiplier=-1)
            for i in range(NE_G):
                pool.memset(desc[:, i:i + 1], float(NE_G - i))
            for i in range(NE):
                pool.memset(idx32[:, i:i + 1], float(i))
            pool.iota(rowid[:, 0, :], pattern=[[128, NT]], base=0, channel_multiplier=1)
            pool.iota(rowid[:, 1, :], pattern=[[128, NT]], base=T, channel_multiplier=1)
            pool.memset(tab0[:, :], SKIP).then_inc(route_const, 1)
            pool.wait_ge(route_const, 1)
            pool.dma_start(tab_d.rearrange("(p n) a -> p (n a)", p=CAP), tab0[0:CAP, :]).then_inc(tab_init, 16)

            pool.wait_ge(u_ready, 4)
            pool.dma_start(o["conv_prompt_T"], U[:, :, TP:TP + PAD]).then_inc(conv_out, 16)
            pool.dma_start(o["conv_sample_T"], U[:, :, UW - PAD:UW]).then_inc(conv_out, 16)
            pool.wait_ge(ck_ready, 2)
            pool.dma_start(o["latent_T"][:, :, 0:TP], ck[:, :, 0:TP]).then_inc(lat_out, 16)
            pool.dma_start(o["latent_T"][:, :, TP:T], ck[:, :, TP + PAST:KEYS]).then_inc(lat_out, 16)
            pool.wait_ge(krot_ready, 1)
            pool.dma_start(o["krope_T"][:, 0:TP], krot[:, 0:TP]).then_inc(lat_out, 16)
            pool.dma_start(o["krope_T"][:, TP:T], krot[:, TP + PAST:KEYS]).then_inc(lat_out, 16)
            pool.wait_ge(mem_proj, 6)
            pool.dma_start(o["mem_k_T"], mkT[:, 0]).then_inc(mem_out, 16)
            pool.dma_start(o["mem_v"], mv[:, 0]).then_inc(mem_out, 16)
            pool.wait_ge(pv_done, MEM_LAST)
            pool.wait_ge(mem_out, 32)
            pool.wait_ge(in_past, 48)
            pool.tensor_copy(kh[64:96, :, :], krot.unsqueeze(1).to_broadcast([32, NH, KEYS])).then_inc(kr_copied, 1)

            for j in range(8):
                pool.wait_ge(gate_mul, 3 * j + 2)
                link(pool.tensor_tensor(gate[:, j % 2, 0, :], gate[:, j % 2, 0, :], gate[:, j % 2, 1, :], ALU.add))
                pool.wait_ge(gate_mul, 3 * j + 3)
                pool.tensor_tensor(merged[:, j, :], gate[:, j % 2, 0, :], gate[:, j % 2, 2, :], ALU.add).then_inc(merged_ready, 1)
            pool.wait_ge(in_ln, 64)
            for tt in range(NT):
                nr = TILES[tt][1]
                pool.wait_ge(ln1_hat, tt + 1)
                link(pool.tensor_tensor(x1[0:nr, tt, :], x1[0:nr, tt, :], lnbc[0:nr, 0, :], ALU.mult))
                pool.tensor_tensor(x1[0:nr, tt, :], x1[0:nr, tt, :], lnbc[0:nr, 1, :], ALU.add).then_inc(x1_ready, 1)

            link(pool.memset(xg[:, :, :], 0.0))
            pool.wait_ge(tab_init, 16)
            for c in range(2):
                pool.wait_ge(addr_ready, c + 1)
                for tt in range(NT):
                    nr = TILES[tt][1]
                    pool.indirect_dma_start(tab_d, bass.IndirectOffsetOnAxis(ap=addr[0:nr, c, tt:tt + 1], axis=0),
                                            rowid[0:nr, c, tt:tt + 1], None).then_inc(tab_written, 16)
            pool.wait_ge(tab_written, 16 * 2 * NT)
            pool.dma_start(tabs[0:CAP, :], tab_d.rearrange("(p n) a -> p (n a)", p=CAP)).then_inc(tab_loaded, 16)
            pool.wait_ge(tab_loaded, 16)
            pool.wait_ge(x1_out, 16 * 2 * NT)

            def gather(b, col):
                return pool.indirect_dma_start(xg[0:CAP, b, :], None, x1_d,
                                               bass.IndirectOffsetOnAxis(ap=tabs[0:CAP, col:col + 1], axis=0),
                                               bounds_check=2 * T - 1, oob_is_err=False)

            def scatter(b, col):
                return pool.indirect_dma_start(y_d, bass.IndirectOffsetOnAxis(ap=tabs[0:CAP, col:col + 1], axis=0),
                                               ysb[0:CAP, b, :], None, bounds_check=2 * T - 1, oob_is_err=False)

            gather(0, 0).then_inc(e_rows[0], 16)
            gather(1, 1).then_inc(e_rows[1], 16)
            for tt in range(NT):
                nr = TILES[tt][1]
                pool.tensor_scalar(x1[0:nr, tt, :], x1[0:nr, tt, :], ALPHA, None, ALU.mult).then_inc(x1_scaled, 1)
            for e in range(NE):
                b = e % 2
                if e + 2 < NE:
                    pool.wait_ge(e_tx, e + 1)
                    gather(b, e + 2).then_inc(e_rows[b], 16)
                pool.wait_ge(e_ya, e + 1)
                pool.wait_ge(e_yb, e + 1)
                scatter(b, e).then_inc(e_out[b], 16)
            pool.wait_ge(flag_ready, 1)
            over = pool.value_load(flag[0:1, 0:1], min_val=0, max_val=T)
            with pool.If(over > CAP):
                for b in range(2):
                    pool.wait_ge(e_out[b], 16 * NE // 2)
                for e in range(NE):
                    for c in range(1, NCH):
                        n = e * (NCH - 1) + c - 1
                        gather(0, c * NE + e).then_inc(ov_rows, 16)
                        pool.wait_ge(ov_ysb, n + 1)
                        scatter(0, c * NE + e).then_inc(ov_out, 16)
                        pool.wait_ge(ov_out, 16 * (n + 1))
            for tt in range(NT):
                nr = TILES[tt][1]
                pool.wait_ge(ln2_hat, tt + 1)
                pool.tensor_tensor(x1[0:nr, tt, :], x1[0:nr, tt, :], lnbc[0:nr, 3, :], ALU.add).then_inc(ln2_out, 1)



def lay_out(x):
    def m_tiles(w):
        K, M = w.shape
        return w.reshape(K // 128, 128, M // 128, 128).transpose(2, 1, 0, 3).reshape(M // 128, 128, K)

    def fm(v):
        return v.reshape(-1, 128).T

    w = x["w_in"][0]
    c = np.cumsum([0, CH, CH, QL, KVL, ROPE, MH * MD, 3 * D])
    r = {}
    xs = np.concatenate([x["x_prompt"][0], x["x_sample"][0]], 0)
    r["x_tok"] = xs
    r["xT"] = xs.T.reshape(KT, 128, T).transpose(1, 0, 2)
    r["memT"] = x["mem_prompt"][0].T.reshape(KT, 128, MT).transpose(1, 0, 2)
    r["w_glu_t"] = np.concatenate([m_tiles(w[:, c[1]:c[2]]), m_tiles(w[:, c[0]:c[1]])], 0)
    r["w_q_t"] = m_tiles(w[:, c[2]:c[3]])
    r["w_kv_t"] = m_tiles(w[:, c[3]:c[4]])
    r["w_kr_t"] = w[:, c[4]:c[5]].reshape(KT, 128, ROPE).transpose(1, 0, 2).reshape(128, KT * ROPE)
    r["w_mq_t"] = m_tiles(w[:, c[5]:c[6]])
    r["w_gate_t"] = m_tiles(w[:, c[6]:c[7]])
    r["w_mk_t"] = m_tiles(x["w_mem_k"][0])
    r["w_mv_t"] = x["w_mem_v"][0].reshape(4, 2, 128, 512).transpose(0, 2, 1, 3).reshape(4, 128, 1024)
    uq = x["w_uq"][0].reshape(QL, NH, QK)
    uq = np.concatenate([uq[:, :, :NOPE].reshape(QL, -1), uq[:, :, NOPE:].reshape(QL, -1)], 1)
    r["w_uq_t"] = m_tiles(uq).reshape(3, 2, 128, QL).transpose(0, 2, 1, 3).reshape(3, 128, 2 * QL)
    r["w_uk_t"] = m_tiles(x["w_uk"][0].reshape(KVL, -1)).transpose(1, 0, 2).reshape(128, 4 * KVL)
    r["w_uv_t"] = x["w_uv"][0].reshape(2, 128, 512).transpose(1, 0, 2).reshape(128, 1024)
    r["w_como_t"] = np.concatenate([m_tiles(x["w_co"][0]), m_tiles(x["w_mo"][0])], 2)
    r["w_xo_t"] = m_tiles(x["w_mem_o"][0])
    r["conv_state_T"] = x["cache_conv"][0, 0].T.reshape(4, 128, PAD).transpose(1, 0, 2)
    r["w_dw_T"] = x["w_dw"][0].T.reshape(4, 128, CW).transpose(1, 0, 2)
    r["conv_vec"] = np.stack([fm(x[n][0]) for n in ("b_dw", "g_cn", "b_cn")], 1)
    r["g_qa_T"] = fm(x["g_qa"][0])
    r["g_kva_T"] = fm(x["g_kva"][0])
    r["b_gate_T"] = fm(x["b_gate"][0])
    half = ROPE // 2
    inv = np.power(np.float32(10000.0), -np.arange(half, dtype=np.float32) / np.float32(half)).astype(np.float32)
    pos = np.concatenate([np.arange(TP), PAST + np.arange(TS)]).astype(np.float32)
    ang = (inv[:, None] * pos[None, :]).astype(np.float32)
    cos, sin = np.cos(ang).astype(np.float32), np.sin(ang).astype(np.float32)
    r["rope_cos"] = np.tile(cos, (8, 1))
    r["rope_sin"] = np.tile(np.concatenate([-sin, sin], 0), (4, 1))
    r["past_krope_T"] = x["cache_mla_krope"][0, 0].T
    r["past_lat_T"] = x["cache_mla_latent"][0, 0].T.reshape(2, 128, PAST)
    r["mem_k_T"] = x["cache_mem_k"][0, 0].transpose(2, 1, 0)
    r["cache_mem_v"] = x["cache_mem_v"][0, 0].reshape(2, 128, MH * MD).transpose(1, 0, 2)
    wr = np.concatenate([x["w_group"][0], x["w_router"][0]], 1)
    r["w_route"] = wr.reshape(KT, 128, NG + NE).transpose(1, 0, 2)
    r["b_route"] = np.concatenate([x["b_group"], x["b_router"]], 1)
    r["w_out"] = x["w_out"][0]
    for n in ("g_ln1", "b_ln1", "g_ln2", "b_ln2"):
        r[n] = x[n]
    r["w_e1"] = x["w_e1"].reshape(NE, D, FE)
    r["w_e3"] = x["w_e3"].reshape(NE, D, FE)
    r["w_e2"] = x["w_e2"].reshape(NE, FE, D)
    return r


OUTS = {"y_prompt": (TP, D), "y_sample": (TS, D), "conv_prompt_T": (128, 4, PAD), "conv_sample_T": (128, 4, PAD),
        "latent_T": (128, 2, T), "krope_T": (ROPE, T), "mem_k_T": (128, MH, MT), "mem_v": (128, 2, MH * MD)}


def kernel(**inputs):
    import concourse.bacc as bacc
    from concourse.bass_utils import run_bass_kernel_spmd

    x = {k: np.asarray(v) for k, v in inputs.items()}
    nc = bacc.Bacc("TRN2", target_bir_lowering=False, num_devices=1)
    arrays, a, o = {}, {}, {}
    for name, v in lay_out(x).items():
        v = np.ascontiguousarray(v)
        arrays[f"in_{name}"] = v
        a[name] = nc.dram_tensor(f"in_{name}", v.shape, mybir.dt.from_np(v.dtype), kind="ExternalInput").ap()
    for name, shape in OUTS.items():
        o[name] = nc.dram_tensor(f"out_{name}", shape, F32, kind="ExternalOutput").ap()
    program(nc, a, o)
    r = run_bass_kernel_spmd(nc, [arrays], core_ids=[0]).results[0]
    g = {n: np.asarray(r[f"out_{n}"]) for n in OUTS}

    def rows(v):
        return np.ascontiguousarray(v.transpose(2, 1, 0).reshape(v.shape[2], -1))

    lat = rows(g["latent_T"])
    kr = np.ascontiguousarray(g["krope_T"].T)
    mk = np.ascontiguousarray(g["mem_k_T"].transpose(2, 1, 0))
    mv = np.ascontiguousarray(g["mem_v"].transpose(1, 0, 2)).reshape(MT, MH, MD)
    return (g["y_prompt"][None], g["y_sample"][None], rows(g["conv_prompt_T"])[None, None], lat[None, None, :TP],
            kr[None, None, :TP], mk[None, None], mv[None, None], rows(g["conv_sample_T"])[None, None],
            lat[None, None, TP:], kr[None, None, TP:])
```

```python
from contextlib import ExitStack

import numpy as np

import concourse.bass as bass
from concourse import mybir

F32 = mybir.dt.float32
BF16 = mybir.dt.bfloat16
I32 = mybir.dt.int32
ALU = mybir.AluOpType
ACT = mybir.ActivationFunctionType
AX = mybir.AxisListType

D = 1024
TP, TS = 512, 64
T = TP + TS
HT = T // 2
PAST = 256
CH = 512
CW = 31
PAD = CW - 1
NH, NOPE, ROPE, VD = 8, 64, 32, 64
QK = NOPE + ROPE
QL, KVL = 384, 256
KEYS = TP + PAST + TS
MH, MD, MT = 4, 128, 256
EPS = 1e-5
ALPHA = 2.0 ** 0.25
NG, NE_G, FE = 4, 8, 256
NE = NG * NE_G
KT = D // 128
CAP = 128
NB = 4
NCH = -(-T // CAP)
TILES = [(i * 128, 128) for i in range(4)] + [(TP, TS)]
NT = len(TILES)
SKIP = 1 << 14
CAUSAL = 64
UW = PAD + TP + PAD + TS

JOBS = []
for _c in range(4):
    JOBS += [f"glu_b{_c}", f"glu_a{_c}"]
JOBS += ["q0", "q1", "q2", "kv0", "kv1", "kr", "mk0", "mk1", "q_ss", "kv_ss", "mk2", "mk3",
         "mv0", "mv1", "mq0", "mq1", "mq2", "mq3", "conv_mean"]
JOBS += [f"un{i}" for i in range(4)] + ["ur0", "ur1", "conv_var"] + [f"uk{i}" for i in range(4)] + [f"uv{i}" for i in range(7)]
for _j in range(8):
    JOBS += [f"g0_{_j}", f"yc_{_j}", f"g1_{_j}", f"ym_{_j}", f"g2_{_j}", f"yx_{_j}"]
JOBS += ["c0", "c1", "t0", "c2", "l0", "t1", "c3", "l1", "t2", "c4", "l2", "t3", "l3", "t4", "l4", "rank", "count", "table"]
JOB = {n: i for i, n in enumerate(JOBS)}

RING = 6
SLOT = 1024
ITEMS = []
for _c in range(4):
    ITEMS += [(f"glu_b{_c}", 1024, f"glu_b{_c}"), (f"glu_a{_c}", 1024, f"glu_a{_c}")]
ITEMS += [(n, 1024, n) for n in ("q0", "q1", "q2", "kv0", "kv1")] + [("kr", 256, "kr")]
ITEMS += [(f"mk{i}", 1024, f"mk{i}") for i in range(4)] + [(f"mv_{i}", 1024, "mv1") for i in range(4)]
ITEMS += [(f"mq{i}", 1024, f"mq{i}") for i in range(4)]
ITEMS += [("uq0", 768, "un1"), ("uq1", 768, "un3"), ("uq2", 768, "ur1"), ("uk", 1024, "uk3"), ("uv", 1024, "uv6")]
for _j in range(8):
    ITEMS += [(f"g0_{_j}", 1024, f"g0_{_j}"), (f"comx_{_j}", 1024, f"ym_{_j}"), (f"g1_{_j}", 1024, f"g1_{_j}"),
              (f"g2_{_j}", 1024, f"g2_{_j}"), (f"xo_{_j}", 512, f"yx_{_j}")]
ITEM = {n: i for i, (n, _, _) in enumerate(ITEMS)}

MEM_UNITS = [("mem", i, h) for i in range(NT) for h in range(MH)]
MLA_UNITS = [("mla", i, h) for i in range(NT) for h in range(NH)]


def key_tiles(kind, i):
    if kind == "mem":
        return [(0, 0, 128), (1, 128, 128)]
    if i < 4:
        return [(k, 128 * k, 128) for k in range(i + 1)]
    return [(4, TP, 128), (5, TP + 128, 128), (6, TP + PAST, TS)]


def program(nc, a, o):
    ctx = ExitStack()
    with ctx:
        def sb(name, shape, dt=F32):
            return ctx.enter_context(nc.sbuf_tensor(name, shape, dt))

        def sem(name):
            return ctx.enter_context(nc.semaphore(name))

        XT = sb("XT", [128, 4608])
        xT = XT[:, :].rearrange("p (k t) -> p k t", k=KT)
        xg = XT[:, 0:4096].rearrange("p (b d) -> p b d", b=NB)
        Z = sb("Z", [128, 2304])
        zT = Z[:, :].rearrange("p (c t) -> p c t", c=4)
        xgT = Z[:, 0:1024].rearrange("p (k s) -> p k s", k=KT)
        hg = Z[:, 1024:1280]
        hm = Z[:, 1280:1536]
        hT = Z[:, 1536:1792].rearrange("p (j s) -> p j s", j=2)
        OM = sb("OM", [128, 2304])
        omT = OM[:, :].rearrange("p (c t) -> p c t", c=4)
        OX = sb("OX", [128, 2304])
        oxT = OX[:, :].rearrange("p (c t) -> p c t", c=4)
        x1T = OX[:, 0:2048].rearrange("p (b k t) -> p b k t", b=2, k=KT)
        slot_col = OX[:, 0:2 * NT * NCH * NE].rearrange("p (c t n) -> p c t n", c=2, t=NT)
        slot_row = OM[:, 0:2 * NT * 128].rearrange("p (c t n) -> p c t n", c=2, t=NT)
        ysb = OM[:, 0:2048].rearrange("p (b d) -> p b d", b=2)
        QG = sb("QG", [128, 14848])
        QH = QG[:, 0:4608]
        qh = QH[:, :].rearrange("p (h t) -> p h t", h=NH)
        merged = QH[:, :].rearrange("p (k t) -> p k t", k=KT)
        GH = QG[:, 4608:14848]
        kh = GH[:, 0:6656].rearrange("p (h t) -> p h t", h=NH)
        V = GH[:, 6656:10240].rearrange("p (k n) -> p k n", k=7)
        memq = GH[:, 0:2304].rearrange("p (h t) -> p h t", h=MH)
        mkT = GH[:, 2304:4352].rearrange("p (s h m) -> p s h m", s=2, h=MH)
        mv = GH[:, 4352:6400].rearrange("p (s k n) -> p s k n", s=2, k=2)
        w_out = GH[:, 0:8192].rearrange("p (k n) -> p k n", k=KT)
        xtok = GH[:, 8192:10240].rearrange("p (b d) -> p b d", b=2)
        RG = sb("RG", [128, RING * SLOT])
        ring = RG[:, :].rearrange("p (r n) -> p r n", r=RING)
        x1 = RG[:, 0:5120].rearrange("p (t d) -> p t d", t=NT)
        KM = sb("KM", [128, 4592])
        U = KM[:, 0:2544].rearrange("p (c t) -> p c t", c=4)
        memT = KM[:, 2544:4592].rearrange("p (k m) -> p k m", k=KT)
        Pb = KM[:, 0:1536].rearrange("p (b n) -> p b n", b=3)
        PT = KM[:, 1536:3072].rearrange("p (b n) -> p b n", b=3)
        osb = KM[:, 3072:4096].rearrange("p (b n) -> p b n", b=2)
        gate = KM[:, 0:3456].rearrange("p (b n t) -> p b n t", b=2, n=3)
        lnbc = KM[:, 0:4096].rearrange("p (n d) -> p n d", n=4)
        WE = sb("WE", [128, 2, 6144])
        we = [WE[:, 0], WE[:, 1], QG[:, 0:6144], QG[:, 6144:12288]]
        w13 = [w[:, 0:4096].rearrange("p (s k f) -> p s k f", s=2, k=KT) for w in we]
        w2 = [w[:, 4096:6144].rearrange("p (j d) -> p j d", j=2) for w in we]
        WF = WE[:, :, :].rearrange("p b n -> p (b n)")
        sq = WF[:, 0:2304].rearrange("p (c t) -> p c t", c=4)
        qd = WF[:, 2304:4032].rearrange("p (c t) -> p c t", c=3)
        kvd = WF[:, 4032:5184].rearrange("p (c t) -> p c t", c=2)
        cos = WF[:, 5184:5760]
        sin = WF[:, 5760:6336]
        krot = WF[0:32, 6336:7168]
        rp = WF[:, 7168:8896].rearrange("p (n t) -> p n t", n=3)
        norms = QG[:, 0:1152].rearrange("p (n t) -> p n t", n=2)
        cnorm = WF[:, 10560:11712].rearrange("p (n t) -> p n t", n=2)
        ck = WF[:, 8896:10560].rearrange("p (c t) -> p c t", c=2)
        yab = WF[:, 0:10240].rearrange("p (t c d) -> p t c d", t=NT, c=2)

        ident = sb("ident", [128, 128])
        ones = sb("ones", [128, 128])
        rowmask = sb("rowmask", [128, 128])
        negrow = sb("negrow", [128, 64])
        wdw = sb("wdw", [128, 4, CW])
        vec = sb("vec", [128, 3, 4])
        gqa = sb("gqa", [128, 3])
        gkva = sb("gkva", [128, 2])
        bgate = sb("bgate", [128, 24])
        eps = sb("eps", [128, 1])
        nb = sb("nb", [128, 8])
        rs = sb("rs", [128, 2, 8])
        rinv = sb("rinv", [128, 2, 8])
        st = sb("st", [128, 2, 2, 6])
        mva = sb("mva", [128, 2, 2])
        rstd = sb("rstd", [128, 2, 2])
        wr = sb("wr", [128, KT, 36])
        rbias = sb("rbias", [128, 36])
        lg = sb("lg", [128, NT, 36])
        tri = sb("tri", [128, 128], BF16)
        onesb = sb("onesb", [128, 128], BF16)
        desc = sb("desc", [128, NE_G])
        iota_i = sb("iota_i", [128, NCH * NE], I32)
        iota = sb("iota", [128, NCH * NE])
        gm = sb("gm", [128, 12, NT])
        g4 = sb("g4", [128, 3, NT, NG])
        e8 = sb("e8", [128, 4, NT, NE_G])
        e32 = sb("e32", [128, 4, NT, NE])
        maskb = sb("maskb", [128, NT, NE], BF16)
        wsel = sb("wsel", [128, 2, NT])
        slot = sb("slot", [128, 2, 2, NT])
        rowid_i = sb("rowid_i", [128, 2, NT], I32)
        rowid = sb("rowid", [128, 2, NT])
        empty = sb("empty", [128, NCH * NE])
        tabs = sb("tabs", [128, NCH * NE], I32)
        flag = sb("flag", [128, 1], I32)

        PS = ctx.enter_context(nc.psum_tensor("PS", [128, 8, 512], F32))

        x1_d = nc.dram_tensor("x1_rows", (2 * T, D), F32, kind="Internal").ap()
        y_d = nc.dram_tensor("expert_rows", (2 * T, D), F32, kind="Internal").ap()

        ring_full = [sem(f"ring_full{i}") for i in range(RING)]
        job_done = sem("job_done")
        in_x = [sem(f"in_x{i}") for i in range(4)]
        in_small = sem("in_small")
        in_conv = sem("in_conv")
        in_mem = sem("in_mem")
        in_cache = sem("in_cache")
        in_past = sem("in_past")
        in_wout = sem("in_wout")
        in_ln = sem("in_ln")
        in_xtok = [sem("in_xtok0"), sem("in_xtok1")]
        in_route = sem("in_route")
        out_sem = sem("out_sem")
        const_ready = sem("const_ready")
        pool_chain = sem("pool_chain")
        dve_chain = sem("dve_chain")
        act_chain = sem("act_chain")
        glu_sig = sem("glu_sig")
        u_ready = sem("u_ready")
        tap_prompt = sem("tap_prompt")
        tap_sample = sem("tap_sample")
        kr_raw = sem("kr_raw")
        mean_read = sem("mean_read")
        conv_std = sem("conv_std")
        route_const = sem("route_const")
        conv_out = sem("conv_out")
        lat_out = sem("lat_out")
        mem_out = sem("mem_out")
        conv_cent = sem("conv_cent")
        conv_sq = sem("conv_sq")
        conv_norm = sem("conv_norm")
        z_ready = sem("z_ready")
        lat_raw = sem("lat_raw")
        lat_sq = sem("lat_sq")
        lat_std = sem("lat_std")
        qn_ready = sem("qn_ready")
        ck_ready = sem("ck_ready")
        krot_ready = sem("krot_ready")
        mem_proj = sem("mem_proj")
        ur_raw = sem("ur_raw")
        ur_rot = sem("ur_rot")
        qk_ready = sem("qk_ready")
        kr_copied = sem("kr_copied")
        score_done = sem("score_done")
        max_done = sem("max_done")
        exp_done = sem("exp_done")
        pt_done = sem("pt_done")
        pt_evac = sem("pt_evac")
        pv_done = sem("pv_done")
        o_norm = sem("o_norm")
        ot_done = sem("ot_done")
        ot_evac = sem("ot_evac")
        gate_sig = sem("gate_sig")
        gate_mul = sem("gate_mul")
        merged_ready = sem("merged_ready")
        ln1_res = sem("ln1_res")
        ln1_var = sem("ln1_var")
        ln1_std = sem("ln1_std")
        ln1_hat = sem("ln1_hat")
        x1_ready = sem("x1_ready")
        x1_out = sem("x1_out")
        x1T_ready = sem("x1T_ready")
        lg_ready = sem("lg_ready")
        route_dve = sem("route_dve")
        route_exp = sem("route_exp")
        mask_ready = sem("mask_ready")
        slot_ready = sem("slot_ready")
        onehot_ready = sem("onehot_ready")
        tab_ready = sem("tab_ready")
        flag_ready = sem("flag_ready")
        x1_scaled = sem("x1_scaled")
        we13 = [sem(f"we13_{i}") for i in range(NB)]
        we2 = [sem(f"we2_{i}") for i in range(NB)]
        e_rows = [sem(f"e_rows_{i}") for i in range(NB)]
        e_tx = sem("e_tx")
        e_xgT = sem("e_xgT")
        e_xgT2 = sem("e_xgT2")
        e_h = sem("e_h")
        e_silu = sem("e_silu")
        e_hm = sem("e_hm")
        e_ht = sem("e_ht")
        e_hT = sem("e_hT")
        e_y = sem("e_y")
        e_ya = sem("e_ya")
        e_yb = sem("e_yb")
        e_out = [sem("e_out0"), sem("e_out1")]
        ov_w = sem("ov_w")
        ov_rows = sem("ov_rows")
        ov_tx = sem("ov_tx")
        ov_xgT = sem("ov_xgT")
        ov_h = sem("ov_h")
        ov_silu = sem("ov_silu")
        ov_hm = sem("ov_hm")
        ov_ht = sem("ov_ht")
        ov_hT = sem("ov_hT")
        ov_y = sem("ov_y")
        ov_ysb = sem("ov_ysb")
        ov_out = sem("ov_out")
        in_y = [sem(f"in_y{i}") for i in range(NT)]
        ln2_var = sem("ln2_var")
        ln2_std = sem("ln2_std")
        ln2_hat = sem("ln2_hat")
        ln2_out = sem("ln2_out")

        def pair(name):
            p = JOB[name] % 4
            return PS[:, 2 * p:2 * p + 2, :]

        def half(name, s, m=128, n=HT):
            return PS[0:m, 2 * (JOB[name] % 4) + s, 0:n]

        def both(name, m=128, n=HT):
            return PS[0:m, 2 * (JOB[name] % 4):2 * (JOB[name] % 4) + 2, 0:n]

        def wait_job(eng, name):
            eng.wait_ge(job_done, JOB[name] + 1)

        def read_of(name):
            kind = name.rstrip("0123456789")
            i = int(name[len(kind):] or 0)
            if kind.endswith("_") and kind[0] in "gy":
                gates = {"g0_": 0, "g1_": 1, "g2_": 2}
                return (gate_sig, 3 * i + gates[kind] + 1) if kind in gates else (gate_mul, 3 * i + {"yc_": 0, "ym_": 1, "yx_": 2}[kind] + 1)
            return {
                "glu_b": (glu_sig, i + 1), "glu_a": (u_ready, i + 1), "q": (lat_raw, i + 1), "kv": (lat_raw, i + 4),
                "kr": (kr_raw, 1), "q_ss": (lat_std, 1), "kv_ss": (lat_std, 2), "mk": (mem_proj, i + 1),
                "mv": (mem_proj, i + 5), "mq": (mem_proj, i + 7), "conv_mean": (mean_read, 1), "conv_var": (conv_std, 1),
                "un": (qk_ready, 2 * i + 2), "ur": (ur_raw, i + 1), "uk": (qk_ready, 2 * i + 10), "uv": (qk_ready, i + 17),
                "c": (ln1_res, i + 1), "t": (x1T_ready, i + 1), "l": (lg_ready, i + 1), "rank": (slot_ready, 2), "table": (tab_ready, 1),
                "count": (flag_ready, 1),
            }[kind]

        def split(ap):
            return ap.rearrange("p (s t) -> p s t", s=2)

        def w_item(name):
            return ring[:, ITEM[name] % RING, :]

        MEM_LAST, MLA_LAST = len(MEM_UNITS), len(MEM_UNITS) + len(MLA_UNITS)
        UNITS = MEM_UNITS + MLA_UNITS
        GROUPS = []
        for u in UNITS:
            if u[:2] not in GROUPS:
                GROUPS.append(u[:2])
        group_of = [GROUPS.index(u[:2]) for u in UNITS]
        last_of_group = {g: max(n for n, x in enumerate(group_of) if x == g) for g in range(len(GROUPS))}
        N_G = len(GROUPS)
        N_MEM_G = NT

        block = ctx.enter_context(nc.Block())

        @block.sync
        def _(sp):
            def src(name):
                for key in ("glu_b", "glu_a"):
                    if name.startswith(key):
                        return a["w_glu_t"][int(name[5:]) + 4 * (key == "glu_a")]
                if name[0] == "q":
                    return a["w_q_t"][int(name[1:])]
                if name == "kr":
                    return a["w_kr_t"]
                if name[:2] == "kv":
                    return a["w_kv_t"][int(name[2:])]
                if name[:2] == "mk":
                    return a["w_mk_t"][int(name[2:])]
                if name[:2] == "mv":
                    return a["w_mv_t"][int(name[3:])]
                if name[:2] == "mq":
                    return a["w_mq_t"][int(name[2:])]
                if name[:2] == "uq":
                    return a["w_uq_t"][int(name[2:])]
                if name == "uk":
                    return a["w_uk_t"]
                if name == "uv":
                    return a["w_uv_t"]
                j = int(name.split("_")[1])
                if name[0] == "g":
                    return a["w_gate_t"][8 * int(name[1]) + j]
                if name[:4] == "comx":
                    return a["w_como_t"][j]
                return a["w_xo_t"][j]

            def load_expert_up(e, b):
                return sp.dma_start(we[b][:, 0:4096], a["w_e13"][bass.ds(e, 1)].rearrange("a p n -> p (a n)")).then_inc(we13[b], 16)

            def load_expert_down(e, b):
                return sp.dma_start(we[b][:, 4096:6144], a["w_e2"][bass.ds(e, 1)].rearrange("a p n -> p (a n)")).then_inc(we2[b], 16)

            sp.dma_start(ring[:, 0, :], src("glu_b0")).then_inc(ring_full[0], 16)
            for q in range(4):
                sp.dma_start(xT[:, 2 * q:2 * q + 2, :], a["xT"][:, 2 * q:2 * q + 2, :]).then_inc(in_x[q], 16)
            for i, (name, n, _) in enumerate(ITEMS):
                if i == 0:
                    continue
                if i >= RING:
                    wait_job(sp, ITEMS[i - RING][2])
                sp.dma_start(ring[:, i % RING, 0:n], src(name)).then_inc(ring_full[i % RING], 16)
                if name == "glu_a0":
                    sp.dma_start(memT, a["memT"]).then_inc(in_mem, 16)
                if name == "g0_0":
                    wait_job(sp, "uv6")
                    sp.wait_ge(qk_ready, 8 + 8 + 7)
                    sp.wait_ge(kr_copied, 1)
                    sp.wait_ge(ur_rot, 2)
                    sp.wait_ge(lat_out, 64)
                    sp.wait_ge(z_ready, 4)
                    for e in range(2):
                        load_expert_up(e, e)
                        load_expert_down(e, e)
                if name == "g0_1":
                    sp.wait_ge(pv_done, MLA_LAST)
                    sp.dma_start(w_out, a["w_out"].rearrange("(k p) n -> p k n", p=128)).then_inc(in_wout, 16)
                    for b in range(2):
                        sp.dma_start(xtok[:, b, :], a["x_tok"][128 * b:128 * b + 128]).then_inc(in_xtok[b], 16)
            sp.wait_ge(merged_ready, 8)
            for n, name in enumerate(("g_ln1", "b_ln1", "g_ln2", "b_ln2")):
                sp.dma_start(lnbc[:, n, :], a[name].broadcast_to([128, D])).then_inc(in_ln, 16)
            for tt in range(2, NT):
                t0, nr = TILES[tt]
                sp.wait_ge(ln1_res, tt - 1)
                sp.dma_start(xtok[0:nr, tt % 2, :], a["x_tok"][t0:t0 + nr]).then_inc(in_xtok[tt % 2], 16)
            for tt in range(NT):
                t0, nr = TILES[tt]
                sp.wait_ge(x1_ready, tt + 1)
                for c in range(2):
                    sp.dma_start(x1_d[c * T + t0:c * T + t0 + nr], x1[0:nr, tt, :]).then_inc(x1_out, 16)

            wait_job(sp, "c4")
            for e in range(2, NB):
                load_expert_up(e, e)
                load_expert_down(e, e)
            with sp.Fori(1, NE // NB) as r:
                for b in range(NB):
                    e = r * NB + b
                    sp.wait_ge(e_h, e - NB + 1)
                    load_expert_up(e, b)
                    sp.wait_ge(e_y, e - NB + 1)
                    load_expert_down(e, b)

            sp.wait_ge(e_y, NE)
            sp.wait_ge(flag_ready, 1)
            over = sp.value_load(flag[0:1, 0:1], min_val=0, max_val=T)
            with sp.If(over > CAP):
                def load_again(e):
                    sp.dma_start(we[0][:, 0:4096], a["w_e13"][bass.ds(e, 1)].rearrange("a p n -> p (a n)")).then_inc(ov_w, 16)
                    sp.dma_start(we[0][:, 4096:6144], a["w_e2"][bass.ds(e, 1)].rearrange("a p n -> p (a n)")).then_inc(ov_w, 16)

                load_again(0)
                with sp.Fori(1, NE) as e:
                    sp.wait_ge(ov_y, e * (NCH - 1))
                    load_again(e)
                sp.wait_ge(ov_out, 16 * NE * (NCH - 1))
            for b in range(2):
                sp.wait_ge(e_out[b], 16 * NE // 2)
            for tt in range(NT):
                t0, nr = TILES[tt]
                for c in range(2):
                    sp.dma_start(yab[0:nr, tt, c, :], y_d[c * T + t0:c * T + t0 + nr]).then_inc(in_y[tt], 16)
            for tt in range(NT):
                t0, nr = TILES[tt]
                sp.wait_ge(ln2_out, tt + 1)
                dst = o["y_prompt"][t0:t0 + nr] if tt < 4 else o["y_sample"]
                sp.dma_start(dst, x1[0:nr, tt, :]).then_inc(out_sem, 16)
            sp.wait_ge(conv_out, 32)
            sp.wait_ge(lat_out, 64)
            sp.wait_ge(mem_out, 32)
            sp.wait_ge(out_sem, 16 * NT)

        @block.tensor
        def _(pe):
            def begin(name):
                n = JOB[name]
                if n >= 4:
                    pe.wait_ge(*read_of(JOBS[n - 4]))

            def item(name):
                i = ITEM[name]
                pe.wait_ge(ring_full[i % RING], 16 * (i // RING + 1))
                return w_item(name)

            def gemm(name, w, rhs, nk, m=128, n=HT, halves=2):
                begin(name)
                for k in range(nk):
                    for s in range(halves):
                        mm = pe.matmul(half(name, s, m, n), w[:, k, :], rhs(k, s), start=(k == 0), stop=(k == nk - 1))
                mm.then_inc(job_done, 1)

            def x_half(k, s):
                if k % 2 == 0 and s == 0:
                    pe.wait_ge(in_x[k // 2], 16)
                return xT[:, k, HT * s:HT * s + HT]

            def on(buf):
                return lambda k, s: buf[:, k, HT * s:HT * s + HT]

            def proj(name, m=128):
                w = item(name)[:, 0:KT * m].rearrange("p (k m) -> p k m", k=KT)
                gemm(name, w, x_half, KT, m)

            def total(name, nk, buf):
                begin(name)
                for k in range(nk):
                    for s in range(2):
                        mm = pe.matmul(half(name, s), ones[:, :], buf[:, k, HT * s:HT * s + HT],
                                       start=(k == 0), stop=(k == nk - 1))
                mm.then_inc(job_done, 1)

            for c in range(4):
                proj(f"glu_b{c}")
                proj(f"glu_a{c}")
            for name in ("q0", "q1", "q2", "kv0", "kv1"):
                proj(name)
            proj("kr", 32)
            pe.wait_ge(const_ready, 6)
            pe.wait_ge(in_mem, 16)

            def mem_key(h):
                w = item(f"mk{h}").rearrange("p (k m) -> p k m", k=KT)
                gemm(f"mk{h}", w, lambda k, s: memT[:, k, :], KT, n=MT, halves=1)

            mem_key(0)
            mem_key(1)
            pe.wait_ge(lat_sq, 3)
            total("q_ss", 3, sq)
            pe.wait_ge(lat_sq, 5)
            total("kv_ss", 2, rp)
            mem_key(2)
            mem_key(3)
            begin("mv0")
            begin("mv1")
            for i in range(4):
                w = item(f"mv_{i}").rearrange("p (k n) -> p k n", k=2)
                for kk in range(2):
                    k = 2 * i + kk
                    for m in range(2):
                        mm = pe.matmul(half(f"mv{m}", 0, 128, 512), memT[:, k, 128 * m:128 * m + 128], w[:, kk, :],
                                       start=(k == 0), stop=(k == KT - 1))
                        if k == KT - 1:
                            mm.then_inc(job_done, 1)
            for h in range(MH):
                proj(f"mq{h}")
            pe.wait_ge(tap_prompt, 4 * CW)
            pe.wait_ge(tap_sample, 4 * CW)
            total("conv_mean", 4, zT)

            def scores(n):
                kind, i, h = UNITS[n]
                t0, nr = TILES[i]
                if n >= 2:
                    pe.wait_ge(exp_done, n - 1)
                out = PS[0:nr, n % 2, :]
                if kind == "mem":
                    mm = pe.matmul(out[:, 0:MT], memq[:, h, t0:t0 + nr], mkT[:, i // 4, h, :], start=True, stop=True)
                elif i < 4:
                    nk = 128 * (i + 1)
                    pe.matmul(out[:, 0:nk], qh[0:QK, h, t0:t0 + nr], kh[0:QK, h, 0:nk], start=True, stop=True)
                    mm = pe.matmul(out[:, nk - CAUSAL:nk], rowmask[0:QK, :], negrow[0:QK, :], start=False, stop=True,
                                   skip_group_check=True)
                else:
                    mm = pe.matmul(out[:, 0:PAST + TS], qh[0:QK, h, t0:t0 + nr], kh[0:QK, h, TP:KEYS], start=True, stop=True)
                mm.then_inc(score_done, 1)

            def turn(n):
                kind, i, h = UNITS[n]
                nr = TILES[i][1]
                pe.wait_ge(exp_done, n + 1)
                if n >= 2:
                    pe.wait_ge(pt_evac, n - 1)
                kts = key_tiles(kind, i)
                for j, (_, c0, nk) in enumerate(kts):
                    mm = pe.transpose(PS[0:nk, 2 + n % 2, 128 * j:128 * j + nr], Pb[0:nr, n % 3, 128 * j:128 * j + nk],
                                      ident[0:nr, 0:nr])
                mm.then_inc(pt_done, 1)

            def values(n):
                kind, i, h = UNITS[n]
                nr = TILES[i][1]
                g = group_of[n]
                pe.wait_ge(pt_evac, n + 1)
                if h == 0 and g >= 2:
                    pe.wait_ge(o_norm, g - 1)
                kts = key_tiles(kind, i)
                w = MD if kind == "mem" else VD
                for j, (kt, _, nk) in enumerate(kts):
                    v = mv[0:nk, i // 4, kt, h * MD:(h + 1) * MD] if kind == "mem" else V[0:nk, kt, h * VD:(h + 1) * VD]
                    mm = pe.matmul(PS[0:nr, 4 + g % 2, h * w:(h + 1) * w], PT[0:nk, n % 3, 128 * j:128 * j + nr], v,
                                   start=(j == 0), stop=(j == len(kts) - 1))
                mm.then_inc(pv_done, 1)

            def turn_out(g):
                nr = TILES[GROUPS[g][1]][1]
                pe.wait_ge(o_norm, g + 1)
                if g >= 2:
                    pe.wait_ge(ot_evac, g - 1)
                for c in range(4):
                    mm = pe.transpose(PS[:, 6 + g % 2, 128 * c:128 * c + nr], osb[0:nr, g % 2, 128 * c:128 * c + 128],
                                      ident[0:nr, 0:nr])
                mm.then_inc(ot_done, 1)

            def attend(first, end):
                for n in range(first, end + 4):
                    if n < end:
                        scores(n)
                    if first <= n - 1 < end:
                        turn(n - 1)
                    if first <= n - 2 < end:
                        values(n - 2)
                    if first <= n - 3 < end and last_of_group[group_of[n - 3]] == n - 3:
                        turn_out(group_of[n - 3])

            def all_read():
                for name in JOBS[now - 4:now]:
                    pe.wait_ge(*read_of(name))

            now = JOB["conv_mean"] + 1
            all_read()
            pe.wait_ge(mem_proj, 10)
            pe.wait_ge(in_cache, 32)
            attend(0, MEM_LAST)
            pe.wait_ge(ot_evac, N_MEM_G)

            pe.wait_ge(qn_ready, 3)
            for i in range(3):
                w = item(f"uq{i}")[:, 0:768].rearrange("p (m k n) -> p m k n", m=2, k=3)
                for m in range(2):
                    gemm(f"un{2 * i + m}" if i < 2 else f"ur{m}", w[:, m], on(qd), 3)
            pe.wait_ge(conv_sq, 4)
            total("conv_var", 4, sq)
            pe.wait_ge(ck_ready, 2)
            pe.wait_ge(in_past, 48)
            w = item("uk").rearrange("p (m k n) -> p m k n", m=4, k=2)
            for m in range(4):
                gemm(f"uk{m}", w[:, m], lambda k, s: ck[:, k, 416 * s:416 * s + 416], 2, n=416)
            w = item("uv").rearrange("p (k n) -> p k n", k=2)
            for kt in range(7):
                begin(f"uv{kt}")
                nk = 128 if kt < 6 else TS
                for k in range(2):
                    mm = pe.matmul(half(f"uv{kt}", 0, nk, 512), ck[:, k, 128 * kt:128 * kt + nk], w[:, k, :],
                                   start=(k == 0), stop=(k == 1))
                mm.then_inc(job_done, 1)
            now = JOB["uv6"] + 1
            all_read()
            pe.wait_ge(qk_ready, 8 + 8 + 7)
            pe.wait_ge(ur_rot, 2)
            pe.wait_ge(kr_copied, 1)
            attend(MEM_LAST, MLA_LAST)
            pe.wait_ge(ot_evac, N_G)
            pe.wait_ge(z_ready, 4)

            for j in range(8):
                proj(f"g0_{j}")
                w = item(f"comx_{j}").rearrange("p (b k m) -> p b k m", b=2, k=4)
                gemm(f"yc_{j}", w[:, 0], on(zT), 4)
                proj(f"g1_{j}")
                gemm(f"ym_{j}", w[:, 1], on(omT), 4)
                proj(f"g2_{j}")
                wx = item(f"xo_{j}")[:, 0:512].rearrange("p (k m) -> p k m", k=4)
                gemm(f"yx_{j}", wx, on(oxT), 4)

            def out_proj(tt):
                t0, nr = TILES[tt]
                begin(f"c{tt}")
                for k in range(KT):
                    for s in range(2):
                        mm = pe.matmul(half(f"c{tt}", s, nr, 512), merged[:, k, t0:t0 + nr], w_out[:, k, 512 * s:512 * s + 512],
                                       start=(k == 0), stop=(k == KT - 1))
                mm.then_inc(job_done, 1)

            def turn_x1(tt):
                nr = TILES[tt][1]
                begin(f"t{tt}")
                pe.wait_ge(x1_ready, tt + 1)
                for k in range(KT):
                    mm = pe.transpose(PS[:, 2 * (JOB[f"t{tt}"] % 4) + k // 4, 128 * (k % 4):128 * (k % 4) + nr],
                                      x1[0:nr, tt, 128 * k:128 * k + 128], ident[0:nr, 0:nr])
                mm.then_inc(job_done, 1)

            def router(tt):
                nr = TILES[tt][1]
                begin(f"l{tt}")
                pe.wait_ge(x1T_ready, tt + 1)
                for k in range(KT):
                    mm = pe.matmul(half(f"l{tt}", 0, nr, 36), x1T[:, tt % 2, k, 0:nr], wr[:, k, :],
                                   start=(k == 0), stop=(k == KT - 1))
                mm.then_inc(job_done, 1)

            pe.wait_ge(merged_ready, 8)
            pe.wait_ge(in_wout, 16)
            pe.wait_ge(in_route, 32)
            for name in JOBS[JOB["c0"]:JOB["l4"] + 1]:
                {"c": out_proj, "t": turn_x1, "l": router}[name[0]](int(name[1:]))

            pe.wait_ge(mask_ready, 1)
            pe.wait_ge(route_const, 1)
            begin("rank")
            for tt in range(NT):
                for t2 in range(tt + 1):
                    nr = TILES[t2][1]
                    lhs = tri if t2 == tt else onesb
                    mm = pe.matmul(half("rank", 0, 128, 512)[:, 32 * tt:32 * tt + 32], lhs[0:nr, :], maskb[0:nr, t2, :],
                                   start=(t2 == 0), stop=(t2 == tt))
            mm.then_inc(job_done, 1)
            begin("count")
            for tt in range(NT):
                nr = TILES[tt][1]
                mm = pe.matmul(half("count", 0, 128, 32), onesb[0:nr, :], maskb[0:nr, tt, :], start=(tt == 0), stop=(tt == NT - 1))
            mm.then_inc(job_done, 1)
            begin("table")
            for n in range(2 * NT):
                c, tt = divmod(n, NT)
                nr = TILES[tt][1]
                pe.wait_ge(onehot_ready, n + 1)
                mm = pe.matmul(half("table", 0, 128, NCH * NE), slot_row[0:nr, c, tt, :], slot_col[0:nr, c, tt, :],
                               start=(n == 0), stop=(n == 2 * NT - 1))
            mm.then_inc(job_done, 1)
            now = JOB["table"] + 1
            all_read()

            def expert_turn_rows(b):
                for k in range(KT):
                    mm = pe.transpose(PS[:, k // 4, 128 * (k % 4):128 * (k % 4) + CAP],
                                      xg[0:CAP, b, 128 * k:128 * k + 128], ident[0:CAP, 0:CAP])
                return mm

            def expert_hidden(b):
                for k in range(KT):
                    mm = pe.matmul(PS[0:CAP, 2, :].rearrange("p (s f) -> p s f", s=2), xgT[:, k, 0:CAP], w13[b][:, :, k, :],
                                   start=(k == 0), stop=(k == KT - 1))
                return mm

            def expert_turn_hidden():
                for j in range(2):
                    mm = pe.transpose(PS[:, 3, 128 * j:128 * j + CAP], hm[0:CAP, 128 * j:128 * j + 128],
                                      ident[0:CAP, 0:CAP])
                return mm

            def expert_result(b):
                for j in range(2):
                    for s in range(2):
                        mm = pe.matmul(PS[0:CAP, 4 + s, :], hT[:, j, 0:CAP], w2[b][:, j, 512 * s:512 * s + 512],
                                       start=(j == 0), stop=(j == 1))
                return mm

            def rows_step(e, b, k, first=False):
                pe.wait_ge(e_rows[b], 16 * k)
                if not first:
                    pe.wait_ge(e_xgT, e)
                    pe.wait_ge(e_xgT2, e)
                expert_turn_rows(b).then_inc(e_tx, 1)

            def hidden_step(e, b, k, first=False):
                pe.wait_ge(e_xgT, e + 1)
                pe.wait_ge(e_xgT2, e + 1)
                pe.wait_ge(we13[b], 16 * k)
                if not first:
                    pe.wait_ge(e_hm, e)
                expert_hidden(b).then_inc(e_h, 1)

            def hidden_turn_step(e, first=False):
                pe.wait_ge(e_hm, e + 1)
                if not first:
                    pe.wait_ge(e_hT, e)
                expert_turn_hidden().then_inc(e_ht, 1)

            def result_step(e, b, k):
                pe.wait_ge(e_hT, e + 1)
                pe.wait_ge(we2[b], 16 * k)
                pe.wait_ge(e_ya, e)
                pe.wait_ge(e_yb, e)
                expert_result(b).then_inc(e_y, 1)

            rows_step(0, 0, 1, first=True)
            hidden_step(0, 0, 1, first=True)
            rows_step(1, 1, 1)
            hidden_turn_step(0, first=True)

            def experts(r):
                for i in range(1, NB + 1):
                    e = r * NB + i
                    hidden_step(e, i % NB, r + 1 + i // NB)
                    rows_step(e + 1, (i + 1) % NB, r + 1 + (i + 1) // NB)
                    result_step(e - 1, i - 1, r + 1)
                    hidden_turn_step(e)

            experts(0)
            with pe.Fori(1, NE // NB - 1) as r:
                experts(r)
            for e in range(NE - NB + 1, NE):
                hidden_step(e, e % NB, NE // NB)
                if e + 1 < NE:
                    rows_step(e + 1, (e + 1) % NB, NE // NB)
                result_step(e - 1, (e - 1) % NB, NE // NB)
                hidden_turn_step(e)
            result_step(NE - 1, NB - 1, NE // NB)

            pe.wait_ge(flag_ready, 1)
            over = pe.value_load(flag[0:1, 0:1], min_val=0, max_val=T)
            with pe.If(over > CAP):
                pe.wait_ge(e_ya, NE)
                pe.wait_ge(e_yb, NE)
                with pe.Fori(0, NE) as e:
                    with pe.Fori(0, NCH - 1) as c:
                        n = e * (NCH - 1) + c
                        pe.wait_ge(ov_w, e * 32 + 32)
                        pe.wait_ge(ov_rows, n * 16 + 16)
                        expert_turn_rows(0).then_inc(ov_tx, 1)
                        pe.wait_ge(ov_xgT, n + 1)
                        expert_hidden(0).then_inc(ov_h, 1)
                        pe.wait_ge(ov_hm, n + 1)
                        expert_turn_hidden().then_inc(ov_ht, 1)
                        pe.wait_ge(ov_hT, n + 1)
                        expert_result(0).then_inc(ov_y, 1)

        @block.scalar
        def _(act):
            chain = [0]

            def link(ins):
                chain[0] += 1
                ins.then_inc(act_chain, 1)
                act.wait_ge(act_chain, chain[0])

            act.dma_start(U[:, :, PAD + TP:2 * PAD + TP], a["conv_state_T"]).then_inc(in_conv, 16)
            act.dma_start(wdw[:, :, :], a["w_dw_T"]).then_inc(in_conv, 16)
            for dst, name in ((vec, "conv_vec"), (gqa, "g_qa_T"), (gkva, "g_kva_T"), (bgate, "b_gate_T")):
                act.dma_start(dst[:], a[name]).then_inc(in_small, 16)
            act.dma_start(cos, a["rope_cos"]).then_inc(in_small, 16)
            act.dma_start(sin, a["rope_sin"]).then_inc(in_small, 16)
            act.dma_start(krot[:, TP:TP + PAST], a["past_krope_T"]).then_inc(in_past, 16)
            for c in range(2):
                act.dma_start(ck[:, c, TP:TP + PAST], a["past_lat_T"][c]).then_inc(in_past, 16)
            act.dma_start(mkT[:, 1], a["mem_k_T"]).then_inc(in_cache, 16)
            act.dma_start(mv[:, 1], a["cache_mem_v"]).then_inc(in_cache, 16)
            act.dma_start(wr[:, :, :], a["w_route"]).then_inc(in_route, 16)
            act.dma_start(rbias[:, :], a["b_route"].broadcast_to([128, 36])).then_inc(in_route, 16)

            for c in range(4):
                wait_job(act, f"glu_b{c}")
                act.activation(split(sq[:, c, :]), both(f"glu_b{c}"), ACT.Sigmoid).then_inc(glu_sig, 1)
            act.wait_ge(u_ready, 4)
            for i in range(3):
                wait_job(act, f"q{i}")
                act.activation(split(qd[:, i, :]), both(f"q{i}"), ACT.Copy).then_inc(lat_raw, 1)
                act.wait_ge(lat_raw, i + 1)
                act.activation(sq[:, i, :], qd[:, i, :], ACT.Square).then_inc(lat_sq, 1)
            for i in range(2):
                wait_job(act, f"kv{i}")
                act.activation(split(kvd[:, i, :]), both(f"kv{i}"), ACT.Copy).then_inc(lat_raw, 1)
                act.wait_ge(lat_raw, i + 4)
                act.activation(rp[:, i, :], kvd[:, i, :], ACT.Square).then_inc(lat_sq, 1)
            act.wait_ge(const_ready, 6)
            wait_job(act, "kr")
            act.activation(split(rp[0:32, 2, :]), both("kr", 32), ACT.Copy).then_inc(kr_raw, 1)
            wait_job(act, "q_ss")
            act.activation(split(norms[:, 0, :]), both("q_ss"), ACT.Sqrt, bias=eps[:, :], scale=1.0 / QL).then_inc(lat_std, 1)
            wait_job(act, "kv_ss")
            act.activation(split(norms[:, 1, :]), both("kv_ss"), ACT.Sqrt, bias=eps[:, :], scale=1.0 / KVL).then_inc(lat_std, 1)
            for h in range(MH):
                wait_job(act, f"mk{h}")
                act.activation(mkT[:, 0, h, :], half(f"mk{h}", 0, 128, MT), ACT.Copy).then_inc(mem_proj, 1)
            for m in range(2):
                wait_job(act, f"mv{m}")
                act.activation(mv[:, 0, m, :], half(f"mv{m}", 0, 128, 512), ACT.Copy).then_inc(mem_proj, 1)
            for h in range(MH):
                wait_job(act, f"mq{h}")
                act.activation(split(memq[:, h, :]), both(f"mq{h}"), ACT.Copy, scale=MD ** -0.5).then_inc(mem_proj, 1)

            def attend(first, end):
                for n in range(first, end + 5):
                    if n < end:
                        kind, i, h = UNITS[n]
                        nr = TILES[i][1]
                        nk = sum(k[2] for k in key_tiles(kind, i))
                        g = group_of[n]
                        act.wait_ge(max_done, n + 1)
                        if n >= 3:
                            act.wait_ge(pt_done, n - 2)
                        if h == 0 and g >= 2:
                            act.wait_ge(o_norm, g - 1)
                        act.activation(Pb[0:nr, n % 3, 0:nk], PS[0:nr, n % 2, 0:nk], ACT.Exp, bias=nb[0:nr, n % 8:n % 8 + 1],
                                       accum_out=rs[0:nr, g % 2, h:h + 1]).then_inc(exp_done, 1)
                    if first <= n - 4 < end and last_of_group[group_of[n - 4]] == n - 4:
                        g = group_of[n - 4]
                        kind, i = GROUPS[g]
                        t0, nr = TILES[i]
                        dst = (oxT if kind == "mem" else omT)[:, :, t0:t0 + nr]
                        act.wait_ge(ot_done, g + 1)
                        act.activation(dst, PS[:, 6 + g % 2, :].rearrange("p (c t) -> p c t", c=4)[:, :, 0:nr],
                                       ACT.Copy).then_inc(ot_evac, 1)

            act.wait_ge(conv_out, 32)
            attend(0, MEM_LAST)
            act.wait_ge(conv_cent, 4)
            for c in range(4):
                act.activation(sq[:, c, :], zT[:, c, :], ACT.Square).then_inc(conv_sq, 1)
            act.wait_ge(pv_done, MEM_LAST)
            act.wait_ge(mem_out, 32)
            act.wait_ge(qn_ready, 3)
            act.wait_ge(ck_ready, 2)
            act.wait_ge(krot_ready, 1)
            act.wait_ge(in_past, 48)
            for i in range(4):
                wait_job(act, f"un{i}")
                for s in range(2):
                    act.activation(split(qh[0:64, 2 * i + s, :]), PS[64 * s:64 * s + 64, 2 * (JOB[f"un{i}"] % 4):2 * (JOB[f"un{i}"] % 4) + 2, 0:HT],
                                   ACT.Copy, scale=QK ** -0.5).then_inc(qk_ready, 1)
            for i in range(2):
                wait_job(act, f"ur{i}")
                if i:
                    act.wait_ge(ur_rot, 1)
                act.activation(split(rp[:, 0, :]), both(f"ur{i}"), ACT.Copy, scale=QK ** -0.5).then_inc(ur_raw, 1)
            wait_job(act, "conv_var")
            act.activation(split(cnorm[:, 1, :]), both("conv_var"), ACT.Sqrt, bias=eps[:, :], scale=1.0 / CH).then_inc(conv_std, 1)
            for i in range(4):
                wait_job(act, f"uk{i}")
                for s in range(2):
                    act.activation(kh[0:64, 2 * i + s, :].rearrange("p (s t) -> p s t", s=2),
                                   PS[64 * s:64 * s + 64, 2 * (JOB[f"uk{i}"] % 4):2 * (JOB[f"uk{i}"] % 4) + 2, 0:416],
                                   ACT.Copy).then_inc(qk_ready, 1)
            for i in range(7):
                nk = 128 if i < 6 else TS
                wait_job(act, f"uv{i}")
                act.activation(V[0:nk, i, :], half(f"uv{i}", 0, nk, 512), ACT.Copy).then_inc(qk_ready, 1)
            act.wait_ge(in_small, 96)
            for c in range(4):
                act.wait_ge(conv_norm, c + 1)
                act.activation(zT[:, c, :], zT[:, c, :], ACT.Silu, scale=vec[:, 1, c:c + 1],
                               bias=vec[:, 2, c:c + 1]).then_inc(z_ready, 1)
            attend(MEM_LAST, MLA_LAST)
            for j in range(8):
                for n in range(3):
                    wait_job(act, f"g{n}_{j}")
                    if j >= 2:
                        act.wait_ge(merged_ready, j - 1)
                    act.activation(split(gate[:, j % 2, n, :]), both(f"g{n}_{j}"), ACT.Sigmoid,
                                   bias=bgate[:, 8 * n + j:8 * n + j + 1]).then_inc(gate_sig, 1)
            for tt in range(NT + 1):
                if tt < NT:
                    nr = TILES[tt][1]
                    act.wait_ge(ln1_var, tt + 1)
                    act.activation(rstd[0:nr, tt % 2, 0:1], mva[0:nr, tt % 2, 1:2], ACT.Sqrt, bias=eps[0:nr, :]).then_inc(ln1_std, 1)
                if tt >= 1:
                    u = tt - 1
                    nr = TILES[u][1]
                    wait_job(act, f"t{u}")
                    if u >= 2:
                        wait_job(act, f"l{u - 2}")
                    act.activation(x1T[:, u % 2, :, 0:nr].rearrange("p (s k) t -> p s k t", s=2),
                                   pair(f"t{u}").rearrange("p s (k t) -> p s k t", k=4)[:, :, :, 0:nr], ACT.Copy).then_inc(x1T_ready, 1)
            act.wait_ge(route_dve, 1)
            act.activation(g4[:, 1], g4[:, 0], ACT.Exp).then_inc(route_exp, 1)
            act.wait_ge(route_dve, 2)
            act.activation(gm[:, 5], gm[:, 4], ACT.Exp).then_inc(route_exp, 1)

            def evac_rows(half_no):
                src = PS[:, half_no, :].rearrange("p (k t) -> p k t", k=4)[:, :, 0:CAP]
                return act.activation(xgT[:, 4 * half_no:4 * half_no + 4, 0:CAP], src, ACT.Copy)

            def silu():
                return act.activation(hg[0:CAP, :], PS[0:CAP, 2, 0:FE], ACT.Silu)

            def evac_hidden():
                return act.activation(hT[:, :, 0:CAP], PS[:, 3, 0:256].rearrange("p (j t) -> p j t", j=2)[:, :, 0:CAP], ACT.Copy)

            def evac_result(b, s):
                return act.activation(ysb[0:CAP, b, 512 * s:512 * s + 512], PS[0:CAP, 4 + s, :], ACT.Copy)

            def rows_step(e):
                act.wait_ge(e_tx, e + 1)
                act.wait_ge(e_h, e)
                evac_rows(0).then_inc(e_xgT, 1)

            def silu_step(e):
                act.wait_ge(e_h, e + 1)
                act.wait_ge(e_hm, e)
                silu().then_inc(e_silu, 1)

            def hidden_turn_step(e):
                act.wait_ge(e_ht, e + 1)
                act.wait_ge(e_y, e)
                evac_hidden().then_inc(e_hT, 1)

            def result_step(e, b, k):
                act.wait_ge(e_y, e + 1)
                act.wait_ge(e_out[b], 16 * k)
                evac_result(b, 0).then_inc(e_ya, 1)

            rows_step(0)
            silu_step(0)
            rows_step(1)
            hidden_turn_step(0)
            def expert_pair(h):
                e = h * 2 + 1
                silu_step(e)
                rows_step(e + 1)
                result_step(e - 1, 0, h)
                hidden_turn_step(e)
                silu_step(e + 1)
                rows_step(e + 2)
                result_step(e, 1, h)
                hidden_turn_step(e + 1)

            expert_pair(0)
            with act.Fori(1, NE // 2 - 1) as h:
                expert_pair(h)
            silu_step(NE - 1)
            result_step(NE - 2, 0, NE // 2 - 1)
            hidden_turn_step(NE - 1)
            result_step(NE - 1, 1, NE // 2 - 1)
            act.wait_ge(flag_ready, 1)
            over = act.value_load(flag[0:1, 0:1], min_val=0, max_val=T)
            with act.If(over > CAP):
                with act.Fori(0, NE * (NCH - 1)) as n:
                    act.wait_ge(ov_tx, n + 1)
                    link_free = evac_rows(0)
                    evac_rows(1).then_inc(ov_xgT, 1)
                    act.wait_ge(ov_h, n + 1)
                    silu().then_inc(ov_silu, 1)
                    act.wait_ge(ov_ht, n + 1)
                    evac_hidden().then_inc(ov_hT, 1)
                    act.wait_ge(ov_y, n + 1)
                    evac_result(0, 0)
                    evac_result(0, 1).then_inc(ov_ysb, 1)
            for tt in range(NT):
                nr = TILES[tt][1]
                act.wait_ge(ln2_var, tt + 1)
                act.activation(rstd[0:nr, tt % 2, 0:1], mva[0:nr, tt % 2, 1:2], ACT.Sqrt, bias=eps[0:nr, :]).then_inc(ln2_std, 1)

        @block.vector
        def _(dve):
            chain = [0]

            def link(ins):
                chain[0] += 1
                ins.then_inc(dve_chain, 1)
                dve.wait_ge(dve_chain, chain[0])

            dve.wait_ge(in_conv, 32)
            dve.wait_ge(in_small, 96)
            dve.wait_ge(const_ready, 6)
            for c in range(4):
                wait_job(dve, f"glu_a{c}")
                dve.wait_ge(glu_sig, c + 1)
                dve.tensor_tensor(U[:, c, PAD:PAD + HT], half(f"glu_a{c}", 0), sq[:, c, 0:HT], ALU.mult)
                dve.tensor_tensor(U[:, c, PAD + HT:PAD + TP], half(f"glu_a{c}", 1, 128, TP - HT), sq[:, c, HT:TP], ALU.mult)
                dve.tensor_tensor(U[:, c, 2 * PAD + TP:UW], both(f"glu_a{c}")[:, 1, TP - HT:HT], sq[:, c, TP:T],
                                  ALU.mult).then_inc(u_ready, 1)
                dve.wait_ge(u_ready, c + 1)
                for j in range(CW):
                    parts = ((zT[:, c, 0:TP], U[:, c, j:j + TP], tap_prompt),
                             (zT[:, c, TP:T], U[:, c, PAD + TP + j:PAD + TP + j + TS], tap_sample))
                    for dst, src, tap in parts:
                        if j == 0:
                            ins = dve.tensor_scalar(dst, src, wdw[:, c, 0:1], vec[:, 0, c:c + 1], ALU.mult, ALU.add)
                        else:
                            dve.wait_ge(tap, c * CW + j)
                            ins = dve.scalar_tensor_tensor(dst, src, wdw[:, c, j:j + 1], dst, ALU.mult, ALU.add)
                        ins.then_inc(tap, 1)

            dve.wait_ge(lat_std, 1)
            link(dve.reciprocal(norms[:, 0, :], norms[:, 0, :]))
            dve.wait_ge(lat_raw, 5)
            for i in range(3):
                dve.scalar_tensor_tensor(qd[:, i, :], qd[:, i, :], gqa[:, i:i + 1], norms[:, 0, :], ALU.mult,
                                         ALU.mult).then_inc(qn_ready, 1)
            dve.wait_ge(lat_std, 2)
            link(dve.reciprocal(norms[:, 1, :], norms[:, 1, :]))
            for i in range(2):
                dve.scalar_tensor_tensor(ck[:, i, 0:TP], kvd[:, i, 0:TP], gkva[:, i:i + 1], norms[:, 1, 0:TP], ALU.mult, ALU.mult)
                dve.scalar_tensor_tensor(ck[:, i, TP + PAST:KEYS], kvd[:, i, TP:T], gkva[:, i:i + 1], norms[:, 1, TP:T],
                                         ALU.mult, ALU.mult).then_inc(ck_ready, 1)
            swap = list(range(16, 32)) + list(range(16))
            dve.wait_ge(kr_raw, 1)
            wait_job(dve, "kv_ss")
            link(dve.stream_shuffle(rp[0:32, 1, :], rp[0:32, 2, :], swap))
            dve.tensor_tensor(rp[0:32, 2, :], rp[0:32, 2, :], cos[0:32, :], ALU.mult)
            link(dve.tensor_tensor(rp[0:32, 1, :], rp[0:32, 1, :], sin[0:32, :], ALU.mult))
            dve.tensor_tensor(krot[:, 0:TP], rp[0:32, 2, 0:TP], rp[0:32, 1, 0:TP], ALU.add)
            dve.tensor_tensor(krot[:, TP + PAST:KEYS], rp[0:32, 2, TP:T], rp[0:32, 1, TP:T], ALU.add).then_inc(krot_ready, 1)

            wait_job(dve, "conv_mean")
            dve.tensor_scalar(split(cnorm[:, 0, :]), both("conv_mean"), 1.0 / CH, None, ALU.mult).then_inc(mean_read, 1)
            dve.wait_ge(mean_read, 1)
            for c in range(4):
                dve.tensor_tensor(zT[:, c, :], zT[:, c, :], cnorm[:, 0, :], ALU.subtract).then_inc(conv_cent, 1)

            def row_max(n):
                kind, i, h = UNITS[n]
                nr = TILES[i][1]
                nk = sum(k[2] for k in key_tiles(kind, i))
                dve.wait_ge(score_done, n + 1)
                if n >= 8:
                    dve.wait_ge(exp_done, n - 7)
                dve.tensor_reduce(nb[0:nr, n % 8:n % 8 + 1], PS[0:nr, n % 2, 0:nk], AX.X, ALU.max, negate=True).then_inc(max_done, 1)

            def evac_probs(n):
                kind, i, h = UNITS[n]
                nr = TILES[i][1]
                kts = key_tiles(kind, i)
                dve.wait_ge(pt_done, n + 1)
                if n >= 3:
                    dve.wait_ge(pv_done, n - 2)
                full = len([k for k in kts if k[2] == 128])
                src = PS[:, 2 + n % 2, :].rearrange("p (k t) -> p k t", k=4)
                dst = PT[:, n % 3, :].rearrange("p (k t) -> p k t", k=4)
                ins = dve.tensor_copy(dst[:, 0:full, 0:nr], src[:, 0:full, 0:nr])
                if full < len(kts):
                    ins = dve.tensor_copy(dst[0:TS, full, 0:nr], src[0:TS, full, 0:nr])
                ins.then_inc(pt_evac, 1)

            def normalise(g):
                kind, i = GROUPS[g]
                nr = TILES[i][1]
                heads, w = (MH, MD) if kind == "mem" else (NH, VD)
                dve.wait_ge(exp_done, last_of_group[g] + 1)
                link(dve.reciprocal(rinv[0:nr, g % 2, 0:heads], rs[0:nr, g % 2, 0:heads]))
                dve.wait_ge(pv_done, last_of_group[g] + 1)
                if g >= 2:
                    dve.wait_ge(ot_done, g - 1)
                dve.tensor_tensor(osb[0:nr, g % 2, :].rearrange("p (h v) -> p h v", h=heads),
                                  PS[0:nr, 4 + g % 2, :].rearrange("p (h v) -> p h v", h=heads),
                                  rinv[0:nr, g % 2, 0:heads].unsqueeze(2).to_broadcast([nr, heads, w]), ALU.mult).then_inc(o_norm, 1)

            def attend(first, end):
                for n in range(first, end + 3):
                    if n < end:
                        row_max(n)
                    if first <= n - 1 < end:
                        evac_probs(n - 1)
                    if first <= n - 2 < end and last_of_group[group_of[n - 2]] == n - 2:
                        normalise(group_of[n - 2])

            attend(0, MEM_LAST)
            dve.wait_ge(pv_done, MEM_LAST)
            dve.wait_ge(mem_out, 32)
            dve.wait_ge(in_past, 48)
            dve.tensor_copy(kh[64:96, :, :], krot.unsqueeze(1).to_broadcast([32, NH, KEYS])).then_inc(kr_copied, 1)
            for i in range(2):
                dve.wait_ge(ur_raw, i + 1)
                link(dve.stream_shuffle(rp[:, 1, :], rp[:, 0, :], swap))
                dve.tensor_tensor(rp[:, 0, :], rp[:, 0, :], cos, ALU.mult)
                link(dve.tensor_tensor(rp[:, 1, :], rp[:, 1, :], sin, ALU.mult))
                for q in range(4):
                    ins = dve.tensor_tensor(qh[64:96, 4 * i + q, :], rp[32 * q:32 * q + 32, 0, :], rp[32 * q:32 * q + 32, 1, :], ALU.add)
                ins.then_inc(ur_rot, 1)
            dve.wait_ge(conv_std, 1)
            link(dve.reciprocal(cnorm[:, 1, :], cnorm[:, 1, :]))
            for c in range(4):
                dve.tensor_tensor(zT[:, c, :], zT[:, c, :], cnorm[:, 1, :], ALU.mult).then_inc(conv_norm, 1)
            attend(MEM_LAST, MLA_LAST)

            for j in range(8):
                for n, name in enumerate(("yc", "ym", "yx")):
                    wait_job(dve, f"{name}_{j}")
                    dve.wait_ge(gate_sig, 3 * j + n + 1)
                    dve.tensor_tensor(split(gate[:, j % 2, n, :]), split(gate[:, j % 2, n, :]), both(f"{name}_{j}"),
                                      ALU.mult).then_inc(gate_mul, 1)

            link(dve.memset(lg[:, :, :], 0.0))
            for tt in range(NT + 2):
                if tt < NT:
                    t0, nr = TILES[tt]
                    wait_job(dve, f"c{tt}")
                    dve.wait_ge(in_xtok[tt % 2], 16 * (tt // 2 + 1))
                    dve.scalar_tensor_tensor(x1[0:nr, tt, :].rearrange("p (s d) -> p s d", s=2),
                                             xtok[0:nr, tt % 2, :].rearrange("p (s d) -> p s d", s=2), ALPHA,
                                             pair(f"c{tt}")[0:nr], ALU.mult, ALU.add).then_inc(ln1_res, 1)
                    dve.wait_ge(ln1_res, tt + 1)
                    dve.bn_stats(st[0:nr, tt % 2, 0, :], x1[0:nr, tt, 0:512])
                    link(dve.bn_stats(st[0:nr, tt % 2, 1, :], x1[0:nr, tt, 512:1024]))
                    dve.bn_aggr(mva[0:nr, tt % 2, :], st[0:nr, tt % 2, :, :].rearrange("p a b -> p (a b)")).then_inc(ln1_var, 1)
                    dve.wait_ge(ln1_std, tt + 1)
                    link(dve.reciprocal(rstd[0:nr, tt % 2, 1:2], rstd[0:nr, tt % 2, 0:1]))
                    dve.tensor_scalar(x1[0:nr, tt, :], x1[0:nr, tt, :], mva[0:nr, tt % 2, 0:1], rstd[0:nr, tt % 2, 1:2],
                                      ALU.subtract, ALU.mult).then_inc(ln1_hat, 1)
                if tt >= 2:
                    u = tt - 2
                    nr = TILES[u][1]
                    wait_job(dve, f"l{u}")
                    dve.tensor_tensor(lg[0:nr, u, :], half(f"l{u}", 0, nr, 36), rbias[0:nr, :], ALU.add).then_inc(lg_ready, 1)

            def wide(x, n):
                return x.unsqueeze(2).to_broadcast([128, NT, n])

            def first_max(x, n, m, cand, onehot):
                link(dve.tensor_reduce(gm[:, m], x, AX.X, ALU.max))
                link(dve.tensor_tensor(cand, x, wide(gm[:, m], n), ALU.is_equal))
                link(dve.tensor_tensor(cand, cand, desc[:, NE_G - n:].unsqueeze(1).to_broadcast([128, NT, n]), ALU.mult))
                link(dve.tensor_reduce(gm[:, 11], cand, AX.X, ALU.max))
                link(dve.tensor_tensor(onehot, cand, wide(gm[:, 11], n), ALU.is_equal))

            dve.wait_ge(lg_ready, NT)
            dve.wait_ge(route_const, 1)
            first_max(lg[:, :, 0:NG], NG, 0, g4[:, 0], g4[:, 2])
            dve.tensor_tensor(g4[:, 0], lg[:, :, 0:NG], wide(gm[:, 0], NG), ALU.subtract).then_inc(route_dve, 1)
            prod = e32[:, 3].rearrange("p t (g e) -> p t g e", g=NG)
            for g in range(NG):
                ins = dve.tensor_tensor(prod[:, :, g, :], lg[:, :, NG + 8 * g:NG + 8 * g + 8],
                                        wide(g4[:, 2, :, g], NE_G), ALU.mult)
            link(ins)
            link(dve.tensor_reduce(e8[:, 0], prod.rearrange("p t g e -> p t e g"), AX.X, ALU.add))
            first_max(e8[:, 0], NE_G, 1, e8[:, 1], e8[:, 2])
            link(dve.scalar_tensor_tensor(e8[:, 0], e8[:, 2], -1e30, e8[:, 0], ALU.mult, ALU.add))
            first_max(e8[:, 0], NE_G, 2, e8[:, 1], e8[:, 3])
            dve.tensor_tensor(gm[:, 4], gm[:, 2], gm[:, 1], ALU.subtract).then_inc(route_dve, 1)
            for c in range(2):
                hot = e32[:, c].rearrange("p t (g e) -> p t g e", g=NG)
                for g in range(NG):
                    ins = dve.tensor_tensor(hot[:, :, g, :], e8[:, 2 + c], wide(g4[:, 2, :, g], NE_G), ALU.mult)
            link(ins)
            dve.tensor_tensor(maskb[:, :, :], e32[:, 0], e32[:, 1], ALU.add).then_inc(mask_ready, 1)
            dve.wait_ge(route_exp, 2)
            link(dve.tensor_reduce(gm[:, 6], g4[:, 1], AX.X, ALU.add))
            dve.reciprocal(gm[:, 6], gm[:, 6])
            link(dve.tensor_scalar(gm[:, 7], gm[:, 5], 1.0, None, ALU.add))
            link(dve.reciprocal(gm[:, 7], gm[:, 7]))
            link(dve.tensor_tensor(wsel[:, 0, :], gm[:, 6], gm[:, 7], ALU.mult))
            dve.tensor_tensor(wsel[:, 1, :], wsel[:, 0, :], gm[:, 5], ALU.mult)
            wait_job(dve, "count")
            rank = half("rank", 0, 128, 160).rearrange("p (t e) -> p t e", t=NT)
            for c in range(2):
                link(dve.tensor_tensor(e32[:, 2], e32[:, c], rank, ALU.mult))
                dve.tensor_reduce(gm[:, 8], e32[:, 2], AX.X, ALU.add)
                link(dve.tensor_tensor(e32[:, 3], e32[:, c], iota[:, 0:NE].unsqueeze(1).to_broadcast([128, NT, NE]), ALU.mult))
                link(dve.tensor_reduce(gm[:, 9], e32[:, 3], AX.X, ALU.add))
                link(dve.tensor_scalar(gm[:, 10], gm[:, 8], float(CAP), None, ALU.is_ge))
                for k in range(2, NCH):
                    link(dve.scalar_tensor_tensor(gm[:, 10], gm[:, 8], float(k * CAP), gm[:, 10], ALU.is_ge, ALU.add))
                dve.scalar_tensor_tensor(slot[:, 0, c, :], gm[:, 10], -float(CAP), gm[:, 8], ALU.mult, ALU.add)
                dve.scalar_tensor_tensor(slot[:, 1, c, :], gm[:, 10], float(NE), gm[:, 9], ALU.mult, ALU.add).then_inc(slot_ready, 1)
                dve.wait_ge(slot_ready, c + 1)
                for tt in range(NT):
                    nr = TILES[tt][1]
                    dve.tensor_scalar(slot_row[0:nr, c, tt, :], iota[0:nr, 0:128], slot[0:nr, 0, c, tt:tt + 1], None, ALU.is_equal)
                    dve.tensor_scalar(slot_col[0:nr, c, tt, :], iota[0:nr, :], slot[0:nr, 1, c, tt:tt + 1],
                                      rowid[0:nr, c, tt:tt + 1], ALU.is_equal, ALU.mult).then_inc(onehot_ready, 1)
            wait_job(dve, "table")
            link(dve.tensor_scalar(empty[:, :], half("table", 0, 128, NCH * NE), 0.0, float(SKIP), ALU.is_equal, ALU.mult))
            dve.scalar_tensor_tensor(tabs[:, :], half("table", 0, 128, NCH * NE), -1.0, empty[:, :], ALU.add,
                                     ALU.add).then_inc(tab_ready, 1)
            dve.tensor_reduce(flag[:, :], half("count", 0, 128, NE), AX.X, ALU.max).then_inc(flag_ready, 1)
            dve.wait_ge(flag_ready, 1)

            def evac_rows():
                return dve.tensor_copy(xgT[:, 4:8, 0:CAP], PS[:, 1, :].rearrange("p (k t) -> p k t", k=4)[:, :, 0:CAP])

            def hidden():
                return dve.tensor_tensor(hm[0:CAP, :], hg[0:CAP, :], PS[0:CAP, 2, FE:2 * FE], ALU.mult)

            def rows_step(e):
                dve.wait_ge(e_tx, e + 1)
                dve.wait_ge(e_h, e)
                evac_rows().then_inc(e_xgT2, 1)

            def hidden_step(e):
                dve.wait_ge(e_silu, e + 1)
                dve.wait_ge(e_ht, e)
                hidden().then_inc(e_hm, 1)

            def result_step(e, b, k):
                dve.wait_ge(e_y, e + 1)
                dve.wait_ge(e_out[b], 16 * k)
                dve.tensor_copy(ysb[0:CAP, b, 512:1024], PS[0:CAP, 5, :]).then_inc(e_yb, 1)

            rows_step(0)
            hidden_step(0)
            rows_step(1)
            def expert_pair(h):
                e = h * 2 + 1
                hidden_step(e)
                rows_step(e + 1)
                result_step(e - 1, 0, h)
                hidden_step(e + 1)
                rows_step(e + 2)
                result_step(e, 1, h)

            expert_pair(0)
            with dve.Fori(1, NE // 2 - 1) as h:
                expert_pair(h)
            hidden_step(NE - 1)
            result_step(NE - 2, 0, NE // 2 - 1)
            result_step(NE - 1, 1, NE // 2 - 1)
            over = dve.value_load(flag[0:1, 0:1], min_val=0, max_val=T)
            with dve.If(over > CAP):
                with dve.Fori(0, NE * (NCH - 1)) as n:
                    dve.wait_ge(ov_silu, n + 1)
                    hidden().then_inc(ov_hm, 1)

            dve.wait_ge(x1_scaled, NT)
            for tt in range(NT):
                nr = TILES[tt][1]
                dve.wait_ge(in_y[tt], 32)
                for c in range(2):
                    link(dve.scalar_tensor_tensor(x1[0:nr, tt, :], yab[0:nr, tt, c, :], wsel[0:nr, c, tt:tt + 1], x1[0:nr, tt, :],
                                                  ALU.mult, ALU.add))
                dve.bn_stats(st[0:nr, tt % 2, 0, :], x1[0:nr, tt, 0:512])
                link(dve.bn_stats(st[0:nr, tt % 2, 1, :], x1[0:nr, tt, 512:1024]))
                dve.bn_aggr(mva[0:nr, tt % 2, :], st[0:nr, tt % 2, :, :].rearrange("p a b -> p (a b)")).then_inc(ln2_var, 1)
                dve.wait_ge(ln2_std, tt + 1)
                link(dve.reciprocal(rstd[0:nr, tt % 2, 1:2], rstd[0:nr, tt % 2, 0:1]))
                link(dve.tensor_scalar(x1[0:nr, tt, :], x1[0:nr, tt, :], mva[0:nr, tt % 2, 0:1], rstd[0:nr, tt % 2, 1:2],
                                       ALU.subtract, ALU.mult))
                dve.tensor_tensor(x1[0:nr, tt, :], x1[0:nr, tt, :], lnbc[0:nr, 2, :], ALU.mult).then_inc(ln2_hat, 1)

        @block.gpsimd
        def _(pool):
            chain = [0]

            def link(ins):
                chain[0] += 1
                ins.then_inc(pool_chain, 1)
                pool.wait_ge(pool_chain, chain[0])

            pool.memset(ones[:, :], 1.0).then_inc(const_ready, 1)
            pool.memset(eps[:, :], EPS).then_inc(const_ready, 1)
            pool.memset(U[:, :, 0:PAD], 0.0).then_inc(const_ready, 1)
            pool.memset(ident[:, :], 0.0)
            pool.memset(rowmask[:, :], 0.0)
            link(pool.memset(negrow[:, :], 0.0))
            pool.affine_select(out=ident[:, :], in_=ident[:, :], compare_op=ALU.not_equal, fill=1.0, base=0,
                               pattern=[[-1, 128]], channel_multiplier=1).then_inc(const_ready, 1)
            pool.memset(rowmask[0:1, 0:CAUSAL], 1.0).then_inc(const_ready, 1)
            pool.memset(negrow[0:1, :], -1e30).then_inc(const_ready, 1)
            pool.memset(onesb[:, :], 1.0)
            link(pool.memset(tri[:, :], 1.0))
            pool.affine_select(out=tri[:, :], in_=tri[:, :], compare_op=ALU.is_gt, fill=0.0, base=0,
                               pattern=[[1, 128]], channel_multiplier=-1)
            for i in range(NE_G):
                pool.memset(desc[:, i:i + 1], float(NE_G - i))
            pool.iota(iota_i[:, :], pattern=[[1, NCH * NE]], base=0, channel_multiplier=0)
            pool.iota(rowid_i[:, 0, :], pattern=[[128, NT]], base=1, channel_multiplier=1)
            link(pool.iota(rowid_i[:, 1, :], pattern=[[128, NT]], base=T + 1, channel_multiplier=1))
            pool.tensor_copy(iota[:, :], iota_i[:, :])
            pool.tensor_copy(rowid[:, :, :], rowid_i[:, :, :]).then_inc(route_const, 1)

            pool.wait_ge(u_ready, 4)
            pool.dma_start(o["conv_prompt_T"], U[:, :, TP:TP + PAD]).then_inc(conv_out, 16)
            pool.dma_start(o["conv_sample_T"], U[:, :, UW - PAD:UW]).then_inc(conv_out, 16)
            pool.wait_ge(ck_ready, 2)
            pool.dma_start(o["latent_T"][:, :, 0:TP], ck[:, :, 0:TP]).then_inc(lat_out, 16)
            pool.dma_start(o["latent_T"][:, :, TP:T], ck[:, :, TP + PAST:KEYS]).then_inc(lat_out, 16)
            pool.wait_ge(krot_ready, 1)
            pool.dma_start(o["krope_T"][:, 0:TP], krot[:, 0:TP]).then_inc(lat_out, 16)
            pool.dma_start(o["krope_T"][:, TP:T], krot[:, TP + PAST:KEYS]).then_inc(lat_out, 16)
            pool.wait_ge(mem_proj, 6)
            pool.dma_start(o["mem_k_T"], mkT[:, 0]).then_inc(mem_out, 16)
            pool.dma_start(o["mem_v"], mv[:, 0]).then_inc(mem_out, 16)
            for j in range(8):
                pool.wait_ge(gate_mul, 3 * j + 2)
                link(pool.tensor_tensor(gate[:, j % 2, 0, :], gate[:, j % 2, 0, :], gate[:, j % 2, 1, :], ALU.add))
                pool.wait_ge(gate_mul, 3 * j + 3)
                pool.tensor_tensor(merged[:, j, :], gate[:, j % 2, 0, :], gate[:, j % 2, 2, :], ALU.add).then_inc(merged_ready, 1)
            pool.wait_ge(in_ln, 64)
            for tt in range(NT):
                nr = TILES[tt][1]
                pool.wait_ge(ln1_hat, tt + 1)
                link(pool.tensor_tensor(x1[0:nr, tt, :], x1[0:nr, tt, :], lnbc[0:nr, 0, :], ALU.mult))
                pool.tensor_tensor(x1[0:nr, tt, :], x1[0:nr, tt, :], lnbc[0:nr, 1, :], ALU.add).then_inc(x1_ready, 1)

            link(pool.memset(xg[:, :, :], 0.0))
            pool.wait_ge(x1_out, 16 * 2 * NT)
            pool.wait_ge(tab_ready, 1)

            def gather(b, col):
                return pool.indirect_dma_start(xg[0:CAP, b, :], None, x1_d,
                                               bass.IndirectOffsetOnAxis(ap=tabs[0:CAP, col:col + 1], axis=0),
                                               bounds_check=2 * T - 1, oob_is_err=False)

            def scatter(b, col):
                return pool.indirect_dma_start(y_d, bass.IndirectOffsetOnAxis(ap=tabs[0:CAP, col:col + 1], axis=0),
                                               ysb[0:CAP, b, :], None, bounds_check=2 * T - 1, oob_is_err=False)

            for e in range(NB):
                gather(e, e).then_inc(e_rows[e], 16)
            for tt in range(NT):
                nr = TILES[tt][1]
                pool.tensor_scalar(x1[0:nr, tt, :], x1[0:nr, tt, :], ALPHA, None, ALU.mult).then_inc(x1_scaled, 1)
            for e in range(NE):
                if e + NB < NE:
                    pool.wait_ge(e_tx, e + 1)
                    gather(e % NB, e + NB).then_inc(e_rows[e % NB], 16)
                pool.wait_ge(e_ya, e + 1)
                pool.wait_ge(e_yb, e + 1)
                scatter(e % 2, e).then_inc(e_out[e % 2], 16)
            pool.wait_ge(flag_ready, 1)
            over = pool.value_load(flag[0:1, 0:1], min_val=0, max_val=T)
            with pool.If(over > CAP):
                for b in range(2):
                    pool.wait_ge(e_out[b], 16 * NE // 2)
                for e in range(NE):
                    for c in range(1, NCH):
                        n = e * (NCH - 1) + c - 1
                        gather(0, c * NE + e).then_inc(ov_rows, 16)
                        pool.wait_ge(ov_ysb, n + 1)
                        scatter(0, c * NE + e).then_inc(ov_out, 16)
                        pool.wait_ge(ov_out, 16 * (n + 1))
            for tt in range(NT):
                nr = TILES[tt][1]
                pool.wait_ge(ln2_hat, tt + 1)
                pool.tensor_tensor(x1[0:nr, tt, :], x1[0:nr, tt, :], lnbc[0:nr, 3, :], ALU.add).then_inc(ln2_out, 1)



def lay_out(x):
    def m_tiles(w):
        K, M = w.shape
        return w.reshape(K // 128, 128, M // 128, 128).transpose(2, 1, 0, 3).reshape(M // 128, 128, K)

    def fm(v):
        return v.reshape(-1, 128).T

    w = x["w_in"][0]
    c = np.cumsum([0, CH, CH, QL, KVL, ROPE, MH * MD, 3 * D])
    r = {}
    xs = np.concatenate([x["x_prompt"][0], x["x_sample"][0]], 0)
    r["x_tok"] = xs
    r["xT"] = xs.T.reshape(KT, 128, T).transpose(1, 0, 2)
    r["memT"] = x["mem_prompt"][0].T.reshape(KT, 128, MT).transpose(1, 0, 2)
    r["w_glu_t"] = np.concatenate([m_tiles(w[:, c[1]:c[2]]), m_tiles(w[:, c[0]:c[1]])], 0)
    r["w_q_t"] = m_tiles(w[:, c[2]:c[3]])
    r["w_kv_t"] = m_tiles(w[:, c[3]:c[4]])
    r["w_kr_t"] = w[:, c[4]:c[5]].reshape(KT, 128, ROPE).transpose(1, 0, 2).reshape(128, KT * ROPE)
    r["w_mq_t"] = m_tiles(w[:, c[5]:c[6]])
    r["w_gate_t"] = m_tiles(w[:, c[6]:c[7]])
    r["w_mk_t"] = m_tiles(x["w_mem_k"][0])
    r["w_mv_t"] = x["w_mem_v"][0].reshape(4, 2, 128, 512).transpose(0, 2, 1, 3).reshape(4, 128, 1024)
    uq = x["w_uq"][0].reshape(QL, NH, QK)
    uq = np.concatenate([uq[:, :, :NOPE].reshape(QL, -1), uq[:, :, NOPE:].reshape(QL, -1)], 1)
    r["w_uq_t"] = m_tiles(uq).reshape(3, 2, 128, QL).transpose(0, 2, 1, 3).reshape(3, 128, 2 * QL)
    r["w_uk_t"] = m_tiles(x["w_uk"][0].reshape(KVL, -1)).transpose(1, 0, 2).reshape(128, 4 * KVL)
    r["w_uv_t"] = x["w_uv"][0].reshape(2, 128, 512).transpose(1, 0, 2).reshape(128, 1024)
    r["w_como_t"] = np.concatenate([m_tiles(x["w_co"][0]), m_tiles(x["w_mo"][0])], 2)
    r["w_xo_t"] = m_tiles(x["w_mem_o"][0])
    r["conv_state_T"] = x["cache_conv"][0, 0].T.reshape(4, 128, PAD).transpose(1, 0, 2)
    r["w_dw_T"] = x["w_dw"][0].T.reshape(4, 128, CW).transpose(1, 0, 2)
    r["conv_vec"] = np.stack([fm(x[n][0]) for n in ("b_dw", "g_cn", "b_cn")], 1)
    r["g_qa_T"] = fm(x["g_qa"][0])
    r["g_kva_T"] = fm(x["g_kva"][0])
    r["b_gate_T"] = fm(x["b_gate"][0])
    half = ROPE // 2
    inv = np.power(np.float32(10000.0), -np.arange(half, dtype=np.float32) / np.float32(half)).astype(np.float32)
    pos = np.concatenate([np.arange(TP), PAST + np.arange(TS)]).astype(np.float32)
    ang = (inv[:, None] * pos[None, :]).astype(np.float32)
    cos, sin = np.cos(ang).astype(np.float32), np.sin(ang).astype(np.float32)
    r["rope_cos"] = np.tile(cos, (8, 1))
    r["rope_sin"] = np.tile(np.concatenate([-sin, sin], 0), (4, 1))
    r["past_krope_T"] = x["cache_mla_krope"][0, 0].T
    r["past_lat_T"] = x["cache_mla_latent"][0, 0].T.reshape(2, 128, PAST)
    r["mem_k_T"] = x["cache_mem_k"][0, 0].transpose(2, 1, 0)
    r["cache_mem_v"] = x["cache_mem_v"][0, 0].reshape(2, 128, MH * MD).transpose(1, 0, 2)
    wr = np.concatenate([x["w_group"][0], x["w_router"][0]], 1)
    r["w_route"] = wr.reshape(KT, 128, NG + NE).transpose(1, 0, 2)
    r["b_route"] = np.concatenate([x["b_group"], x["b_router"]], 1)
    r["w_out"] = x["w_out"][0]
    for n in ("g_ln1", "b_ln1", "g_ln2", "b_ln2"):
        r[n] = x[n]
    up = np.stack([x["w_e1"].reshape(NE, KT, 128, FE), x["w_e3"].reshape(NE, KT, 128, FE)], 1)
    r["w_e13"] = up.transpose(0, 3, 1, 2, 4).reshape(NE, 128, 2 * KT * FE)
    r["w_e2"] = x["w_e2"].reshape(NE, 2, 128, D).transpose(0, 2, 1, 3).reshape(NE, 128, 2 * D)
    return r


OUTS = {"y_prompt": (TP, D), "y_sample": (TS, D), "conv_prompt_T": (128, 4, PAD), "conv_sample_T": (128, 4, PAD),
        "latent_T": (128, 2, T), "krope_T": (ROPE, T), "mem_k_T": (128, MH, MT), "mem_v": (128, 2, MH * MD)}


def kernel(**inputs):
    import concourse.bacc as bacc
    from concourse.bass_utils import run_bass_kernel_spmd

    x = {k: np.asarray(v) for k, v in inputs.items()}
    nc = bacc.Bacc("TRN2", target_bir_lowering=False, num_devices=1)
    arrays, a, o = {}, {}, {}
    for name, v in lay_out(x).items():
        v = np.ascontiguousarray(v)
        arrays[f"in_{name}"] = v
        a[name] = nc.dram_tensor(f"in_{name}", v.shape, mybir.dt.from_np(v.dtype), kind="ExternalInput").ap()
    for name, shape in OUTS.items():
        o[name] = nc.dram_tensor(f"out_{name}", shape, F32, kind="ExternalOutput").ap()
    program(nc, a, o)
    r = run_bass_kernel_spmd(nc, [arrays], core_ids=[0]).results[0]
    g = {n: np.asarray(r[f"out_{n}"]) for n in OUTS}

    def rows(v):
        return np.ascontiguousarray(v.transpose(2, 1, 0).reshape(v.shape[2], -1))

    lat = rows(g["latent_T"])
    kr = np.ascontiguousarray(g["krope_T"].T)
    mk = np.ascontiguousarray(g["mem_k_T"].transpose(2, 1, 0))
    mv = np.ascontiguousarray(g["mem_v"].transpose(1, 0, 2)).reshape(MT, MH, MD)
    return (g["y_prompt"][None], g["y_sample"][None], rows(g["conv_prompt_T"])[None, None], lat[None, None, :TP],
            kr[None, None, :TP], mk[None, None], mv[None, None], rows(g["conv_sample_T"])[None, None],
            lat[None, None, TP:], kr[None, None, TP:])
```

```python
from contextlib import ExitStack

import numpy as np

import concourse.bass as bass
from concourse import mybir

F32 = mybir.dt.float32
F32R = mybir.dt.float32r
BF16 = mybir.dt.bfloat16
I32 = mybir.dt.int32
ALU = mybir.AluOpType
ACT = mybir.ActivationFunctionType
AX = mybir.AxisListType

D = 1024
TP, TS = 512, 64
T = TP + TS
HT = T // 2
PAST = 256
CH = 512
CW = 31
PAD = CW - 1
NH, NOPE, ROPE, VD = 8, 64, 32, 64
QK = NOPE + ROPE
QL, KVL = 384, 256
KEYS = TP + PAST + TS
MH, MD, MT = 4, 128, 256
EPS = 1e-5
ALPHA = 2.0 ** 0.25
NG, NE_G, FE = 4, 8, 256
NE = NG * NE_G
KT = D // 128
CAP = 128
NB = 4
NCH = -(-T // CAP)
TILES = [(i * 128, 128) for i in range(4)] + [(TP, TS)]
NT = len(TILES)
SKIP = 1 << 14
GAIN_BY_DVE = NT - 2
CAUSAL = 64
UW = PAD + TP + PAD + TS

JOBS = []
for _c in range(4):
    JOBS += [f"glu_b{_c}", f"glu_a{_c}"]
JOBS += ["q0", "q1", "q2", "kv0", "kv1", "kr", "mk0", "mk1", "q_ss", "kv_ss", "mk2", "mk3",
         "mv0", "mv1", "mq0", "mq1", "mq2", "mq3", "conv_mean"]
JOBS += [f"un{i}" for i in range(4)] + ["ur0", "ur1", "conv_var"] + [f"uk{i}" for i in range(4)] + [f"uv{i}" for i in range(7)]
for _j in range(8):
    JOBS += [f"g0_{_j}", f"g1_{_j}", f"yc_{_j}", f"ym_{_j}", f"g2_{_j}", f"yx_{_j}"]
JOBS += ["c0", "c1", "t0", "c2", "l0", "t1", "c3", "l1", "t2", "c4", "l2", "t3", "l3", "t4", "l4", "rank", "count", "table"]
JOB = {n: i for i, n in enumerate(JOBS)}

RING = 3
SLOT = 1024
ITEMS = []
for _c in range(4):
    ITEMS += [(f"glu_b{_c}", 1024, f"glu_b{_c}"), (f"glu_a{_c}", 1024, f"glu_a{_c}")]
ITEMS += [(n, 1024, n) for n in ("q0", "q1", "q2", "kv0", "kv1")] + [("kr", 256, "kr")]
ITEMS += [(f"mk{i}", 1024, f"mk{i}") for i in range(4)] + [(f"mv_{i}", 1024, "mv1") for i in range(4)]
ITEMS += [(f"mq{i}", 1024, f"mq{i}") for i in range(4)]
ITEMS += [("uq0", 768, "un1"), ("uq1", 768, "un3"), ("uq2", 768, "ur1"), ("uk", 1024, "uk3"), ("uv", 1024, "uv6")]
for _j in range(8):
    ITEMS += [(f"g0_{_j}", 1024, f"g0_{_j}"), (f"g1_{_j}", 1024, f"g1_{_j}"), (f"comx_{_j}", 1024, f"ym_{_j}"),
              (f"g2_{_j}", 1024, f"g2_{_j}"), (f"xo_{_j}", 512, f"yx_{_j}")]
ITEM = {n: i for i, (n, _, _) in enumerate(ITEMS)}
SPLIT = [n for n, _, _ in ITEMS if n != "kr" and n[0] != "u" and n[:2] not in ("mk", "mv")]
SP_AT = {n: i for i, n in enumerate(SPLIT)}

MEM_UNITS = [("mem", i, h) for i in range(NT) for h in range(MH)]
MLA_UNITS = [("mla", i, h) for i in range(NT) for h in range(NH)]


def key_tiles(kind, i):
    if kind == "mem":
        return [(0, 0, 128), (1, 128, 128)]
    if i < 4:
        return [(k, 128 * k, 128) for k in range(i + 1)]
    return [(4, TP, 128), (5, TP + 128, 128), (6, TP + PAST, TS)]


def program(nc, a, o):
    ctx = ExitStack()
    with ctx:
        def sb(name, shape, dt=F32):
            return ctx.enter_context(nc.sbuf_tensor(name, shape, dt))

        def sem(name):
            return ctx.enter_context(nc.semaphore(name))

        XHL, BR, QGo, RAW, WHL, KMo, WFo, END = 0, 9216, 16128, 30976, 34048, 38144, 42240, 50496

        ident = sb("ident", [128, 128])
        ones = sb("ones", [128, 128])
        rowmask = sb("rowmask", [128, 128])
        negrow = sb("negrow", [128, 64])
        wdw = sb("wdw", [128, 4, CW])
        vec = sb("vec", [128, 3, 4])
        gqa = sb("gqa", [128, 3])
        gkva = sb("gkva", [128, 2])
        bgate = sb("bgate", [128, 24])
        eps = sb("eps", [128, 1])
        warm = sb("warm", [128, 1])
        nb = sb("nb", [128, 8])
        rs = sb("rs", [128, 2, 8])
        rinv = sb("rinv", [128, 2, 8])
        st = sb("st", [128, 2, 2, 6])
        mva = sb("mva", [128, 2, 2])
        rstd = sb("rstd", [128, 2, 3])
        wr = sb("wr", [128, KT, 36])
        rbias = sb("rbias", [128, 36])
        lg = sb("lg", [128, NT, 36])
        tri = sb("tri", [128, 128], BF16)
        onesb = sb("onesb", [128, 128], BF16)
        desc = sb("desc", [128, NE_G])
        iota_i = sb("iota_i", [128, NCH * NE], I32)
        iota = sb("iota", [128, NCH * NE])
        gm = sb("gm", [128, 12, NT])
        g4 = sb("g4", [128, 3, NT, NG])
        maskb = sb("maskb", [128, NT, NE], BF16)
        wsel = sb("wsel", [128, 2, NT])
        slot = sb("slot", [128, 2, 2, NT])
        rowid_i = sb("rowid_i", [128, 2, NT], I32)
        rowid = sb("rowid", [128, 2, NT])
        tabs = sb("tabs", [128, NCH * NE], I32)
        flag = sb("flag", [128, 1], I32)

        base = (nc.sbuf_base + 31) // 32 * 32
        assert base + 4 * END <= nc.sbuf_usable_end

        def region(name, at, n):
            return nc.alloc_sbuf_tensor_at(name, [128, n], F32, offset=base + 4 * at)[:, :]

        XH = nc.alloc_sbuf_tensor_at("x_hi", [128, KT, T], F32R, offset=base + 4 * XHL)
        XL = nc.alloc_sbuf_tensor_at("x_lo", [128, KT, T], F32R, offset=base + 4 * (XHL + 4608))
        WH = nc.alloc_sbuf_tensor_at("w_hi", [128, 2, SLOT], F32R, offset=base + 4 * WHL)
        WL = nc.alloc_sbuf_tensor_at("w_lo", [128, 2, SLOT], F32R, offset=base + 4 * (WHL + 2 * SLOT))
        zT = region("conv_z", BR, 2304).rearrange("p (c t) -> p c t", c=4)
        omT = region("mla_out", BR + 2304, 2304).rearrange("p (c t) -> p c t", c=4)
        oxT = region("mem_out_T", BR + 4608, 2304).rearrange("p (c t) -> p c t", c=4)
        branch = {"z": zT, "om": omT, "ox": oxT}
        BH = {n: nc.alloc_sbuf_tensor_at(f"{n}_hi", [128, 4, T], F32R, offset=base + 4 * (WFo + 2304 * i)) for i, n in enumerate(branch)}
        BL = {n: nc.alloc_sbuf_tensor_at(f"{n}_lo", [128, 4, T], F32R, offset=base + 4 * (BR + 2304 * i)) for i, n in enumerate(branch)}
        x_raw = region("x_raw", BR + 2304, 4608).rearrange("p (k t) -> p k t", k=KT)
        QG = region("heads", QGo, 14848)
        QH, GH = QG[:, 0:4608], QG[:, 4608:14848]
        norms = QH[:, 0:1152].rearrange("p (n t) -> p n t", n=2)
        memT = QH[:, 1152:3200].rearrange("p (k m) -> p k m", k=KT)
        qh = QH.rearrange("p (h t) -> p h t", h=NH)
        merged = QH.rearrange("p (k t) -> p k t", k=KT)
        kh = GH[:, 0:6656].rearrange("p (h t) -> p h t", h=NH)
        V = GH[:, 6656:10240].rearrange("p (k n) -> p k n", k=7)
        memq = GH[:, 0:2304].rearrange("p (h t) -> p h t", h=MH)
        mkT = GH[:, 2304:4352].rearrange("p (s h m) -> p s h m", s=2, h=MH)
        mv = GH[:, 4352:6400].rearrange("p (s k n) -> p s k n", s=2, k=2)
        sq = GH[:, 6656:8960].rearrange("p (c t) -> p c t", c=4)
        kvd = GH[:, 8960:10112].rearrange("p (c t) -> p c t", c=2)
        w_out = GH[:, 0:8192].rearrange("p (k n) -> p k n", k=KT)
        MERGED_H = nc.alloc_sbuf_tensor_at("merged_hi", [128, KT, T], F32R, offset=base + 4 * XHL)
        MERGED_L = nc.alloc_sbuf_tensor_at("merged_lo", [128, KT, T], F32R, offset=base + 4 * QGo)
        WOUT_H = nc.alloc_sbuf_tensor_at("w_out_hi", [128, KT, D], F32R, offset=base + 4 * WFo)
        WOUT_L = nc.alloc_sbuf_tensor_at("w_out_lo", [128, KT, D], F32R, offset=base + 4 * (QGo + 4608))
        xtok = GH[:, 8192:10240].rearrange("p (b d) -> p b d", b=2)
        ring = region("raw_ring", RAW, RING * SLOT).rearrange("p (r n) -> p r n", r=RING)
        x1 = region("x1_tiles", RAW, 5120).rearrange("p (t d) -> p t d", t=NT)
        KM = region("attn_tmp", KMo, 4096)
        U = KM[:, 0:2544].rearrange("p (c t) -> p c t", c=4)
        Pb = KM[:, 0:1536].rearrange("p (b n) -> p b n", b=3)
        PT = KM[:, 1536:3072].rearrange("p (b n) -> p b n", b=3)
        osb = KM[:, 3072:4096].rearrange("p (b n) -> p b n", b=2)
        gate = KM[:, 0:3456].rearrange("p (b n t) -> p b n t", b=2, n=3)
        lnbc = KM.rearrange("p (n d) -> p n d", n=4)
        WF = region("proj_tmp", WFo, 8256)
        qd = WF[:, 0:1728].rearrange("p (c t) -> p c t", c=3)
        cos = WF[:, 1728:2304]
        sin = WF[:, 2304:2880]
        krot = WF[0:32, 2880:3712]
        rp = WF[:, 3712:5440].rearrange("p (n t) -> p n t", n=3)
        ck = WF[:, 5440:7104].rearrange("p (c t) -> p c t", c=2)
        cnorm = WF[:, 7104:8256].rearrange("p (n t) -> p n t", n=2)
        we = [WF[:, 0:6144], region("expert1", XHL, 6144), region("expert2", XHL + 6144, 6144), QG[:, 0:6144]]
        w13 = [w[:, 0:4096].rearrange("p (s k f) -> p s k f", s=2, k=KT) for w in we]
        w2 = [w[:, 4096:6144].rearrange("p (j d) -> p j d", j=2) for w in we]
        w2_at = [WFo + 4096, XHL + 4096, XHL + 6144 + 4096, QGo + 4096]
        W2L = [nc.alloc_sbuf_tensor_at(f"w2_lo{b}", [128, 2, D], F32R, offset=base + 4 * at) for b, at in enumerate(w2_at)]
        W2H = [nc.alloc_sbuf_tensor_at(f"w2_hi{b}", [128, 2, D], F32R, offset=base + 4 * (QGo + 6144 + 2048 * b)) for b in range(2)]
        HTH = nc.alloc_sbuf_tensor_at("hidden_hi", [128, 2, CAP], F32R, offset=base + 4 * (QGo + 10240))
        HTL = nc.alloc_sbuf_tensor_at("hidden_lo", [128, 2, CAP], F32R, offset=base + 4 * (QGo + 10496))
        xg = [region("rows0", RAW + 5120, 1024), region("rows1", RAW + 6144, 1024), WF[:, 6144:7168], WF[:, 7168:8192]]
        MISC = region("moe_tmp", XHL + 12288, 3840)
        x1T = MISC[:, 0:2048].rearrange("p (b k t) -> p b k t", b=2, k=KT)
        slot_col = MISC[:, 0:1600].rearrange("p (c t n) -> p c t n", c=2, t=NT)
        slot_row = MISC[:, 1600:2880].rearrange("p (c t n) -> p c t n", c=2, t=NT)
        e32 = MISC[:, 2880:3520].rearrange("p (n t e) -> p n t e", n=4, t=NT)
        e8 = MISC[:, 3520:3680].rearrange("p (n t e) -> p n t e", n=4, t=NT)
        empty = MISC[:, 3680:3840]
        ysb = MISC[:, 0:2048].rearrange("p (b d) -> p b d", b=2)
        xgT = MISC[:, 2048:3072].rearrange("p (k s) -> p k s", k=KT)
        hg = MISC[:, 3072:3328]
        hm = MISC[:, 3328:3584]
        hT = MISC[:, 3584:3840].rearrange("p (j s) -> p j s", j=2)
        yab = [region(f"expert_out{t}", XHL + 2048 * t, 2048) for t in range(NT)]

        PS = ctx.enter_context(nc.psum_tensor("PS", [128, 8, 512], F32))

        x1_d = nc.dram_tensor("x1_rows", (2 * T, D), F32, kind="Internal").ap()
        y_d = nc.dram_tensor("expert_rows", (2 * T, D), F32, kind="Internal").ap()

        ring_full = [sem(f"ring_full{i}") for i in range(RING)]
        job_done = sem("job_done")
        in_x = [sem(f"in_x{i}") for i in range(4)]
        in_small = sem("in_small")
        in_conv = sem("in_conv")
        in_rope = sem("in_rope")
        in_mem = sem("in_mem")
        in_cache = sem("in_cache")
        in_past = sem("in_past")
        in_wout = sem("in_wout")
        in_ln = sem("in_ln")
        in_xtok = [sem("in_xtok0"), sem("in_xtok1")]
        in_route = sem("in_route")
        out_sem = sem("out_sem")
        const_ready = sem("const_ready")
        pool_chain = sem("pool_chain")
        dve_chain = sem("dve_chain")
        act_chain = sem("act_chain")
        glu_sig = sem("glu_sig")
        glu_raw = sem("glu_raw")
        u_ready = sem("u_ready")
        x_hi = sem("x_hi_done")
        x_lo = sem("x_lo_done")
        w_hi = sem("w_hi_done")
        w_lo = sem("w_lo_done")
        ox_split = sem("ox_split")
        z_hi = sem("z_hi_done")
        z_split = sem("z_split")
        om_split = sem("om_split")
        branch_hi = sem("branch_hi")
        mv_used = sem("mv_used")
        tap_prompt = sem("tap_prompt")
        tap_sample = sem("tap_sample")
        kr_raw = sem("kr_raw")
        mean_read = sem("mean_read")
        conv_std = sem("conv_std")
        route_const = sem("route_const")
        conv_out = sem("conv_out")
        lat_out = sem("lat_out")
        mem_out = sem("mem_out")
        conv_cent = sem("conv_cent")
        conv_sq = sem("conv_sq")
        conv_norm = sem("conv_norm")
        z_ready = sem("z_ready")
        lat_raw = sem("lat_raw")
        lat_sq = sem("lat_sq")
        lat_std = sem("lat_std")
        qn_ready = sem("qn_ready")
        ck_ready = sem("ck_ready")
        krot_ready = sem("krot_ready")
        mem_proj = sem("mem_proj")
        ur_raw = sem("ur_raw")
        ur_rot = sem("ur_rot")
        qk_ready = sem("qk_ready")
        kr_copied = sem("kr_copied")
        score_done = sem("score_done")
        max_done = sem("max_done")
        exp_done = sem("exp_done")
        pt_done = sem("pt_done")
        pt_evac = sem("pt_evac")
        pv_done = sem("pv_done")
        o_norm = sem("o_norm")
        ot_done = sem("ot_done")
        ot_evac = sem("ot_evac")
        gate_sig = sem("gate_sig")
        gate_mul = sem("gate_mul")
        merged_ready = sem("merged_ready")
        merged_hi = sem("merged_hi_done")
        merged_lo = sem("merged_lo_done")
        wout_hi = sem("w_out_hi_done")
        wout_lo = sem("w_out_lo_done")
        ln1_res = sem("ln1_res")
        ln1_var = sem("ln1_var")
        ln1_std = sem("ln1_std")
        ln1_hat = sem("ln1_hat")
        x1_ready = sem("x1_ready")
        x1_out = sem("x1_out")
        x1T_ready = sem("x1T_ready")
        lg_ready = sem("lg_ready")
        route_dve = sem("route_dve")
        route_exp = sem("route_exp")
        mask_ready = sem("mask_ready")
        slot_ready = sem("slot_ready")
        onehot_ready = sem("onehot_ready")
        tab_ready = sem("tab_ready")
        flag_ready = sem("flag_ready")
        x1_scaled = sem("x1_scaled")
        we13 = [sem(f"we13_{i}") for i in range(NB)]
        we2 = [sem(f"we2_{i}") for i in range(NB)]
        e_rows = [sem(f"e_rows_{i}") for i in range(NB)]
        e_tx = sem("e_tx")
        e_xgT = sem("e_xgT")
        e_xgT2 = sem("e_xgT2")
        e_h = sem("e_h")
        e_silu = sem("e_silu")
        e_hm = sem("e_hm")
        e_ht = sem("e_ht")
        e_hT = sem("e_hT")
        e_hTlo = sem("e_hTlo")
        w2_hi = sem("w2_hi_done")
        w2_lo = sem("w2_lo_done")
        e_y = sem("e_y")
        e_ya = sem("e_ya")
        e_yb = sem("e_yb")
        e_out = [sem("e_out0"), sem("e_out1")]
        ov_w = sem("ov_w")
        ov_rows = sem("ov_rows")
        ov_tx = sem("ov_tx")
        ov_xgT = sem("ov_xgT")
        ov_h = sem("ov_h")
        ov_silu = sem("ov_silu")
        ov_hm = sem("ov_hm")
        ov_ht = sem("ov_ht")
        ov_hT = sem("ov_hT")
        ov_y = sem("ov_y")
        ov_ysb = sem("ov_ysb")
        ov_out = sem("ov_out")
        in_y = [sem(f"in_y{i}") for i in range(NT)]
        ln2_var = sem("ln2_var")
        ln2_std = sem("ln2_std")
        ln2_hat = sem("ln2_hat")
        ln2_gain = sem("ln2_gain")
        ln2_last = sem("ln2_last")
        ln2_scales = sem("ln2_scales")
        ln2_out = sem("ln2_out")

        def pair(name):
            p = JOB[name] % 4
            return PS[:, 2 * p:2 * p + 2, :]

        def half(name, s, m=128, n=HT):
            return PS[0:m, 2 * (JOB[name] % 4) + s, 0:n]

        def both(name, m=128, n=HT):
            return PS[0:m, 2 * (JOB[name] % 4):2 * (JOB[name] % 4) + 2, 0:n]

        def wait_job(eng, name):
            eng.wait_ge(job_done, JOB[name] + 1)

        def read_of(name):
            kind = name.rstrip("0123456789")
            i = int(name[len(kind):] or 0)
            if kind.endswith("_") and kind[0] in "gy":
                gates = {"g0_": 0, "g1_": 1, "g2_": 2}
                return (gate_sig, 3 * i + gates[kind] + 1) if kind in gates else (gate_mul, 3 * i + {"yc_": 0, "ym_": 1, "yx_": 2}[kind] + 1)
            return {
                "glu_b": (glu_sig, i + 1), "glu_a": (glu_raw, i + 1), "q": (lat_raw, i + 1), "kv": (lat_raw, i + 4),
                "kr": (kr_raw, 1), "q_ss": (lat_std, 1), "kv_ss": (lat_std, 2), "mk": (mem_proj, i + 1),
                "mv": (mem_proj, i + 5), "mq": (mem_proj, i + 7), "conv_mean": (mean_read, 1), "conv_var": (conv_std, 1),
                "un": (qk_ready, 2 * i + 2), "ur": (ur_raw, i + 1), "uk": (qk_ready, 2 * i + 10), "uv": (qk_ready, i + 17),
                "c": (ln1_res, i + 1), "t": (x1T_ready, i + 1), "l": (lg_ready, i + 1), "rank": (slot_ready, 2), "table": (tab_ready, 1),
                "count": (flag_ready, 1),
            }[kind]

        def split(ap):
            return ap.rearrange("p (s t) -> p s t", s=2)

        def released(name):
            if name in SP_AT:
                return (w_lo, SP_AT[name] + 1)
            if name[:3] == "mv_" and name != "mv_3":
                return (mv_used, int(name[3:]) + 1)
            return (job_done, JOB[ITEMS[ITEM[name]][2]] + 1)

        def w_item(name):
            return ring[:, ITEM[name] % RING, :]

        MEM_LAST, MLA_LAST = len(MEM_UNITS), len(MEM_UNITS) + len(MLA_UNITS)
        UNITS = MEM_UNITS + MLA_UNITS
        GROUPS = []
        for u in UNITS:
            if u[:2] not in GROUPS:
                GROUPS.append(u[:2])
        group_of = [GROUPS.index(u[:2]) for u in UNITS]
        last_of_group = {g: max(n for n, x in enumerate(group_of) if x == g) for g in range(len(GROUPS))}
        N_G = len(GROUPS)
        N_MEM_G = NT

        LOW_BY_DVE = [SP_AT[f"g0_{j}"] for j in range(1, 8)]

        def low_part(eng, n):
            i = ITEM[SPLIT[n]]
            size = ITEMS[i][1]
            eng.wait_ge(w_hi, n + 1)
            if n >= 1:
                eng.wait_ge(w_lo, n)
            eng.tensor_tensor(WL[:, n % 2, 0:size], ring[:, i % RING, 0:size], WH[:, n % 2, 0:size].bitcast(F32),
                              ALU.subtract).then_inc(w_lo, 1)

        block = ctx.enter_context(nc.Block())

        @block.sync
        def _(sp):
            def src(name):
                for key in ("glu_b", "glu_a"):
                    if name.startswith(key):
                        return a["w_glu_t"][int(name[5:]) + 4 * (key == "glu_a")]
                if name[0] == "q":
                    return a["w_q_t"][int(name[1:])]
                if name == "kr":
                    return a["w_kr_t"]
                if name[:2] == "kv":
                    return a["w_kv_t"][int(name[2:])]
                if name[:2] == "mk":
                    return a["w_mk_t"][int(name[2:])]
                if name[:2] == "mv":
                    return a["w_mv_t"][int(name[3:])]
                if name[:2] == "mq":
                    return a["w_mq_t"][int(name[2:])]
                if name[:2] == "uq":
                    return a["w_uq_t"][int(name[2:])]
                if name == "uk":
                    return a["w_uk_t"]
                if name == "uv":
                    return a["w_uv_t"]
                j = int(name.split("_")[1])
                if name[0] == "g":
                    return a["w_gate_t"][8 * int(name[1]) + j]
                if name[:4] == "comx":
                    return a["w_como_t"][j]
                return a["w_xo_t"][j]

            def load_expert_up(e, b):
                return sp.dma_start(we[b][:, 0:4096], a["w_e13"][bass.ds(e, 1)].rearrange("a p n -> p (a n)")).then_inc(we13[b], 16)

            def load_expert_down(e, b):
                return sp.dma_start(we[b][:, 4096:6144], a["w_e2"][bass.ds(e, 1)].rearrange("a p n -> p (a n)")).then_inc(we2[b], 16)

            sp.dma_start(ring[:, 0, :], src("glu_b0")).then_inc(ring_full[0], 16)
            for q in range(4):
                sp.dma_start(x_raw[:, 2 * q:2 * q + 2, :], a["xT"][:, 2 * q:2 * q + 2, :]).then_inc(in_x[q], 16)
            for i, (name, n, _) in enumerate(ITEMS):
                if i == 0:
                    continue
                if i >= RING:
                    sp.wait_ge(*released(ITEMS[i - RING][0]))
                sp.dma_start(ring[:, i % RING, 0:n], src(name)).then_inc(ring_full[i % RING], 16)
                if name == "glu_a0":
                    sp.dma_start(U[:, :, PAD + TP:2 * PAD + TP], a["conv_state_T"]).then_inc(in_conv, 16)
                    sp.dma_start(wdw[:, :, :], a["w_dw_T"]).then_inc(in_conv, 16)
                    for dst, key in ((vec, "conv_vec"), (gqa, "g_qa_T"), (gkva, "g_kva_T"), (bgate, "b_gate_T")):
                        sp.dma_start(dst[:], a[key]).then_inc(in_small, 16)
                if name == "glu_a1":
                    sp.dma_start(memT, a["memT"]).then_inc(in_mem, 16)
                    sp.dma_start(cos, a["rope_cos"]).then_inc(in_rope, 16)
                    sp.dma_start(sin, a["rope_sin"]).then_inc(in_rope, 16)
                if name == "glu_a2":
                    sp.dma_start(krot[:, TP:TP + PAST], a["past_krope_T"]).then_inc(in_past, 16)
                    for c in range(2):
                        sp.dma_start(ck[:, c, TP:TP + PAST], a["past_lat_T"][c]).then_inc(in_past, 16)
                if name == "glu_a3":
                    sp.dma_start(mkT[:, 1], a["mem_k_T"]).then_inc(in_cache, 16)
                    sp.dma_start(mv[:, 1], a["cache_mem_v"]).then_inc(in_cache, 16)
                if name == "q0":
                    sp.dma_start(wr[:, :, :], a["w_route"]).then_inc(in_route, 16)
                    sp.dma_start(rbias[:, :], a["b_route"].broadcast_to([128, 36])).then_inc(in_route, 16)
                if name == "g0_1":
                    sp.wait_ge(pv_done, MLA_LAST)
                    sp.dma_start(w_out, a["w_out"].rearrange("(k p) n -> p k n", p=128)).then_inc(in_wout, 16)
                    for b in range(2):
                        sp.dma_start(xtok[:, b, :], a["x_tok"][128 * b:128 * b + 128]).then_inc(in_xtok[b], 16)
            sp.wait_ge(merged_ready, 8)
            for n, name in enumerate(("g_ln1", "b_ln1", "g_ln2", "b_ln2")):
                sp.dma_start(lnbc[:, n, :], a[name].broadcast_to([128, D])).then_inc(in_ln, 16)
            load_expert_up(2, 2)
            load_expert_down(2, 2)
            for tt in range(2, NT):
                t0, nr = TILES[tt]
                sp.wait_ge(ln1_res, tt - 1)
                sp.dma_start(xtok[0:nr, tt % 2, :], a["x_tok"][t0:t0 + nr]).then_inc(in_xtok[tt % 2], 16)
            for tt in range(NT):
                t0, nr = TILES[tt]
                if tt == NT - 1:
                    wait_job(sp, "c4")
                    load_expert_up(0, 0)
                    load_expert_down(0, 0)
                sp.wait_ge(x1_ready, tt + 1)
                for c in range(2):
                    sp.dma_start(x1_d[c * T + t0:c * T + t0 + nr], x1[0:nr, tt, :]).then_inc(x1_out, 16)
            for e in (1, 3):
                load_expert_up(e, e)
                load_expert_down(e, e)
            def load_next(e, b, more=True):
                if more:
                    sp.wait_ge(e_h, e - NB + 2)
                    load_expert_up(e + 1, (b + 1) % NB)
                sp.wait_ge(e_y, e - NB + 1)
                load_expert_down(e, b)

            sp.wait_ge(e_h, 1)
            load_expert_up(NB, 0)
            with sp.Fori(1, NE // NB - 1) as r:
                for b in range(NB):
                    load_next(r * NB + b, b)
            for b in range(NB):
                load_next(NE - NB + b, b, more=b < NB - 1)

            sp.wait_ge(e_y, NE)
            sp.wait_ge(flag_ready, 1)
            over = sp.value_load(flag[0:1, 0:1], min_val=0, max_val=T)
            with sp.If(over > CAP):
                def load_again(e):
                    sp.dma_start(we[0][:, 0:4096], a["w_e13"][bass.ds(e, 1)].rearrange("a p n -> p (a n)")).then_inc(ov_w, 16)
                    sp.dma_start(we[0][:, 4096:6144], a["w_e2"][bass.ds(e, 1)].rearrange("a p n -> p (a n)")).then_inc(ov_w, 16)

                load_again(0)
                with sp.Fori(1, NE) as e:
                    sp.wait_ge(ov_y, e * (NCH - 1))
                    load_again(e)
                sp.wait_ge(ov_out, 16 * NE * (NCH - 1))
            for b in range(2):
                sp.wait_ge(e_out[b], 16 * NE // 2)
            for tt in range(NT):
                t0, nr = TILES[tt]
                for c in range(2):
                    sp.dma_start(yab[tt][0:nr, c * D:(c + 1) * D], y_d[c * T + t0:c * T + t0 + nr]).then_inc(in_y[tt], 16)
            for tt in range(NT):
                t0, nr = TILES[tt]
                if tt < NT - 1:
                    sp.wait_ge(ln2_out, tt + 1)
                else:
                    sp.wait_ge(ln2_last, 1)
                dst = o["y_prompt"][t0:t0 + nr] if tt < 4 else o["y_sample"]
                sp.dma_start(dst, x1[0:nr, tt, :]).then_inc(out_sem, 16)
            sp.wait_ge(conv_out, 32)
            sp.wait_ge(lat_out, 64)
            sp.wait_ge(mem_out, 32)
            sp.wait_ge(out_sem, 16 * NT)

        @block.tensor
        def _(pe):
            def begin(name):
                n = JOB[name]
                if n >= 4:
                    pe.wait_ge(*read_of(JOBS[n - 4]))

            def item(name):
                i = ITEM[name]
                pe.wait_ge(ring_full[i % RING], 16 * (i // RING + 1))
                return w_item(name)

            def gemm(name, w, rhs, nk, m=128, n=HT, halves=2):
                begin(name)
                for k in range(nk):
                    for s in range(halves):
                        mm = pe.matmul(half(name, s, m, n), w[:, k, :], rhs(k, s), start=(k == 0), stop=(k == nk - 1))
                mm.then_inc(job_done, 1)

            def on(buf):
                return lambda k, s: buf[:, k, HT * s:HT * s + HT]

            def product(name, it, xh, xl, nk, at=0, first=False):
                n = SP_AT[it]
                begin(name)
                pe.wait_ge(w_lo, n + 1)
                for k in range(nk):
                    if first:
                        pe.wait_ge(x_lo, k + 1)
                    for w, x in ((WH, xh), (WH, xl), (WL, xh)):
                        for s in range(2):
                            mm = pe.matmul(half(name, s), w[:, n % 2, at + 128 * k:at + 128 * k + 128], x[:, k, HT * s:HT * s + HT],
                                           start=(k == 0 and w is WH and x is xh), stop=(k == nk - 1 and w is WL))
                mm.then_inc(job_done, 1)

            def proj(name, first=False):
                product(name, name, XH, XL, KT, first=first)

            def total(name, nk, buf):
                begin(name)
                for k in range(nk):
                    for s in range(2):
                        mm = pe.matmul(half(name, s), ones[:, :], buf[:, k, HT * s:HT * s + HT],
                                       start=(k == 0), stop=(k == nk - 1))
                mm.then_inc(job_done, 1)

            for c in range(4):
                proj(f"glu_b{c}", first=(c == 0))
                proj(f"glu_a{c}")
            for name in ("q0", "q1", "q2", "kv0", "kv1"):
                proj(name)
            gemm("kr", item("kr")[:, 0:KT * ROPE].rearrange("p (k m) -> p k m", k=KT), on(x_raw), KT, ROPE)
            pe.wait_ge(const_ready, 6)
            pe.wait_ge(in_mem, 16)

            def mem_key(h):
                w = item(f"mk{h}").rearrange("p (k m) -> p k m", k=KT)
                gemm(f"mk{h}", w, lambda k, s: memT[:, k, :], KT, n=MT, halves=1)

            mem_key(0)
            mem_key(1)
            pe.wait_ge(lat_sq, 3)
            total("q_ss", 3, sq)
            pe.wait_ge(lat_sq, 5)
            total("kv_ss", 2, rp)
            mem_key(2)
            mem_key(3)
            begin("mv0")
            begin("mv1")
            for i in range(4):
                w = item(f"mv_{i}").rearrange("p (k n) -> p k n", k=2)
                for kk in range(2):
                    k = 2 * i + kk
                    for m in range(2):
                        mm = pe.matmul(half(f"mv{m}", 0, 128, 512), memT[:, k, 128 * m:128 * m + 128], w[:, kk, :],
                                       start=(k == 0), stop=(k == KT - 1))
                        if k == KT - 1:
                            mm.then_inc(job_done, 1)
                if i < 3:
                    mm.then_inc(mv_used, 1)
            for h in range(MH):
                proj(f"mq{h}")
            pe.wait_ge(tap_prompt, 4 * CW)
            pe.wait_ge(tap_sample, 4 * CW)
            total("conv_mean", 4, zT)

            def scores(n):
                kind, i, h = UNITS[n]
                t0, nr = TILES[i]
                if n >= 2:
                    pe.wait_ge(exp_done, n - 1)
                out = PS[0:nr, n % 2, :]
                if kind == "mem":
                    mm = pe.matmul(out[:, 0:MT], memq[:, h, t0:t0 + nr], mkT[:, i // 4, h, :], start=True, stop=True)
                elif i < 4:
                    nk = 128 * (i + 1)
                    pe.matmul(out[:, 0:nk], qh[0:QK, h, t0:t0 + nr], kh[0:QK, h, 0:nk], start=True, stop=True)
                    mm = pe.matmul(out[:, nk - CAUSAL:nk], rowmask[0:QK, :], negrow[0:QK, :], start=False, stop=True,
                                   skip_group_check=True)
                else:
                    mm = pe.matmul(out[:, 0:PAST + TS], qh[0:QK, h, t0:t0 + nr], kh[0:QK, h, TP:KEYS], start=True, stop=True)
                mm.then_inc(score_done, 1)

            def turn(n):
                kind, i, h = UNITS[n]
                nr = TILES[i][1]
                pe.wait_ge(exp_done, n + 1)
                if n >= 2:
                    pe.wait_ge(pt_evac, n - 1)
                kts = key_tiles(kind, i)
                for j, (_, c0, nk) in enumerate(kts):
                    mm = pe.transpose(PS[0:nk, 2 + n % 2, 128 * j:128 * j + nr], Pb[0:nr, n % 3, 128 * j:128 * j + nk],
                                      ident[0:nr, 0:nr])
                mm.then_inc(pt_done, 1)

            def values(n):
                kind, i, h = UNITS[n]
                nr = TILES[i][1]
                g = group_of[n]
                pe.wait_ge(pt_evac, n + 1)
                if h == 0 and g >= 2:
                    pe.wait_ge(o_norm, g - 1)
                kts = key_tiles(kind, i)
                w = MD if kind == "mem" else VD
                for j, (kt, _, nk) in enumerate(kts):
                    v = mv[0:nk, i // 4, kt, h * MD:(h + 1) * MD] if kind == "mem" else V[0:nk, kt, h * VD:(h + 1) * VD]
                    mm = pe.matmul(PS[0:nr, 4 + g % 2, h * w:(h + 1) * w], PT[0:nk, n % 3, 128 * j:128 * j + nr], v,
                                   start=(j == 0), stop=(j == len(kts) - 1))
                mm.then_inc(pv_done, 1)

            def turn_out(g):
                nr = TILES[GROUPS[g][1]][1]
                pe.wait_ge(o_norm, g + 1)
                if g >= 2:
                    pe.wait_ge(ot_evac, g - 1)
                for c in range(4):
                    mm = pe.transpose(PS[:, 6 + g % 2, 128 * c:128 * c + nr], osb[0:nr, g % 2, 128 * c:128 * c + 128],
                                      ident[0:nr, 0:nr])
                mm.then_inc(ot_done, 1)

            def attend(first, end):
                for n in range(first, end + 5):
                    if n < end:
                        scores(n)
                    if first <= n - 2 < end:
                        turn(n - 2)
                    if first <= n - 3 < end:
                        values(n - 3)
                    if first <= n - 4 < end and last_of_group[group_of[n - 4]] == n - 4:
                        turn_out(group_of[n - 4])

            def all_read():
                for name in JOBS[now - 4:now]:
                    pe.wait_ge(*read_of(name))

            now = JOB["conv_mean"] + 1
            all_read()
            pe.wait_ge(mem_proj, 10)
            pe.wait_ge(in_cache, 32)
            attend(0, MEM_LAST)
            pe.wait_ge(ot_evac, N_MEM_G)

            pe.wait_ge(qn_ready, 3)
            for i in range(3):
                w = item(f"uq{i}")[:, 0:768].rearrange("p (m k n) -> p m k n", m=2, k=3)
                for m in range(2):
                    gemm(f"un{2 * i + m}" if i < 2 else f"ur{m}", w[:, m], on(qd), 3)
            pe.wait_ge(conv_sq, 4)
            total("conv_var", 4, sq)
            pe.wait_ge(ck_ready, 2)
            pe.wait_ge(in_past, 48)
            w = item("uk").rearrange("p (m k n) -> p m k n", m=4, k=2)
            for m in range(4):
                gemm(f"uk{m}", w[:, m], lambda k, s: ck[:, k, 416 * s:416 * s + 416], 2, n=416)
            w = item("uv").rearrange("p (k n) -> p k n", k=2)
            for kt in range(7):
                begin(f"uv{kt}")
                nk = 128 if kt < 6 else TS
                for k in range(2):
                    mm = pe.matmul(half(f"uv{kt}", 0, nk, 512), ck[:, k, 128 * kt:128 * kt + nk], w[:, k, :],
                                   start=(k == 0), stop=(k == 1))
                mm.then_inc(job_done, 1)
            now = JOB["uv6"] + 1
            all_read()
            pe.wait_ge(qk_ready, 8 + 8 + 7)
            pe.wait_ge(ur_rot, 2)
            pe.wait_ge(kr_copied, 1)
            attend(MEM_LAST, MLA_LAST)
            pe.wait_ge(ot_evac, N_G)

            for j in range(8):
                proj(f"g0_{j}")
                proj(f"g1_{j}")
                pe.wait_ge(z_split, 4)
                product(f"yc_{j}", f"comx_{j}", BH["z"], BL["z"], 4)
                pe.wait_ge(om_split, NT)
                product(f"ym_{j}", f"comx_{j}", BH["om"], BL["om"], 4, at=512)
                proj(f"g2_{j}")
                pe.wait_ge(ox_split, 4)
                product(f"yx_{j}", f"xo_{j}", BH["ox"], BL["ox"], 4)

            def out_proj(tt):
                t0, nr = TILES[tt]
                begin(f"c{tt}")
                for k in range(KT):
                    if tt == 0:
                        pe.wait_ge(merged_lo, k + 1)
                        pe.wait_ge(wout_lo, k + 1)
                    for m, w in ((MERGED_H, WOUT_H), (MERGED_H, WOUT_L), (MERGED_L, WOUT_H)):
                        for s in range(2):
                            mm = pe.matmul(half(f"c{tt}", s, nr, 512), m[:, k, t0:t0 + nr], w[:, k, 512 * s:512 * s + 512],
                                           start=(k == 0 and m is MERGED_H and w is WOUT_H), stop=(k == KT - 1 and m is MERGED_L))
                mm.then_inc(job_done, 1)

            def turn_x1(tt):
                nr = TILES[tt][1]
                begin(f"t{tt}")
                pe.wait_ge(x1_ready, tt + 1)
                for k in range(KT):
                    mm = pe.transpose(PS[:, 2 * (JOB[f"t{tt}"] % 4) + k // 4, 128 * (k % 4):128 * (k % 4) + nr],
                                      x1[0:nr, tt, 128 * k:128 * k + 128], ident[0:nr, 0:nr])
                mm.then_inc(job_done, 1)

            def router(tt):
                nr = TILES[tt][1]
                begin(f"l{tt}")
                pe.wait_ge(x1T_ready, tt + 1)
                for k in range(KT):
                    mm = pe.matmul(half(f"l{tt}", 0, nr, 36), x1T[:, tt % 2, k, 0:nr], wr[:, k, :],
                                   start=(k == 0), stop=(k == KT - 1))
                mm.then_inc(job_done, 1)

            pe.wait_ge(in_route, 32)
            for name in JOBS[JOB["c0"]:JOB["l4"] + 1]:
                {"c": out_proj, "t": turn_x1, "l": router}[name[0]](int(name[1:]))

            pe.wait_ge(mask_ready, 1)
            pe.wait_ge(route_const, 1)
            begin("rank")
            for tt in range(NT):
                for t2 in range(tt + 1):
                    nr = TILES[t2][1]
                    lhs = tri if t2 == tt else onesb
                    mm = pe.matmul(half("rank", 0, 128, 512)[:, 32 * tt:32 * tt + 32], lhs[0:nr, :], maskb[0:nr, t2, :],
                                   start=(t2 == 0), stop=(t2 == tt))
            mm.then_inc(job_done, 1)
            begin("count")
            for tt in range(NT):
                nr = TILES[tt][1]
                mm = pe.matmul(half("count", 0, 128, 32), onesb[0:nr, :], maskb[0:nr, tt, :], start=(tt == 0), stop=(tt == NT - 1))
            mm.then_inc(job_done, 1)
            begin("table")
            for n in range(2 * NT):
                c, tt = divmod(n, NT)
                nr = TILES[tt][1]
                pe.wait_ge(onehot_ready, n + 1)
                mm = pe.matmul(half("table", 0, 128, NCH * NE), slot_row[0:nr, c, tt, :], slot_col[0:nr, c, tt, :],
                               start=(n == 0), stop=(n == 2 * NT - 1))
            mm.then_inc(job_done, 1)
            now = JOB["table"] + 1
            all_read()

            def expert_turn_rows(b):
                for k in range(KT):
                    mm = pe.transpose(PS[:, k // 4, 128 * (k % 4):128 * (k % 4) + CAP],
                                      xg[b][0:CAP, 128 * k:128 * k + 128], ident[0:CAP, 0:CAP])
                return mm

            def expert_hidden(b):
                for k in range(KT):
                    mm = pe.matmul(PS[0:CAP, 2, :].rearrange("p (s f) -> p s f", s=2), xgT[:, k, 0:CAP], w13[b][:, :, k, :],
                                   start=(k == 0), stop=(k == KT - 1))
                return mm

            def expert_turn_hidden():
                for j in range(2):
                    mm = pe.transpose(PS[:, 3, 128 * j:128 * j + CAP], hm[0:CAP, 128 * j:128 * j + 128],
                                      ident[0:CAP, 0:CAP])
                return mm

            def expert_result(b):
                for j in range(2):
                    for s in range(2):
                        mm = pe.matmul(PS[0:CAP, 4 + s, :], hT[:, j, 0:CAP], w2[b][:, j, 512 * s:512 * s + 512],
                                       start=(j == 0), stop=(j == 1))
                return mm

            def expert_result_parts(b, hb):
                for j in range(2):
                    for h, w in ((HTH, W2H[hb]), (HTH, W2L[b]), (HTL, W2H[hb])):
                        for s in range(2):
                            mm = pe.matmul(PS[0:CAP, 4 + s, :], h[:, j, 0:CAP], w[:, j, 512 * s:512 * s + 512],
                                           start=(j == 0 and h is HTH and w is W2H[hb]), stop=(j == 1 and h is HTL))
                return mm

            def rows_step(e, b, k, first=False):
                pe.wait_ge(e_rows[b], 16 * k)
                if not first:
                    pe.wait_ge(e_xgT, e)
                    pe.wait_ge(e_xgT2, e)
                expert_turn_rows(b).then_inc(e_tx, 1)

            def hidden_step(e, b, k, first=False):
                pe.wait_ge(e_xgT, e + 1)
                pe.wait_ge(e_xgT2, e + 1)
                pe.wait_ge(we13[b], 16 * k)
                if not first:
                    pe.wait_ge(e_hm, e)
                expert_hidden(b).then_inc(e_h, 1)

            def hidden_turn_step(e, first=False):
                pe.wait_ge(e_hm, e + 1)
                if not first:
                    pe.wait_ge(e_hTlo, e)
                expert_turn_hidden().then_inc(e_ht, 1)

            def result_step(e, b):
                pe.wait_ge(e_hTlo, e + 1)
                pe.wait_ge(w2_lo, e + 1)
                pe.wait_ge(e_ya, e)
                pe.wait_ge(e_yb, e)
                expert_result_parts(b, b % 2).then_inc(e_y, 1)

            rows_step(0, 0, 1, first=True)
            hidden_step(0, 0, 1, first=True)
            rows_step(1, 1, 1)
            hidden_turn_step(0, first=True)

            def experts(r):
                for i in range(1, NB + 1):
                    e = r * NB + i
                    hidden_step(e, i % NB, r + 1 + i // NB)
                    rows_step(e + 1, (i + 1) % NB, r + 1 + (i + 1) // NB)
                    result_step(e - 1, i - 1)
                    hidden_turn_step(e)

            experts(0)
            with pe.Fori(1, NE // NB - 1) as r:
                experts(r)
            for e in range(NE - NB + 1, NE):
                hidden_step(e, e % NB, NE // NB)
                if e + 1 < NE:
                    rows_step(e + 1, (e + 1) % NB, NE // NB)
                result_step(e - 1, (e - 1) % NB)
                hidden_turn_step(e)
            result_step(NE - 1, NB - 1)

            pe.wait_ge(flag_ready, 1)
            over = pe.value_load(flag[0:1, 0:1], min_val=0, max_val=T)
            with pe.If(over > CAP):
                pe.wait_ge(e_ya, NE)
                pe.wait_ge(e_yb, NE)
                with pe.Fori(0, NE) as e:
                    with pe.Fori(0, NCH - 1) as c:
                        n = e * (NCH - 1) + c
                        pe.wait_ge(ov_w, e * 32 + 32)
                        pe.wait_ge(ov_rows, n * 16 + 16)
                        expert_turn_rows(0).then_inc(ov_tx, 1)
                        pe.wait_ge(ov_xgT, n + 1)
                        expert_hidden(0).then_inc(ov_h, 1)
                        pe.wait_ge(ov_hm, n + 1)
                        expert_turn_hidden().then_inc(ov_ht, 1)
                        pe.wait_ge(ov_hT, n + 1)
                        expert_result(0).then_inc(ov_y, 1)

        @block.scalar
        def _(act):
            chain = [0]

            def link(ins):
                chain[0] += 1
                ins.then_inc(act_chain, 1)
                act.wait_ge(act_chain, chain[0])

            parts = [0]

            def high_parts(upto):
                while parts[0] <= SP_AT[upto]:
                    n = parts[0]
                    i = ITEM[SPLIT[n]]
                    act.wait_ge(ring_full[i % RING], 16 * (i // RING + 1))
                    if n >= 2:
                        wait_job(act, ITEMS[ITEM[SPLIT[n - 2]]][2])
                    size = ITEMS[i][1]
                    act.activation(WH[:, n % 2, 0:size], ring[:, i % RING, 0:size], ACT.Copy).then_inc(w_hi, 1)
                    parts[0] += 1

            high_parts("glu_b0")
            for k in range(KT):
                act.wait_ge(in_x[k // 2], 16)
                act.activation(XH[:, k, :], x_raw[:, k, :], ACT.Copy).then_inc(x_hi, 1)
            for c in range(4):
                high_parts(f"glu_a{c}")
                wait_job(act, f"glu_b{c}")
                act.activation(split(sq[:, c, :]), both(f"glu_b{c}"), ACT.Sigmoid).then_inc(glu_sig, 1)
                high_parts(f"glu_b{c + 1}" if c < 3 else "q0")
                wait_job(act, f"glu_a{c}")
                if c >= 2:
                    act.wait_ge(u_ready, c - 1)
                act.activation(split(rp[:, c % 2, :]), both(f"glu_a{c}"), ACT.Copy).then_inc(glu_raw, 1)
            high_parts("q1")
            act.wait_ge(u_ready, 4)
            for i in range(3):
                high_parts(("q1", "q2", "kv0")[i])
                wait_job(act, f"q{i}")
                act.activation(split(qd[:, i, :]), both(f"q{i}"), ACT.Copy).then_inc(lat_raw, 1)
                act.wait_ge(lat_raw, i + 1)
                act.activation(sq[:, i, :], qd[:, i, :], ACT.Square).then_inc(lat_sq, 1)
            for i in range(2):
                high_parts("kv1")
                wait_job(act, f"kv{i}")
                act.activation(split(kvd[:, i, :]), both(f"kv{i}"), ACT.Copy).then_inc(lat_raw, 1)
                act.wait_ge(lat_raw, i + 4)
                act.activation(rp[:, i, :], kvd[:, i, :], ACT.Square).then_inc(lat_sq, 1)
            act.wait_ge(const_ready, 6)
            wait_job(act, "kr")
            act.activation(split(rp[0:32, 2, :]), both("kr", 32), ACT.Copy).then_inc(kr_raw, 1)

            def key_out(h):
                wait_job(act, f"mk{h}")
                act.activation(mkT[:, 0, h, :], half(f"mk{h}", 0, 128, MT), ACT.Copy).then_inc(mem_proj, 1)

            key_out(0)
            key_out(1)
            wait_job(act, "q_ss")
            act.activation(split(norms[:, 0, :]), both("q_ss"), ACT.Sqrt, bias=eps[:, :], scale=1.0 / QL).then_inc(lat_std, 1)
            wait_job(act, "kv_ss")
            act.activation(split(norms[:, 1, :]), both("kv_ss"), ACT.Sqrt, bias=eps[:, :], scale=1.0 / KVL).then_inc(lat_std, 1)
            key_out(2)
            key_out(3)
            high_parts("mq1")
            for m in range(2):
                wait_job(act, f"mv{m}")
                act.activation(mv[:, 0, m, :], half(f"mv{m}", 0, 128, 512), ACT.Copy).then_inc(mem_proj, 1)
            for h in range(MH):
                high_parts(f"mq{min(h + 1, 3)}")
                if h == MH - 1:
                    act.activation(warm[:, :], eps[:, :], ACT.Exp)
                wait_job(act, f"mq{h}")
                act.activation(split(memq[:, h, :]), both(f"mq{h}"), ACT.Copy, scale=MD ** -0.5).then_inc(mem_proj, 1)

            def attend(first, end):
                for n in range(first, end + 6):
                    if n < end:
                        kind, i, h = UNITS[n]
                        nr = TILES[i][1]
                        nk = sum(k[2] for k in key_tiles(kind, i))
                        g = group_of[n]
                        act.wait_ge(max_done, n + 1)
                        if n >= 3:
                            act.wait_ge(pt_done, n - 2)
                        if h == 0 and g >= 2:
                            act.wait_ge(o_norm, g - 1)
                        act.activation(Pb[0:nr, n % 3, 0:nk], PS[0:nr, n % 2, 0:nk], ACT.Exp, bias=nb[0:nr, n % 8:n % 8 + 1],
                                       accum_out=rs[0:nr, g % 2, h:h + 1]).then_inc(exp_done, 1)
                    if first <= n - 5 < end and last_of_group[group_of[n - 5]] == n - 5:
                        g = group_of[n - 5]
                        kind, i = GROUPS[g]
                        t0, nr = TILES[i]
                        dst = (oxT if kind == "mem" else omT)[:, :, t0:t0 + nr]
                        act.wait_ge(ot_done, g + 1)
                        act.activation(dst, PS[:, 6 + g % 2, :].rearrange("p (c t) -> p c t", c=4)[:, :, 0:nr],
                                       ACT.Copy).then_inc(ot_evac, 1)

            act.wait_ge(conv_out, 32)
            attend(0, MEM_LAST)
            act.wait_ge(conv_cent, 4)
            for c in range(4):
                act.activation(sq[:, c, :], zT[:, c, :], ACT.Square).then_inc(conv_sq, 1)
            act.wait_ge(pv_done, MEM_LAST)
            act.wait_ge(mem_out, 32)
            act.wait_ge(qn_ready, 3)
            act.wait_ge(ck_ready, 2)
            act.wait_ge(krot_ready, 1)
            act.wait_ge(in_past, 48)
            for i in range(4):
                wait_job(act, f"un{i}")
                for s in range(2):
                    act.activation(split(qh[0:64, 2 * i + s, :]), PS[64 * s:64 * s + 64, 2 * (JOB[f"un{i}"] % 4):2 * (JOB[f"un{i}"] % 4) + 2, 0:HT],
                                   ACT.Copy, scale=QK ** -0.5).then_inc(qk_ready, 1)
            for i in range(2):
                wait_job(act, f"ur{i}")
                if i:
                    act.wait_ge(ur_rot, 1)
                act.activation(split(rp[:, 0, :]), both(f"ur{i}"), ACT.Copy, scale=QK ** -0.5).then_inc(ur_raw, 1)
            wait_job(act, "conv_var")
            act.activation(split(cnorm[:, 1, :]), both("conv_var"), ACT.Sqrt, bias=eps[:, :], scale=1.0 / CH).then_inc(conv_std, 1)
            act.activation(warm[:, :], eps[:, :], ACT.Exp)
            for i in range(4):
                wait_job(act, f"uk{i}")
                for s in range(2):
                    act.activation(kh[0:64, 2 * i + s, :].rearrange("p (s t) -> p s t", s=2),
                                   PS[64 * s:64 * s + 64, 2 * (JOB[f"uk{i}"] % 4):2 * (JOB[f"uk{i}"] % 4) + 2, 0:416],
                                   ACT.Copy).then_inc(qk_ready, 1)
            for i in range(7):
                nk = 128 if i < 6 else TS
                wait_job(act, f"uv{i}")
                act.activation(V[0:nk, i, :], half(f"uv{i}", 0, nk, 512), ACT.Copy).then_inc(qk_ready, 1)
            high_parts("g0_0")
            attend(MEM_LAST, MLA_LAST)
            high_parts("g1_0")
            act.wait_ge(in_small, 64)
            act.wait_ge(ur_rot, 2)
            for c in range(4):
                act.wait_ge(conv_norm, c + 1)
                act.activation(zT[:, c, :], zT[:, c, :], ACT.Silu, scale=vec[:, 1, c:c + 1],
                               bias=vec[:, 2, c:c + 1]).then_inc(z_ready, 1)
                act.wait_ge(z_ready, c + 1)
                act.activation(BH["z"][:, c, :], zT[:, c, :], ACT.Copy).then_inc(z_hi, 1)
            for j in range(8):
                for n in range(3):
                    high_parts((f"comx_{j}", f"g2_{j}", f"g0_{j + 1}" if j < 7 else "xo_7")[n])
                    wait_job(act, f"g{n}_{j}")
                    if j >= 2:
                        act.wait_ge(merged_ready, j - 1)
                    act.activation(split(gate[:, j % 2, n, :]), both(f"g{n}_{j}"), ACT.Sigmoid,
                                   bias=bgate[:, 8 * n + j:8 * n + j + 1]).then_inc(gate_sig, 1)

            def merged_high(k):
                act.wait_ge(merged_ready, k + 1)
                act.activation(MERGED_H[:, k, :], merged[:, k, :], ACT.Copy).then_inc(merged_hi, 1)

            def wout_high(k):
                act.activation(WOUT_H[:, k, :], w_out[:, k, :], ACT.Copy).then_inc(wout_hi, 1)

            for k in range(4):
                merged_high(k)
            wait_job(act, "yx_7")
            act.wait_ge(in_wout, 16)
            wout_high(0)
            wout_high(1)
            for k in range(4, KT):
                wout_high(k - 2)
                merged_high(k)
            wout_high(6)
            wout_high(7)
            for tt in range(NT + 1):
                if tt < NT:
                    nr = TILES[tt][1]
                    act.wait_ge(ln1_var, tt + 1)
                    act.activation(rstd[0:nr, tt % 2, 0:1], mva[0:nr, tt % 2, 1:2], ACT.Sqrt, bias=eps[0:nr, :]).then_inc(ln1_std, 1)
                if tt >= 1:
                    u = tt - 1
                    nr = TILES[u][1]
                    wait_job(act, f"t{u}")
                    if u >= 2:
                        wait_job(act, f"l{u - 2}")
                    act.activation(x1T[:, u % 2, :, 0:nr].rearrange("p (s k) t -> p s k t", s=2),
                                   pair(f"t{u}").rearrange("p s (k t) -> p s k t", k=4)[:, :, :, 0:nr], ACT.Copy).then_inc(x1T_ready, 1)
            act.wait_ge(route_dve, 1)
            act.activation(g4[:, 1], g4[:, 0], ACT.Exp).then_inc(route_exp, 1)
            act.wait_ge(route_dve, 2)
            act.activation(gm[:, 5], gm[:, 4], ACT.Exp).then_inc(route_exp, 1)
            act.wait_ge(x1_out, 16 * 2 * NT)
            for tt in range(NT):
                nr = TILES[tt][1]
                act.activation(x1[0:nr, tt, :], x1[0:nr, tt, :], ACT.Copy, scale=ALPHA).then_inc(x1_scaled, 1)

            def evac_rows(half_no):
                src = PS[:, half_no, :].rearrange("p (k t) -> p k t", k=4)[:, :, 0:CAP]
                return act.activation(xgT[:, 4 * half_no:4 * half_no + 4, 0:CAP], src, ACT.Copy)

            def silu():
                return act.activation(hg[0:CAP, :], PS[0:CAP, 2, 0:FE], ACT.Silu)

            def evac_hidden():
                return act.activation(hT[:, :, 0:CAP], PS[:, 3, 0:256].rearrange("p (j t) -> p j t", j=2)[:, :, 0:CAP], ACT.Copy)

            def evac_result(b, s):
                return act.activation(ysb[0:CAP, b, 512 * s:512 * s + 512], PS[0:CAP, 4 + s, :], ACT.Copy)

            def rows_step(e):
                act.wait_ge(e_tx, e + 1)
                act.wait_ge(e_h, e)
                evac_rows(0).then_inc(e_xgT, 1)

            def silu_step(e):
                act.wait_ge(e_h, e + 1)
                act.wait_ge(e_hm, e)
                silu().then_inc(e_silu, 1)

            def hidden_turn_step(e):
                act.wait_ge(e_ht, e + 1)
                act.wait_ge(e_y, e)
                act.activation(HTH[:, :, 0:CAP], PS[:, 3, 0:256].rearrange("p (j t) -> p j t", j=2)[:, :, 0:CAP],
                               ACT.Copy).then_inc(e_hT, 1)

            def result_step(e, b, k):
                act.wait_ge(e_y, e + 1)
                act.wait_ge(e_out[b], 16 * k)
                evac_result(b, 0).then_inc(e_ya, 1)

            def w2_high(e, b, k, first=False):
                act.wait_ge(we2[b], 16 * k)
                if not first:
                    act.wait_ge(e_y, e - 1)
                act.activation(W2H[b % 2][:, :, :], w2[b], ACT.Copy).then_inc(w2_hi, 1)

            w2_high(0, 0, 1, first=True)
            w2_high(1, 1, 1, first=True)
            rows_step(0)
            silu_step(0)
            rows_step(1)
            hidden_turn_step(0)

            def experts(r):
                for i in range(1, NB + 1):
                    e = r * NB + i
                    silu_step(e)
                    rows_step(e + 1)
                    result_step(e - 1, (i - 1) % 2, r * (NB // 2) + (i - 1) // 2)
                    hidden_turn_step(e)
                    w2_high(e + 1, (i + 1) % NB, r + 1 + (i + 1) // NB)

            experts(0)
            with act.Fori(1, NE // NB - 1) as r:
                experts(r)
            for e in range(NE - NB + 1, NE):
                silu_step(e)
                if e + 1 < NE:
                    rows_step(e + 1)
                result_step(e - 1, (e - 1) % 2, (e - 1) // 2)
                hidden_turn_step(e)
                if e + 1 < NE:
                    w2_high(e + 1, (e + 1) % NB, NE // NB)
            result_step(NE - 1, 1, NE // 2 - 1)
            act.wait_ge(flag_ready, 1)
            over = act.value_load(flag[0:1, 0:1], min_val=0, max_val=T)
            with act.If(over > CAP):
                with act.Fori(0, NE * (NCH - 1)) as n:
                    act.wait_ge(ov_tx, n + 1)
                    evac_rows(0)
                    evac_rows(1).then_inc(ov_xgT, 1)
                    act.wait_ge(ov_h, n + 1)
                    silu().then_inc(ov_silu, 1)
                    act.wait_ge(ov_ht, n + 1)
                    evac_hidden().then_inc(ov_hT, 1)
                    act.wait_ge(ov_y, n + 1)
                    evac_result(0, 0)
                    evac_result(0, 1).then_inc(ov_ysb, 1)
            for tt in range(NT + 1):
                if tt < NT:
                    nr = TILES[tt][1]
                    act.wait_ge(ln2_var, tt + 1)
                    act.activation(rstd[0:nr, tt % 2, 0:1], mva[0:nr, tt % 2, 1:2], ACT.Sqrt, bias=eps[0:nr, :]).then_inc(ln2_std, 1)
                if tt >= 1:
                    u, b = tt - 1, (tt - 1) % 2
                    nr = TILES[u][1]
                    act.wait_ge(ln2_scales, u + 1)
                    act.activation(x1[0:nr, u, :], x1[0:nr, u, :], ACT.Identity, scale=rstd[0:nr, b, 1:2],
                                   bias=rstd[0:nr, b, 2:3]).then_inc(ln2_hat, 1)

        @block.vector
        def _(dve):
            chain = [0]

            def link(ins):
                chain[0] += 1
                ins.then_inc(dve_chain, 1)
                dve.wait_ge(dve_chain, chain[0])

            for k in range(KT):
                dve.wait_ge(x_hi, k + 1)
                dve.tensor_tensor(XL[:, k, :], x_raw[:, k, :], XH[:, k, :].bitcast(F32), ALU.subtract).then_inc(x_lo, 1)
            dve.wait_ge(in_conv, 32)
            dve.wait_ge(in_small, 64)
            dve.wait_ge(const_ready, 6)
            for c in range(4):
                dve.wait_ge(u_ready, c + 1)
                for j in range(CW):
                    parts = ((zT[:, c, 0:TP], U[:, c, j:j + TP], tap_prompt),
                             (zT[:, c, TP:T], U[:, c, PAD + TP + j:PAD + TP + j + TS], tap_sample))
                    for dst, src, tap in parts:
                        if j == 0:
                            ins = dve.tensor_scalar(dst, src, wdw[:, c, 0:1], vec[:, 0, c:c + 1], ALU.mult, ALU.add)
                        else:
                            dve.wait_ge(tap, c * CW + j)
                            ins = dve.scalar_tensor_tensor(dst, src, wdw[:, c, j:j + 1], dst, ALU.mult, ALU.add)
                        ins.then_inc(tap, 1)

            dve.wait_ge(lat_std, 1)
            link(dve.reciprocal(norms[:, 0, :], norms[:, 0, :]))
            dve.wait_ge(lat_raw, 5)
            for i in range(3):
                dve.scalar_tensor_tensor(qd[:, i, :], qd[:, i, :], gqa[:, i:i + 1], norms[:, 0, :], ALU.mult,
                                         ALU.mult).then_inc(qn_ready, 1)
            dve.wait_ge(lat_std, 2)
            link(dve.reciprocal(norms[:, 1, :], norms[:, 1, :]))
            for i in range(2):
                dve.scalar_tensor_tensor(ck[:, i, 0:TP], kvd[:, i, 0:TP], gkva[:, i:i + 1], norms[:, 1, 0:TP], ALU.mult, ALU.mult)
                dve.scalar_tensor_tensor(ck[:, i, TP + PAST:KEYS], kvd[:, i, TP:T], gkva[:, i:i + 1], norms[:, 1, TP:T],
                                         ALU.mult, ALU.mult).then_inc(ck_ready, 1)
            swap = list(range(16, 32)) + list(range(16))
            dve.wait_ge(kr_raw, 1)
            dve.wait_ge(in_rope, 32)
            wait_job(dve, "kv_ss")
            link(dve.stream_shuffle(rp[0:32, 1, :], rp[0:32, 2, :], swap))
            dve.tensor_tensor(rp[0:32, 2, :], rp[0:32, 2, :], cos[0:32, :], ALU.mult)
            link(dve.tensor_tensor(rp[0:32, 1, :], rp[0:32, 1, :], sin[0:32, :], ALU.mult))
            dve.tensor_tensor(krot[:, 0:TP], rp[0:32, 2, 0:TP], rp[0:32, 1, 0:TP], ALU.add)
            dve.tensor_tensor(krot[:, TP + PAST:KEYS], rp[0:32, 2, TP:T], rp[0:32, 1, TP:T], ALU.add).then_inc(krot_ready, 1)

            wait_job(dve, "conv_mean")
            dve.tensor_scalar(split(cnorm[:, 0, :]), both("conv_mean"), 1.0 / CH, None, ALU.mult).then_inc(mean_read, 1)

            def row_max(n):
                kind, i, h = UNITS[n]
                nr = TILES[i][1]
                nk = sum(k[2] for k in key_tiles(kind, i))
                dve.wait_ge(score_done, n + 1)
                if n >= 8:
                    dve.wait_ge(exp_done, n - 7)
                dve.tensor_reduce(nb[0:nr, n % 8:n % 8 + 1], PS[0:nr, n % 2, 0:nk], AX.X, ALU.max, negate=True).then_inc(max_done, 1)

            def evac_probs(n):
                kind, i, h = UNITS[n]
                nr = TILES[i][1]
                kts = key_tiles(kind, i)
                dve.wait_ge(pt_done, n + 1)
                if n >= 3:
                    dve.wait_ge(pv_done, n - 2)
                full = len([k for k in kts if k[2] == 128])
                src = PS[:, 2 + n % 2, :].rearrange("p (k t) -> p k t", k=4)
                dst = PT[:, n % 3, :].rearrange("p (k t) -> p k t", k=4)
                ins = dve.tensor_copy(dst[:, 0:full, 0:nr], src[:, 0:full, 0:nr])
                if full < len(kts):
                    ins = dve.tensor_copy(dst[0:TS, full, 0:nr], src[0:TS, full, 0:nr])
                ins.then_inc(pt_evac, 1)

            def normalise(g):
                kind, i = GROUPS[g]
                nr = TILES[i][1]
                heads, w = (MH, MD) if kind == "mem" else (NH, VD)
                dve.wait_ge(exp_done, last_of_group[g] + 1)
                link(dve.reciprocal(rinv[0:nr, g % 2, 0:heads], rs[0:nr, g % 2, 0:heads]))
                dve.wait_ge(pv_done, last_of_group[g] + 1)
                if g >= 2:
                    dve.wait_ge(ot_done, g - 1)
                dve.tensor_tensor(osb[0:nr, g % 2, :].rearrange("p (h v) -> p h v", h=heads),
                                  PS[0:nr, 4 + g % 2, :].rearrange("p (h v) -> p h v", h=heads),
                                  rinv[0:nr, g % 2, 0:heads].unsqueeze(2).to_broadcast([nr, heads, w]), ALU.mult).then_inc(o_norm, 1)

            def attend(first, end):
                for n in range(first, end + 4):
                    if n < end:
                        row_max(n)
                    if first <= n - 2 < end:
                        evac_probs(n - 2)
                    if first <= n - 3 < end and last_of_group[group_of[n - 3]] == n - 3:
                        normalise(group_of[n - 3])

            attend(0, MEM_LAST)
            dve.wait_ge(mean_read, 1)
            for c in range(4):
                dve.tensor_tensor(zT[:, c, :], zT[:, c, :], cnorm[:, 0, :], ALU.subtract).then_inc(conv_cent, 1)
            dve.wait_ge(pv_done, MEM_LAST)
            dve.wait_ge(mem_out, 32)
            dve.wait_ge(in_past, 48)
            dve.tensor_copy(kh[64:96, :, :], krot.unsqueeze(1).to_broadcast([32, NH, KEYS])).then_inc(kr_copied, 1)
            for i in range(2):
                dve.wait_ge(ur_raw, i + 1)
                link(dve.stream_shuffle(rp[:, 1, :], rp[:, 0, :], swap))
                dve.tensor_tensor(rp[:, 0, :], rp[:, 0, :], cos, ALU.mult)
                link(dve.tensor_tensor(rp[:, 1, :], rp[:, 1, :], sin, ALU.mult))
                for q in range(4):
                    ins = dve.tensor_tensor(qh[64:96, 4 * i + q, :], rp[32 * q:32 * q + 32, 0, :], rp[32 * q:32 * q + 32, 1, :], ALU.add)
                ins.then_inc(ur_rot, 1)
            dve.wait_ge(conv_std, 1)
            link(dve.reciprocal(cnorm[:, 1, :], cnorm[:, 1, :]))
            for c in range(4):
                dve.tensor_tensor(zT[:, c, :], zT[:, c, :], cnorm[:, 1, :], ALU.mult).then_inc(conv_norm, 1)
            attend(MEM_LAST, MLA_LAST)
            for c in range(4):
                dve.wait_ge(z_hi, c + 1)
                dve.tensor_tensor(BL["z"][:, c, :], zT[:, c, :], BH["z"][:, c, :].bitcast(F32), ALU.subtract).then_inc(z_split, 1)

            for j in range(8):
                for n, name in enumerate(("yc", "ym", "yx")):
                    if name == "yx" and j < 7:
                        low_part(dve, SP_AT[f"g0_{j + 1}"])
                    wait_job(dve, f"{name}_{j}")
                    dve.wait_ge(gate_sig, 3 * j + n + 1)
                    dve.tensor_tensor(split(gate[:, j % 2, n, :]), split(gate[:, j % 2, n, :]), both(f"{name}_{j}"),
                                      ALU.mult).then_inc(gate_mul, 1)

            for k in range(KT):
                dve.wait_ge(wout_hi, k + 1)
                dve.tensor_tensor(WOUT_L[:, k, :], w_out[:, k, :], WOUT_H[:, k, :].bitcast(F32), ALU.subtract).then_inc(wout_lo, 1)
            link(dve.memset(lg[:, :, :], 0.0))
            for tt in range(NT + 2):
                if tt < NT:
                    t0, nr = TILES[tt]
                    wait_job(dve, f"c{tt}")
                    dve.wait_ge(in_xtok[tt % 2], 16 * (tt // 2 + 1))
                    dve.scalar_tensor_tensor(x1[0:nr, tt, :].rearrange("p (s d) -> p s d", s=2),
                                             xtok[0:nr, tt % 2, :].rearrange("p (s d) -> p s d", s=2), ALPHA,
                                             pair(f"c{tt}")[0:nr], ALU.mult, ALU.add).then_inc(ln1_res, 1)
                    dve.wait_ge(ln1_res, tt + 1)
                    dve.bn_stats(st[0:nr, tt % 2, 0, :], x1[0:nr, tt, 0:512])
                    link(dve.bn_stats(st[0:nr, tt % 2, 1, :], x1[0:nr, tt, 512:1024]))
                    dve.bn_aggr(mva[0:nr, tt % 2, :], st[0:nr, tt % 2, :, :].rearrange("p a b -> p (a b)")).then_inc(ln1_var, 1)
                    dve.wait_ge(ln1_std, tt + 1)
                    link(dve.reciprocal(rstd[0:nr, tt % 2, 1:2], rstd[0:nr, tt % 2, 0:1]))
                    dve.tensor_scalar(x1[0:nr, tt, :], x1[0:nr, tt, :], mva[0:nr, tt % 2, 0:1], rstd[0:nr, tt % 2, 1:2],
                                      ALU.subtract, ALU.mult).then_inc(ln1_hat, 1)
                if tt >= 2:
                    u = tt - 2
                    nr = TILES[u][1]
                    wait_job(dve, f"l{u}")
                    dve.tensor_tensor(lg[0:nr, u, :], half(f"l{u}", 0, nr, 36), rbias[0:nr, :], ALU.add).then_inc(lg_ready, 1)

            def wide(x, n):
                return x.unsqueeze(2).to_broadcast([128, NT, n])

            def first_max(x, n, m, cand, onehot):
                link(dve.tensor_reduce(gm[:, m], x, AX.X, ALU.max))
                link(dve.tensor_tensor(cand, x, wide(gm[:, m], n), ALU.is_equal))
                link(dve.tensor_tensor(cand, cand, desc[:, NE_G - n:].unsqueeze(1).to_broadcast([128, NT, n]), ALU.mult))
                link(dve.tensor_reduce(gm[:, 11], cand, AX.X, ALU.max))
                link(dve.tensor_tensor(onehot, cand, wide(gm[:, 11], n), ALU.is_equal))

            dve.wait_ge(lg_ready, NT)
            dve.wait_ge(route_const, 1)
            first_max(lg[:, :, 0:NG], NG, 0, g4[:, 0], g4[:, 2])
            dve.tensor_tensor(g4[:, 0], lg[:, :, 0:NG], wide(gm[:, 0], NG), ALU.subtract).then_inc(route_dve, 1)
            prod = e32[:, 3].rearrange("p t (g e) -> p t g e", g=NG)
            for g in range(NG):
                ins = dve.tensor_tensor(prod[:, :, g, :], lg[:, :, NG + 8 * g:NG + 8 * g + 8],
                                        wide(g4[:, 2, :, g], NE_G), ALU.mult)
            link(ins)
            link(dve.tensor_reduce(e8[:, 0], prod.rearrange("p t g e -> p t e g"), AX.X, ALU.add))
            first_max(e8[:, 0], NE_G, 1, e8[:, 1], e8[:, 2])
            link(dve.scalar_tensor_tensor(e8[:, 0], e8[:, 2], -1e30, e8[:, 0], ALU.mult, ALU.add))
            first_max(e8[:, 0], NE_G, 2, e8[:, 1], e8[:, 3])
            dve.tensor_tensor(gm[:, 4], gm[:, 2], gm[:, 1], ALU.subtract).then_inc(route_dve, 1)
            for c in range(2):
                hot = e32[:, c].rearrange("p t (g e) -> p t g e", g=NG)
                for g in range(NG):
                    ins = dve.tensor_tensor(hot[:, :, g, :], e8[:, 2 + c], wide(g4[:, 2, :, g], NE_G), ALU.mult)
            link(ins)
            dve.tensor_tensor(maskb[:, :, :], e32[:, 0], e32[:, 1], ALU.add).then_inc(mask_ready, 1)
            def flat(x):
                return x.rearrange("p c t -> p (c t)")

            hot, tmp = e32[:, 0:2], e32[:, 2:4]
            link(dve.tensor_tensor(tmp.rearrange("p c t e -> p (c t) e"), hot.rearrange("p c t e -> p (c t) e"),
                                   iota[:, 0:NE].unsqueeze(1).to_broadcast([128, 2 * NT, NE]), ALU.mult))
            link(dve.tensor_reduce(flat(gm[:, 2:4]), tmp.rearrange("p c t e -> p (c t) e"), AX.X, ALU.add))
            wait_job(dve, "count")
            link(dve.tensor_tensor(tmp.rearrange("p c t e -> p c (t e)"), hot.rearrange("p c t e -> p c (t e)"),
                                   half("rank", 0, 128, 160).unsqueeze(1).to_broadcast([128, 2, 160]), ALU.mult))
            link(dve.tensor_reduce(flat(gm[:, 8:10]), tmp.rearrange("p c t e -> p (c t) e"), AX.X, ALU.add))
            link(dve.tensor_scalar(gm[:, 10:12], gm[:, 8:10], float(CAP), None, ALU.is_ge))
            for k in range(2, NCH):
                link(dve.scalar_tensor_tensor(gm[:, 10:12], gm[:, 8:10], float(k * CAP), gm[:, 10:12], ALU.is_ge, ALU.add))
            dve.scalar_tensor_tensor(slot[:, 0], gm[:, 10:12], -float(CAP), gm[:, 8:10], ALU.mult, ALU.add).then_inc(slot_ready, 1)
            dve.scalar_tensor_tensor(slot[:, 1], gm[:, 10:12], float(NE), gm[:, 2:4], ALU.mult, ALU.add).then_inc(slot_ready, 1)
            dve.wait_ge(slot_ready, 2)
            for c in range(2):
                for tt in range(NT):
                    nr = TILES[tt][1]
                    dve.tensor_scalar(slot_row[0:nr, c, tt, :], iota[0:nr, 0:128], slot[0:nr, 0, c, tt:tt + 1], None, ALU.is_equal)
                    dve.tensor_scalar(slot_col[0:nr, c, tt, :], iota[0:nr, :], slot[0:nr, 1, c, tt:tt + 1],
                                      rowid[0:nr, c, tt:tt + 1], ALU.is_equal, ALU.mult).then_inc(onehot_ready, 1)
            wait_job(dve, "table")
            link(dve.tensor_scalar(empty[:, :], half("table", 0, 128, NCH * NE), 0.0, float(SKIP), ALU.is_equal, ALU.mult))
            dve.scalar_tensor_tensor(tabs[:, :], half("table", 0, 128, NCH * NE), -1.0, empty[:, :], ALU.add,
                                     ALU.add).then_inc(tab_ready, 1)
            dve.tensor_reduce(flag[:, :], half("count", 0, 128, NE), AX.X, ALU.max).then_inc(flag_ready, 1)
            dve.wait_ge(flag_ready, 1)
            dve.wait_ge(route_exp, 2)
            link(dve.tensor_reduce(gm[:, 6], g4[:, 1], AX.X, ALU.add))
            dve.reciprocal(gm[:, 6], gm[:, 6])
            link(dve.tensor_scalar(gm[:, 7], gm[:, 5], 1.0, None, ALU.add))
            link(dve.reciprocal(gm[:, 7], gm[:, 7]))
            link(dve.tensor_tensor(wsel[:, 0, :], gm[:, 6], gm[:, 7], ALU.mult))
            dve.tensor_tensor(wsel[:, 1, :], wsel[:, 0, :], gm[:, 5], ALU.mult)

            def evac_rows():
                return dve.tensor_copy(xgT[:, 4:8, 0:CAP], PS[:, 1, :].rearrange("p (k t) -> p k t", k=4)[:, :, 0:CAP])

            def hidden():
                return dve.tensor_tensor(hm[0:CAP, :], hg[0:CAP, :], PS[0:CAP, 2, FE:2 * FE], ALU.mult)

            def rows_step(e):
                dve.wait_ge(e_tx, e + 1)
                dve.wait_ge(e_h, e)
                evac_rows().then_inc(e_xgT2, 1)

            def hidden_step(e):
                dve.wait_ge(e_silu, e + 1)
                dve.wait_ge(e_ht, e)
                hidden().then_inc(e_hm, 1)

            def result_step(e, b, k):
                dve.wait_ge(e_y, e + 1)
                dve.wait_ge(e_out[b], 16 * k)
                dve.tensor_copy(ysb[0:CAP, b, 512:1024], PS[0:CAP, 5, :]).then_inc(e_yb, 1)

            def hidden_low(e):
                dve.wait_ge(e_hT, e + 1)
                dve.tensor_tensor(HTL[:, :, 0:CAP], PS[:, 3, 0:256].rearrange("p (j t) -> p j t", j=2)[:, :, 0:CAP],
                                  HTH[:, :, 0:CAP].bitcast(F32), ALU.subtract).then_inc(e_hTlo, 1)

            def w2_low(e, b):
                dve.wait_ge(w2_hi, e + 1)
                dve.tensor_tensor(W2L[b][:, :, :], w2[b], W2H[b % 2][:, :, :].bitcast(F32), ALU.subtract).then_inc(w2_lo, 1)

            w2_low(0, 0)
            rows_step(0)
            hidden_step(0)
            rows_step(1)
            hidden_low(0)
            w2_low(1, 1)

            def experts(r):
                for i in range(1, NB + 1):
                    e = r * NB + i
                    hidden_step(e)
                    rows_step(e + 1)
                    result_step(e - 1, (i - 1) % 2, r * (NB // 2) + (i - 1) // 2)
                    hidden_low(e)
                    w2_low(e + 1, (i + 1) % NB)

            experts(0)
            with dve.Fori(1, NE // NB - 1) as r:
                experts(r)
            for e in range(NE - NB + 1, NE):
                hidden_step(e)
                if e + 1 < NE:
                    rows_step(e + 1)
                result_step(e - 1, (e - 1) % 2, (e - 1) // 2)
                hidden_low(e)
                if e + 1 < NE:
                    w2_low(e + 1, (e + 1) % NB)
            result_step(NE - 1, 1, NE // 2 - 1)
            over = dve.value_load(flag[0:1, 0:1], min_val=0, max_val=T)
            with dve.If(over > CAP):
                with dve.Fori(0, NE * (NCH - 1)) as n:
                    dve.wait_ge(ov_silu, n + 1)
                    hidden().then_inc(ov_hm, 1)

            dve.wait_ge(x1_scaled, NT)
            for tt in range(NT + 1):
                if tt < NT:
                    nr = TILES[tt][1]
                    dve.wait_ge(in_y[tt], 32)
                    for c in range(2):
                        link(dve.scalar_tensor_tensor(x1[0:nr, tt, :], yab[tt][0:nr, c * D:(c + 1) * D], wsel[0:nr, c, tt:tt + 1],
                                                      x1[0:nr, tt, :], ALU.mult, ALU.add))
                    dve.bn_stats(st[0:nr, tt % 2, 0, :], x1[0:nr, tt, 0:512])
                    link(dve.bn_stats(st[0:nr, tt % 2, 1, :], x1[0:nr, tt, 512:1024]))
                    dve.bn_aggr(mva[0:nr, tt % 2, :], st[0:nr, tt % 2, :, :].rearrange("p a b -> p (a b)")).then_inc(ln2_var, 1)
                if tt >= 1:
                    u, b = tt - 1, (tt - 1) % 2
                    nr = TILES[u][1]
                    dve.wait_ge(ln2_std, u + 1)
                    if u >= 2:
                        dve.wait_ge(ln2_hat, u - 1)
                    link(dve.reciprocal(rstd[0:nr, b, 1:2], rstd[0:nr, b, 0:1]))
                    dve.scalar_tensor_tensor(rstd[0:nr, b, 2:3], mva[0:nr, b, 0:1], -1.0, rstd[0:nr, b, 1:2],
                                             ALU.mult, ALU.mult).then_inc(ln2_scales, 1)
            for u in range(GAIN_BY_DVE, NT):
                nr = TILES[u][1]
                dve.wait_ge(ln2_hat, u + 1)
                dve.tensor_tensor(x1[0:nr, u, :], x1[0:nr, u, :], lnbc[0:nr, 2, :], ALU.mult).then_inc(ln2_gain, 1)
            dve.wait_ge(ln2_gain, NT - GAIN_BY_DVE)
            dve.tensor_tensor(x1[0:nr, u, :], x1[0:nr, u, :], lnbc[0:nr, 3, :], ALU.add).then_inc(ln2_last, 1)

        @block.gpsimd
        def _(pool):
            chain = [0]

            def link(ins):
                chain[0] += 1
                ins.then_inc(pool_chain, 1)
                pool.wait_ge(pool_chain, chain[0])

            pool.memset(ones[:, :], 1.0).then_inc(const_ready, 1)
            pool.memset(eps[:, :], EPS).then_inc(const_ready, 1)
            pool.memset(U[:, :, 0:PAD], 0.0).then_inc(const_ready, 1)
            parts = [0]

            def low_parts(upto):
                while parts[0] <= SP_AT[upto]:
                    if parts[0] not in LOW_BY_DVE:
                        low_part(pool, parts[0])
                    parts[0] += 1

            low_parts("glu_b0")
            pool.memset(ident[:, :], 0.0)
            pool.memset(rowmask[:, :], 0.0)
            link(pool.memset(negrow[:, :], 0.0))
            pool.affine_select(out=ident[:, :], in_=ident[:, :], compare_op=ALU.not_equal, fill=1.0, base=0,
                               pattern=[[-1, 128]], channel_multiplier=1).then_inc(const_ready, 1)
            pool.memset(rowmask[0:1, 0:CAUSAL], 1.0).then_inc(const_ready, 1)
            pool.memset(negrow[0:1, :], -1e30).then_inc(const_ready, 1)
            pool.memset(onesb[:, :], 1.0)
            link(pool.memset(tri[:, :], 1.0))
            pool.affine_select(out=tri[:, :], in_=tri[:, :], compare_op=ALU.is_gt, fill=0.0, base=0,
                               pattern=[[1, 128]], channel_multiplier=-1)
            for i in range(NE_G):
                pool.memset(desc[:, i:i + 1], float(NE_G - i))
            pool.iota(iota_i[:, :], pattern=[[1, NCH * NE]], base=0, channel_multiplier=0)
            pool.iota(rowid_i[:, 0, :], pattern=[[128, NT]], base=1, channel_multiplier=1)
            link(pool.iota(rowid_i[:, 1, :], pattern=[[128, NT]], base=T + 1, channel_multiplier=1))
            pool.tensor_copy(iota[:, :], iota_i[:, :])
            pool.tensor_copy(rowid[:, :, :], rowid_i[:, :, :]).then_inc(route_const, 1)

            for c in range(4):
                low_parts(f"glu_a{c + 1}" if c < 3 else "q1")
                pool.wait_ge(glu_raw, c + 1)
                pool.tensor_tensor(U[:, c, PAD:PAD + TP], rp[:, c % 2, 0:TP], sq[:, c, 0:TP], ALU.mult)
                pool.tensor_tensor(U[:, c, 2 * PAD + TP:UW], rp[:, c % 2, TP:T], sq[:, c, TP:T], ALU.mult).then_inc(u_ready, 1)
            low_parts("mq3")
            pool.wait_ge(u_ready, 4)
            pool.dma_start(o["conv_prompt_T"], U[:, :, TP:TP + PAD]).then_inc(conv_out, 16)
            pool.dma_start(o["conv_sample_T"], U[:, :, UW - PAD:UW]).then_inc(conv_out, 16)
            pool.wait_ge(ck_ready, 2)
            pool.dma_start(o["latent_T"][:, :, 0:TP], ck[:, :, 0:TP]).then_inc(lat_out, 16)
            pool.dma_start(o["latent_T"][:, :, TP:T], ck[:, :, TP + PAST:KEYS]).then_inc(lat_out, 16)
            pool.wait_ge(krot_ready, 1)
            pool.dma_start(o["krope_T"][:, 0:TP], krot[:, 0:TP]).then_inc(lat_out, 16)
            pool.dma_start(o["krope_T"][:, TP:T], krot[:, TP + PAST:KEYS]).then_inc(lat_out, 16)
            pool.wait_ge(mem_proj, 6)
            pool.dma_start(o["mem_k_T"], mkT[:, 0]).then_inc(mem_out, 16)
            pool.dma_start(o["mem_v"], mv[:, 0]).then_inc(mem_out, 16)
            low_parts("g0_0")

            def split_branch(name, c, t0, nr, done):
                high_count[0] += 1
                hi = BH[name][:, c, t0:t0 + nr]
                pool.tensor_copy(hi, branch[name][:, c, t0:t0 + nr]).then_inc(branch_hi, 1)
                pool.wait_ge(branch_hi, high_count[0])
                pool.tensor_tensor(BL[name][:, c, t0:t0 + nr], branch[name][:, c, t0:t0 + nr], hi.bitcast(F32),
                                   ALU.subtract).then_inc(done, 1)

            high_count = [0]
            pool.wait_ge(qk_ready, 8 + 8 + 7)
            pool.wait_ge(kr_copied, 1)
            pool.wait_ge(ur_rot, 2)
            pool.wait_ge(lat_out, 64)
            pool.wait_ge(conv_norm, 4)
            pool.wait_ge(ot_evac, N_MEM_G)
            for c in range(4):
                split_branch("ox", c, 0, T, ox_split)
            for i in range(NT):
                pool.wait_ge(ot_evac, N_MEM_G + i + 1)
                split_branch("om", slice(0, 4), *TILES[i], om_split)
            for j in range(8):
                low_parts(f"xo_{j}")
                pool.wait_ge(gate_mul, 3 * j + 2)
                link(pool.tensor_tensor(gate[:, j % 2, 0, :], gate[:, j % 2, 0, :], gate[:, j % 2, 1, :], ALU.add))
                if j < 7:
                    low_parts(f"g1_{j + 1}")
                pool.wait_ge(gate_mul, 3 * j + 3)
                pool.tensor_tensor(merged[:, j, :], gate[:, j % 2, 0, :], gate[:, j % 2, 2, :], ALU.add).then_inc(merged_ready, 1)
            for k in range(KT):
                pool.wait_ge(merged_hi, k + 1)
                pool.tensor_tensor(MERGED_L[:, k, :], merged[:, k, :], MERGED_H[:, k, :].bitcast(F32), ALU.subtract).then_inc(merged_lo, 1)
            pool.wait_ge(in_ln, 64)
            for tt in range(NT):
                nr = TILES[tt][1]
                pool.wait_ge(ln1_hat, tt + 1)
                link(pool.tensor_tensor(x1[0:nr, tt, :], x1[0:nr, tt, :], lnbc[0:nr, 0, :], ALU.mult))
                pool.tensor_tensor(x1[0:nr, tt, :], x1[0:nr, tt, :], lnbc[0:nr, 1, :], ALU.add).then_inc(x1_ready, 1)

            for b in range(NB):
                ins = pool.memset(xg[b], 0.0)
            link(ins)
            pool.wait_ge(x1_out, 16 * 2 * NT)
            pool.wait_ge(tab_ready, 1)

            def gather(b, col):
                return pool.indirect_dma_start(xg[b][0:CAP, :], None, x1_d,
                                               bass.IndirectOffsetOnAxis(ap=tabs[0:CAP, col:col + 1], axis=0),
                                               bounds_check=2 * T - 1, oob_is_err=False)

            def scatter(b, col):
                return pool.indirect_dma_start(y_d, bass.IndirectOffsetOnAxis(ap=tabs[0:CAP, col:col + 1], axis=0),
                                               ysb[0:CAP, b, :], None, bounds_check=2 * T - 1, oob_is_err=False)

            for e in range(NB):
                gather(e, e).then_inc(e_rows[e], 16)
            for e in range(NE):
                if e + NB < NE:
                    pool.wait_ge(e_tx, e + 1)
                    gather(e % NB, e + NB).then_inc(e_rows[e % NB], 16)
                pool.wait_ge(e_ya, e + 1)
                pool.wait_ge(e_yb, e + 1)
                scatter(e % 2, e).then_inc(e_out[e % 2], 16)
            pool.wait_ge(flag_ready, 1)
            over = pool.value_load(flag[0:1, 0:1], min_val=0, max_val=T)
            with pool.If(over > CAP):
                for b in range(2):
                    pool.wait_ge(e_out[b], 16 * NE // 2)
                for e in range(NE):
                    for c in range(1, NCH):
                        n = e * (NCH - 1) + c - 1
                        gather(0, c * NE + e).then_inc(ov_rows, 16)
                        pool.wait_ge(ov_ysb, n + 1)
                        scatter(0, c * NE + e).then_inc(ov_out, 16)
                        pool.wait_ge(ov_out, 16 * (n + 1))
            for tt in range(NT - 1):
                nr = TILES[tt][1]
                if tt < GAIN_BY_DVE:
                    pool.wait_ge(ln2_hat, tt + 1)
                    link(pool.tensor_tensor(x1[0:nr, tt, :], x1[0:nr, tt, :], lnbc[0:nr, 2, :], ALU.mult))
                else:
                    pool.wait_ge(ln2_gain, tt - GAIN_BY_DVE + 1)
                pool.tensor_tensor(x1[0:nr, tt, :], x1[0:nr, tt, :], lnbc[0:nr, 3, :], ALU.add).then_inc(ln2_out, 1)



def lay_out(x):
    def m_tiles(w):
        K, M = w.shape
        return w.reshape(K // 128, 128, M // 128, 128).transpose(2, 1, 0, 3).reshape(M // 128, 128, K)

    def fm(v):
        return v.reshape(-1, 128).T

    w = x["w_in"][0]
    c = np.cumsum([0, CH, CH, QL, KVL, ROPE, MH * MD, 3 * D])
    r = {}
    xs = np.concatenate([x["x_prompt"][0], x["x_sample"][0]], 0)
    r["x_tok"] = xs
    r["xT"] = xs.T.reshape(KT, 128, T).transpose(1, 0, 2)
    r["memT"] = x["mem_prompt"][0].T.reshape(KT, 128, MT).transpose(1, 0, 2)
    r["w_glu_t"] = np.concatenate([m_tiles(w[:, c[1]:c[2]]), m_tiles(w[:, c[0]:c[1]])], 0)
    r["w_q_t"] = m_tiles(w[:, c[2]:c[3]])
    r["w_kv_t"] = m_tiles(w[:, c[3]:c[4]])
    r["w_kr_t"] = w[:, c[4]:c[5]].reshape(KT, 128, ROPE).transpose(1, 0, 2).reshape(128, KT * ROPE)
    r["w_mq_t"] = m_tiles(w[:, c[5]:c[6]])
    r["w_gate_t"] = m_tiles(w[:, c[6]:c[7]])
    r["w_mk_t"] = m_tiles(x["w_mem_k"][0])
    r["w_mv_t"] = x["w_mem_v"][0].reshape(4, 2, 128, 512).transpose(0, 2, 1, 3).reshape(4, 128, 1024)
    uq = x["w_uq"][0].reshape(QL, NH, QK)
    uq = np.concatenate([uq[:, :, :NOPE].reshape(QL, -1), uq[:, :, NOPE:].reshape(QL, -1)], 1)
    r["w_uq_t"] = m_tiles(uq).reshape(3, 2, 128, QL).transpose(0, 2, 1, 3).reshape(3, 128, 2 * QL)
    r["w_uk_t"] = m_tiles(x["w_uk"][0].reshape(KVL, -1)).transpose(1, 0, 2).reshape(128, 4 * KVL)
    r["w_uv_t"] = x["w_uv"][0].reshape(2, 128, 512).transpose(1, 0, 2).reshape(128, 1024)
    r["w_como_t"] = np.concatenate([m_tiles(x["w_co"][0]), m_tiles(x["w_mo"][0])], 2)
    r["w_xo_t"] = m_tiles(x["w_mem_o"][0])
    r["conv_state_T"] = x["cache_conv"][0, 0].T.reshape(4, 128, PAD).transpose(1, 0, 2)
    r["w_dw_T"] = x["w_dw"][0].T.reshape(4, 128, CW).transpose(1, 0, 2)
    r["conv_vec"] = np.stack([fm(x[n][0]) for n in ("b_dw", "g_cn", "b_cn")], 1)
    r["g_qa_T"] = fm(x["g_qa"][0])
    r["g_kva_T"] = fm(x["g_kva"][0])
    r["b_gate_T"] = fm(x["b_gate"][0])
    half = ROPE // 2
    inv = np.power(np.float32(10000.0), -np.arange(half, dtype=np.float32) / np.float32(half)).astype(np.float32)
    pos = np.concatenate([np.arange(TP), PAST + np.arange(TS)]).astype(np.float32)
    ang = (inv[:, None] * pos[None, :]).astype(np.float32)
    cos, sin = np.cos(ang).astype(np.float32), np.sin(ang).astype(np.float32)
    r["rope_cos"] = np.tile(cos, (8, 1))
    r["rope_sin"] = np.tile(np.concatenate([-sin, sin], 0), (4, 1))
    r["past_krope_T"] = x["cache_mla_krope"][0, 0].T
    r["past_lat_T"] = x["cache_mla_latent"][0, 0].T.reshape(2, 128, PAST)
    r["mem_k_T"] = x["cache_mem_k"][0, 0].transpose(2, 1, 0)
    r["cache_mem_v"] = x["cache_mem_v"][0, 0].reshape(2, 128, MH * MD).transpose(1, 0, 2)
    wr = np.concatenate([x["w_group"][0], x["w_router"][0]], 1)
    r["w_route"] = wr.reshape(KT, 128, NG + NE).transpose(1, 0, 2)
    r["b_route"] = np.concatenate([x["b_group"], x["b_router"]], 1)
    r["w_out"] = x["w_out"][0]
    for n in ("g_ln1", "b_ln1", "g_ln2", "b_ln2"):
        r[n] = x[n]
    up = np.stack([x["w_e1"].reshape(NE, KT, 128, FE), x["w_e3"].reshape(NE, KT, 128, FE)], 1)
    r["w_e13"] = up.transpose(0, 3, 1, 2, 4).reshape(NE, 128, 2 * KT * FE)
    r["w_e2"] = x["w_e2"].reshape(NE, 2, 128, D).transpose(0, 2, 1, 3).reshape(NE, 128, 2 * D)
    return r


OUTS = {"y_prompt": (TP, D), "y_sample": (TS, D), "conv_prompt_T": (128, 4, PAD), "conv_sample_T": (128, 4, PAD),
        "latent_T": (128, 2, T), "krope_T": (ROPE, T), "mem_k_T": (128, MH, MT), "mem_v": (128, 2, MH * MD)}


def kernel(**inputs):
    import concourse.bacc as bacc
    from concourse.bass_utils import run_bass_kernel_spmd

    x = {k: np.asarray(v) for k, v in inputs.items()}
    nc = bacc.Bacc("TRN2", target_bir_lowering=False, num_devices=1)
    arrays, a, o = {}, {}, {}
    for name, v in lay_out(x).items():
        v = np.ascontiguousarray(v)
        arrays[f"in_{name}"] = v
        a[name] = nc.dram_tensor(f"in_{name}", v.shape, mybir.dt.from_np(v.dtype), kind="ExternalInput").ap()
    for name, shape in OUTS.items():
        o[name] = nc.dram_tensor(f"out_{name}", shape, F32, kind="ExternalOutput").ap()
    program(nc, a, o)
    r = run_bass_kernel_spmd(nc, [arrays], core_ids=[0]).results[0]
    g = {n: np.asarray(r[f"out_{n}"]) for n in OUTS}

    def rows(v):
        return np.ascontiguousarray(v.transpose(2, 1, 0).reshape(v.shape[2], -1))

    lat = rows(g["latent_T"])
    kr = np.ascontiguousarray(g["krope_T"].T)
    mk = np.ascontiguousarray(g["mem_k_T"].transpose(2, 1, 0))
    mv = np.ascontiguousarray(g["mem_v"].transpose(1, 0, 2)).reshape(MT, MH, MD)
    return (g["y_prompt"][None], g["y_sample"][None], rows(g["conv_prompt_T"])[None, None], lat[None, None, :TP],
            kr[None, None, :TP], mk[None, None], mv[None, None], rows(g["conv_sample_T"])[None, None],
            lat[None, None, TP:], kr[None, None, TP:])
```
